# Optimizing a Trainium2 kernel written in Bass

```python
import jax, jax.numpy as jnp
from jax import lax
import numpy as np

D_MODEL = 1024
BATCH = 1
SEQ = 256
DEPTH = 1
DEC_BATCH = 8
DEC_SEQ = 4
PAST_LEN = 256
PAGE_SIZE = 128

N_HEADS = 8
HEAD_DIM = D_MODEL // N_HEADS
N_KV_HEADS = 2
GROUP = N_HEADS // N_KV_HEADS
N_IDX_HEADS = 8
IDX_DIM = 64
TOPK_MAX = 256
Q_BLOCK = 128
D_CONV = D_MODEL
CONV_WIDTH = 31
N_SUBKEYS = 128
N_EXPERTS = N_SUBKEYS * N_SUBKEYS
PEER_HEADS = 8
PEER_KEY_DIM = 256
PEER_HALF = PEER_KEY_DIM // 2
PEER_TOPK = 16
PEER_CHUNK = 256
N_ADA = 6
EPS = 1e-6
NEG_INF = -1e30
SPLITS = (N_HEADS * HEAD_DIM, N_KV_HEADS * HEAD_DIM, N_KV_HEADS * HEAD_DIM,
          N_IDX_HEADS * IDX_DIM, IDX_DIM, N_IDX_HEADS, 2 * D_CONV, 2 * D_MODEL)
D_IN = sum(SPLITS)
F32 = jnp.float32

kernel_name = 'dsa_conformer_peer_adaln_decode_step'

def rms_norm(x, g):
    xf = x.astype(F32)
    y = xf * lax.rsqrt(jnp.mean(xf * xf, axis=-1, keepdims=True) + EPS)
    return (y * g.astype(F32)).astype(x.dtype)

def layer_norm(x, g, b):
    xf = x.astype(F32)
    xc = xf - jnp.mean(xf, axis=-1, keepdims=True)
    y = xc * lax.rsqrt(jnp.mean(xc * xc, axis=-1, keepdims=True) + EPS)
    return (y * g.astype(F32) + b.astype(F32)).astype(x.dtype)

def alibi_slopes():
    return jnp.exp2(-8.0 * jnp.arange(1, N_HEADS + 1, dtype=F32) / N_HEADS)

def ada_mod(c, w_ada, b_ada):
    m = jax.nn.silu(c) @ w_ada + b_ada
    return jnp.split(m[:, None, :], N_ADA, axis=-1)

def take_rows(a, idx):
    return jax.vmap(lambda ab, ib: ab[ib])(a, idx)

def sparse_attn_block(q, qi, wi, q_pos, ki_all, topk, gather_kv, slopes):
    n, tq = q.shape[:2]
    L = ki_all.shape[1]
    s = jnp.einsum('nthd,nsd->nths', qi.astype(F32), ki_all.astype(F32)) * (IDX_DIM ** -0.5)
    iscore = jnp.einsum('nths,nth->nts', jax.nn.relu(s), wi.astype(F32)) * (N_IDX_HEADS ** -0.5)
    causal = jnp.arange(L, dtype=jnp.int32)[None, :] <= q_pos[:, None]
    iscore = jnp.where(causal[None], iscore, NEG_INF)
    _, idx = lax.top_k(iscore, topk)
    valid = idx <= q_pos[None, :, None]
    k_sel, v_sel = gather_kv(idx)
    qg = q.reshape(n, tq, N_KV_HEADS, GROUP, HEAD_DIM).astype(F32)
    logits = jnp.einsum('ntvgd,ntjvd->ntvgj', qg, k_sel.astype(F32)) * (HEAD_DIM ** -0.5)
    dist = (q_pos[None, :, None] - idx).astype(F32)
    logits = logits - slopes.reshape(N_KV_HEADS, GROUP)[None, None, :, :, None] * dist[:, :, None, None, :]
    logits = jnp.where(valid[:, :, None, None, :], logits, NEG_INF)
    p = jax.nn.softmax(logits, axis=-1)
    out = jnp.einsum('ntvgj,ntjvd->ntvgd', p, v_sel.astype(F32))
    return out.reshape(n, tq, N_HEADS * HEAD_DIM).astype(q.dtype)

def prompt_attention(q, k, v, qi, ki, wi):
    b, s = q.shape[:2]
    nblk = s // Q_BLOCK
    topk = min(TOPK_MAX, s // 4)
    slopes = alibi_slopes()

    def gather_kv(idx):
        return take_rows(k, idx), take_rows(v, idx)

    def blocks(a):
        return jnp.swapaxes(a.reshape((b, nblk, Q_BLOCK) + a.shape[2:]), 0, 1)

    pos = jnp.arange(s, dtype=jnp.int32).reshape(nblk, Q_BLOCK)
    out = lax.map(lambda a: sparse_attn_block(a[0], a[1], a[2], a[3], ki, topk, gather_kv, slopes),
                  (blocks(q), blocks(qi), blocks(wi), pos))
    return jnp.swapaxes(out, 0, 1).reshape(b, s, N_HEADS * HEAD_DIM)

def sample_attention(q, k, v, qi, ki, wi, cache_k, cache_v, cache_idx_k, page_table):
    bd, t = q.shape[:2]
    page = cache_k.shape[1]
    past = page_table.shape[1] * page
    ki_past = cache_idx_k[page_table].reshape(bd, past, IDX_DIM)
    ki_all = jnp.concatenate([ki_past, ki.astype(ki_past.dtype)], axis=1)
    topk = min(TOPK_MAX, (past + t) // 4)

    def gather_kv(idx):
        in_past = (idx < past)[..., None, None]
        pidx = jnp.minimum(idx, past - 1)
        phys = jnp.take_along_axis(page_table, (pidx // page).reshape(bd, -1), axis=1).reshape(idx.shape)
        off = pidx % page
        nidx = jnp.clip(idx - past, 0, t - 1)
        return (jnp.where(in_past, cache_k[phys, off], take_rows(k, nidx)),
                jnp.where(in_past, cache_v[phys, off], take_rows(v, nidx)))

    q_pos = past + jnp.arange(t, dtype=jnp.int32)
    return sparse_attn_block(q, qi, wi, q_pos, ki_all, topk, gather_kv, alibi_slopes())

def conv_branch(u, left, w_dw, b_dw, ln_g, ln_b, w_conv_out):
    a, g = jnp.split(u, 2, axis=-1)
    z = a * jax.nn.sigmoid(g)
    zp = jnp.concatenate([left.astype(z.dtype), z], axis=1)
    y = lax.conv_general_dilated(zp, w_dw[:, None, :].astype(z.dtype), (1,), 'VALID',
                                 dimension_numbers=('NWC', 'WIO', 'NWC'),
                                 feature_group_count=D_CONV) + b_dw
    y = jax.nn.silu(layer_norm(y, ln_g, ln_b))
    return y @ w_conv_out, zp[:, zp.shape[1] - (CONV_WIDTH - 1):]

def peer(h, w_q_peer, sub_keys1, sub_keys2, u_emb, v_emb):
    shape = h.shape
    flat = h.reshape(-1, shape[-1])
    m = flat.shape[0]
    nch = -(-m // PEER_CHUNK)
    flat = jnp.pad(flat, ((0, nch * PEER_CHUNK - m), (0, 0))).reshape(nch, PEER_CHUNK, shape[-1])
    n_cand = PEER_TOPK * PEER_TOPK

    def chunk(xc):
        qh = (xc @ w_q_peer).astype(F32).reshape(PEER_CHUNK, PEER_HEADS, 2, PEER_HALF)
        s1 = jnp.einsum('chd,kd->chk', qh[:, :, 0], sub_keys1.astype(F32))
        s2 = jnp.einsum('chd,kd->chk', qh[:, :, 1], sub_keys2.astype(F32))
        v1, i1 = lax.top_k(s1, PEER_TOPK)
        v2, i2 = lax.top_k(s2, PEER_TOPK)
        cand_s = (v1[..., :, None] + v2[..., None, :]).reshape(PEER_CHUNK, PEER_HEADS, n_cand)
        cand_id = (i1[..., :, None] * N_SUBKEYS + i2[..., None, :]).reshape(PEER_CHUNK, PEER_HEADS, n_cand)
        top_s, top_j = lax.top_k(cand_s, PEER_TOPK)
        eid = jnp.take_along_axis(cand_id, top_j, axis=-1)
        gate = jax.nn.softmax(top_s, axis=-1)
        act = jax.nn.gelu(jnp.einsum('chkd,cd->chk', u_emb[eid], xc).astype(F32))
        return jnp.einsum('chk,chkd->cd', (gate * act).astype(v_emb.dtype), v_emb[eid])

    out = lax.map(chunk, flat).reshape(-1, shape[-1])[:m]
    return out.reshape(shape).astype(h.dtype)

def trunk_layer(x, c, attn_fn, conv_left, p):
    shift1, scale1, gate1, shift2, scale2, gate2 = ada_mod(c, p['w_ada'], p['b_ada'])
    n, t, _ = x.shape
    h = rms_norm(x, p['g_norm1']) * (1 + scale1) + shift1
    points = np.cumsum(SPLITS)[:-1].tolist()
    q, k, v, qi, ki, wi, u_conv, gates = jnp.split(h @ p['w_in'], points, axis=-1)
    q = rms_norm(q.reshape(n, t, N_HEADS, HEAD_DIM), p['g_q'])
    k = rms_norm(k.reshape(n, t, N_KV_HEADS, HEAD_DIM), p['g_k'])
    v = v.reshape(n, t, N_KV_HEADS, HEAD_DIM)
    qi = qi.reshape(n, t, N_IDX_HEADS, IDX_DIM)
    attn = attn_fn(q, k, v, qi, ki, wi)
    conv_out, conv_state = conv_branch(u_conv, conv_left, p['w_dw'], p['b_dw'],
                                       p['ln_g'], p['ln_b'], p['w_conv_out'])
    g_attn, g_conv = jnp.split(jax.nn.sigmoid(gates), 2, axis=-1)
    merged = g_attn * (attn @ p['w_o_attn']) + g_conv * conv_out
    x = x + gate1 * (merged @ p['w_out'])
    h2 = rms_norm(x, p['g_norm2']) * (1 + scale2) + shift2
    x = x + gate2 * peer(h2, p['w_q_peer'], p['sub_keys1'], p['sub_keys2'], p['u_emb'], p['v_emb'])
    return x, k, v, ki, conv_state

def setup_inputs(seed: int = 0) -> dict:
    key = jax.random.key(seed)
    ks = jax.random.split(key, 32)
    n_pages = PAST_LEN // PAGE_SIZE
    n_used = DEC_BATCH * n_pages
    n_pool = n_used + (n_used + 3) // 4

    def nrm(k, shape, s=1.0):
        return s * jax.random.normal(k, shape, F32)

    page_table = jax.random.permutation(ks[6], n_pool)[:n_used].reshape(DEC_BATCH, n_pages).astype(jnp.int32)
    return {
        'x_prompt': nrm(ks[0], (BATCH, SEQ, D_MODEL)),
        'x_sample': nrm(ks[1], (DEC_BATCH, DEC_SEQ, D_MODEL)),
        'cache_k': nrm(ks[2], (n_pool, PAGE_SIZE, N_KV_HEADS, HEAD_DIM)),
        'cache_v': nrm(ks[3], (n_pool, PAGE_SIZE, N_KV_HEADS, HEAD_DIM)),
        'cache_idx_k': nrm(ks[4], (n_pool, PAGE_SIZE, IDX_DIM)),
        'state_conv': nrm(ks[5], (DEC_BATCH, CONV_WIDTH - 1, D_CONV), 0.5),
        'page_table': page_table,
        'c_prompt': nrm(ks[7], (BATCH, D_MODEL)),
        'c_sample': nrm(ks[8], (DEC_BATCH, D_MODEL)),
        'w_ada': nrm(ks[9], (D_MODEL, N_ADA * D_MODEL), 0.5 * D_MODEL ** -0.5),
        'b_ada': nrm(ks[10], (N_ADA * D_MODEL,), 0.01),
        'g_norm1': 1.0 + nrm(ks[11], (D_MODEL,), 0.01),
        'g_norm2': 1.0 + nrm(ks[12], (D_MODEL,), 0.01),
        'w_in': nrm(ks[13], (D_MODEL, D_IN), D_MODEL ** -0.5),
        'g_q': 1.0 + nrm(ks[14], (HEAD_DIM,), 0.01),
        'g_k': 1.0 + nrm(ks[15], (HEAD_DIM,), 0.01),
        'w_o_attn': nrm(ks[16], (N_HEADS * HEAD_DIM, D_MODEL), (N_HEADS * HEAD_DIM) ** -0.5),
        'w_dw': nrm(ks[17], (CONV_WIDTH, D_CONV), CONV_WIDTH ** -0.5),
        'b_dw': nrm(ks[18], (D_CONV,), 0.01),
        'ln_g': 1.0 + nrm(ks[19], (D_CONV,), 0.01),
        'ln_b': nrm(ks[20], (D_CONV,), 0.01),
        'w_conv_out': nrm(ks[21], (D_CONV, D_MODEL), D_CONV ** -0.5),
        'w_out': nrm(ks[22], (D_MODEL, D_MODEL), D_MODEL ** -0.5),
        'w_q_peer': nrm(ks[23], (D_MODEL, PEER_HEADS * PEER_KEY_DIM), D_MODEL ** -0.5),
        'sub_keys1': nrm(ks[24], (N_SUBKEYS, PEER_HALF), PEER_HALF ** -0.5),
        'sub_keys2': nrm(ks[25], (N_SUBKEYS, PEER_HALF), PEER_HALF ** -0.5),
        'u_emb': nrm(ks[26], (N_EXPERTS, D_MODEL), D_MODEL ** -0.5),
        'v_emb': nrm(ks[27], (N_EXPERTS, D_MODEL), 0.25),
    }

def reference(x_prompt, x_sample, cache_k, cache_v, cache_idx_k, state_conv, page_table, c_prompt, c_sample,
              w_ada, b_ada, g_norm1, g_norm2, w_in, g_q, g_k, w_o_attn, w_dw, b_dw, ln_g, ln_b,
              w_conv_out, w_out, w_q_peer, sub_keys1, sub_keys2, u_emb, v_emb):
    p = {'w_ada': w_ada, 'b_ada': b_ada, 'g_norm1': g_norm1, 'g_norm2': g_norm2, 'w_in': w_in,
         'g_q': g_q, 'g_k': g_k, 'w_o_attn': w_o_attn, 'w_dw': w_dw, 'b_dw': b_dw, 'ln_g': ln_g,
         'ln_b': ln_b, 'w_conv_out': w_conv_out, 'w_out': w_out, 'w_q_peer': w_q_peer,
         'sub_keys1': sub_keys1, 'sub_keys2': sub_keys2, 'u_emb': u_emb, 'v_emb': v_emb}

    def sample_attn(q, k, v, qi, ki, wi):
        return sample_attention(q, k, v, qi, ki, wi, cache_k, cache_v, cache_idx_k, page_table)

    y_prompt, y_sample = x_prompt, x_sample
    for _ in range(DEPTH):
        prompt_left = jnp.zeros((x_prompt.shape[0], CONV_WIDTH - 1, D_CONV), x_prompt.dtype)
        y_prompt, k_p, v_p, ki_p, conv_p = trunk_layer(y_prompt, c_prompt, prompt_attention, prompt_left, p)
        y_sample, k_s, v_s, ki_s, conv_s = trunk_layer(y_sample, c_sample, sample_attn, state_conv, p)
    return (y_prompt, y_sample, k_p, v_p, ki_p, conv_p, k_s, v_s, ki_s, conv_s)


_drawn_inputs = setup_inputs


def setup_inputs(seed=0):
    import zlib

    import numpy as np

    out = dict(_drawn_inputs(seed))
    spreads = {}
    factors = {'b_ada': 3.874,
     'g_norm1': 3.939,
     'g_norm2': 22.595,
     'g_q': 8.0,
     'g_k': 5.618,
     'b_dw': 8.0,
     'ln_g': 31.136,
     'ln_b': 31.692}
    for name, (base, spread) in spreads.items():
        noise = np.random.default_rng([zlib.crc32(name.encode()), seed]).standard_normal(out[name].shape)
        drawn = base * np.exp(spread * noise) if base else spread * noise
        out[name] = __import__('jax').numpy.asarray(drawn.astype(out[name].dtype))
    for name, factor in factors.items():
        out[name] = (out[name] * factor).astype(out[name].dtype)
    return out
```

```python
from contextlib import ExitStack

import numpy as np

import concourse.bass as bass
from concourse import mybir

P = 128
D = 1024
KC = D // P
TP, NSEQ, TD = 256, 8, 4
TS = NSEQ * TD
T = TP + TS
NQ = TP // P
NT = NQ + 1
NG = 1 + NSEQ
H, KV = 8, 2
HG = H // KV
IH, ID = 8, 64
CW = 31
LEFT = CW - 1
PAGE, NPAGES = 128, 2
PAST = PAGE * NPAGES
PROMPT_TOPK = TP // 4
SAMPLE_TOPK = (PAST + TD) // 4
NSUB, PH, PTOP = 128, 8, 16
EPS = 1e-6
NEG = -1e30
TAKEN = -3e38
R = 4
ADA_COLS = 512
NADA = 6 * D // ADA_COLS * R
QK_SCALE = P ** -0.5
IDX_SCALE = ID ** -0.5
HEAD_SCALE = IH ** -0.5
VW = KV * P + IH

LINEAR = ([(kind, k) for k in range(KC) for kind in ("conv_a", "conv_g")] + [("ki", 0)]
          + [("qi", n) for n in range(4)] + [("k", n) for n in range(KV)] + [("q", n) for n in range(H)]
          + [("gate_a", n) for n in range(KC)] + [("gate_b", n) for n in range(KC)]
          + [("conv_out", n) for n in range(KC)] + [("attn_out", n) for n in range(KC)]
          + [("out", n) for n in range(KC)] + [("peer_q", n) for n in range(2 * PH)])
TILE = {key: NADA + n for n, key in enumerate(LINEAR)}
NLIN = NADA + len(LINEAR)
NTILES = NLIN + 2 * NSUB
U_SLOT = [NLIN % R, (NLIN + 1) % R]
V_SLOT = [(NLIN + 2) % R, (NLIN + 3) % R]

BANKED = []
for key in LINEAR:
    if key == ("k", 0):
        BANKED += [("v", t) for t in range(NT)]
    BANKED.append(key)
NBANK = 3
BANK = {key: n % NBANK for n, key in enumerate(BANKED)}
ACT_EVAC, n_evac = {}, 0
for key in BANKED:
    if key[0] in ("ki", "qi", "v", "gate_a", "gate_b", "peer_q"):
        n_evac += 1
        ACT_EVAC[key] = n_evac
    if key[0] in ("k", "q"):
        n_evac += 2
        ACT_EVAC[key] = n_evac
QK = [("k", n) for n in range(KV)] + [("q", n) for n in range(H)]


def tokens(t):
    return (slice(t * P, t * P + P), P) if t < NQ else (slice(TP, T), TS)


def build(nc, a):
    f32, i32, u32 = mybir.dt.float32, mybir.dt.int32, mybir.dt.uint32
    ALU, ACT, AX = mybir.AluOpType, mybir.ActivationFunctionType, mybir.AxisListType

    with ExitStack() as ctx:
        def sb(name, *shape, dt=f32):
            return ctx.enter_context(nc.sbuf_tensor(name, [P] + list(shape), dt))

        def sem(name):
            return ctx.enter_context(nc.semaphore(name))

        x = sb("x", KC, T)
        h2 = sb("h2", KC, T)
        mod = sb("mod", 6, KC, NG)
        scl = sb("scl", 2, KC, NG)
        ident = sb("ident", P)
        ones = sb("ones", P)
        iota = sb("iota", P)
        gnorm = sb("gnorm", 2, KC)
        cT = sb("cT", KC, NG)
        cs = sb("cs", KC, NG)
        badaT = sb("badaT", 6 * KC)
        ring = sb("ring", R, D)
        picked = sb("picked", 3, T)
        pages = sb("pages", NSEQ * NPAGES, dt=i32)
        NBIG = NSUB * T
        big = sb("big", NBIG)
        NSMALL = 4400
        small = sb("small", NSMALL)
        gate_mat = big[:, :].rearrange("p (i t) -> p i t", t=T)

        class Region:

            def __init__(self, tensor, size):
                self.tensor, self.size, self.at = tensor, size, 0

            def take(self, *shape, dt=None):
                n = int(np.prod(shape))
                v = self.tensor[:, self.at:self.at + n]
                self.at += n
                assert self.at <= self.size, (self.at, self.size)
                if dt is not None:
                    v = v.bitcast(dt)
                names = "abcd"[:len(shape)]
                if len(shape) > 1:
                    v = v.rearrange(f"p ({' '.join(names)}) -> p {' '.join(names)}",
                                    **{c: s for c, s in zip(names[1:], shape[1:])})
                return v

        early = Region(big, NBIG)
        hT = early.take(KC, T)
        xn = early.take(KC, T)
        q = early.take(H, T)
        kT = early.take(KV, T)
        qi = early.take(4, T)
        ki = early.take(T)
        vtok = early.take(NT, VW)
        zp = early.take(KC, LEFT + TP)
        zs = early.take(KC, NSEQ, LEFT + TD)
        m_at = early.at
        y = early.take(KC, T)
        ga = early.take(KC, T)
        gb = early.take(KC, T)
        attn = early.take(KC, T)
        m_row = big[0:NG, m_at:m_at + 6 * D]
        v_w = attn[:, :, 0:VW]
        cache_k = early.take(NSEQ * NPAGES, KV, PAGE)
        cache_v = early.take(NSEQ * NPAGES, KV * P)
        cache_i = early.take(NSEQ * NPAGES, PAGE)
        wdw = early.take(KC, CW)
        cvec = early.take(3, KC)
        qkg = early.take(2)
        dist = early.take(NQ, TP)
        causal = early.take(NQ, TP)
        alibi_past = early.take(NPAGES, NSEQ * H * TD)
        alibi_new = early.take(NSEQ * H * TD)
        own = early.take(PAST + TS)
        sq_qk = [gb[:, n] for n in range(KV)] + [attn[:, n] for n in range(H)]
        rs_k = early.take(KV, T)

        r0 = Region(big, KC * T)
        s_relu = r0.take(NPAGES, IH * TS)
        n_relu = r0.take(IH * TS)
        wi_all = r0.take(IH, TS)
        wi_diag = r0.take(IH, TS)
        s_iscT = r0.take(NPAGES + 1, TS)
        s_isc = r0.take(PAST + TS)
        s_sel = r0.take(PAST + TS)
        s_max8 = r0.take(8)
        r1 = Region(big, 2 * KC * T)
        r1.at = KC * T
        s_selT = r1.take(NPAGES + 1, TS)
        s_lT = r1.take(NPAGES + 1, NSEQ * H * TD)
        s_row = r1.take(2, PAST + TS)
        s_prT = s_lT
        s_stat = r1.take(2, 4)

        s1 = Region(small, NSMALL)
        rstd = s1.take(T)
        sig = s1.take(2, T)
        relu = s1.take(2, TP)
        isc = s1.take(NQ, TP)
        selb = s1.take(NQ, TP)
        max8 = s1.take(NQ, 8)
        bias_h = s1.take(2, TP)
        lg = s1.take(2, TP)
        prT = s1.take(2, TP)
        stat = s1.take(NQ * H, 3)

        late = Region(big, NBIG)
        qh = late.take(2 * PH, T)
        sk = late.take(2, NSUB)
        sc = late.take(NT, 2 * PH, NSUB)
        scw = late.take(NT, 2 * PH, NSUB)
        va = late.take(NT, 2 * PH, PTOP)
        ix = late.take(NT, 2 * PH, PTOP, dt=u32)
        ixf = late.take(NT, 2 * PH, PTOP)
        cand = sc.rearrange("p t (h c) k -> p t h (c k)", c=2)
        tv = late.take(NT, PH, PTOP)
        tj = late.take(NT, PH, PTOP, dt=u32)
        tab_u = late.take(2, NT, PH * PTOP, dt=u32)
        tab = late.take(2, NT, PH * PTOP)
        tsel = late.take(NT, 3, PH * PTOP)
        gsum = late.take(NT, PH, 2)
        eq = late.take(PH * PTOP, PTOP)

        s3 = Region(small, NSMALL)
        NH = 8
        hot1 = s3.take(NH, P)
        hot2 = s3.take(NH, P)
        act = s3.take(2, T)
        wgt = s3.take(2, T)
        dtmp = s3.take(TS)
        zeros = s3.take(512)

        ps = [ctx.enter_context(nc.psum_tensor(f"ps{b}", [P, 512], f32)) for b in range(8)]
        lin, stb, pa = ps[0:NBANK], ps[3], ps[4:8]

        tile_loaded = [sem(f"tile_loaded{s}") for s in range(R)]
        tile_done = sem("tile_done")
        v_done = sem("v_done")
        u_done = sem("u_done")
        o_done = sem("o_done")
        inputs = sem("inputs")
        consts = sem("consts")
        conv_in = sem("conv_in")
        vw_in = sem("vw_in")
        pages_in = sem("pages_in")
        cache_in = sem("cache_in")
        attn_in = sem("attn_in")
        peer_in = sem("peer_in")
        zeroed = sem("zeroed")
        squares = sem("squares")
        stats = sem("stats")
        stat_v = sem("stat_v")
        stat_r = sem("stat_r")
        c_sig = sem("c_sig")
        c_silu = sem("c_silu")
        ada_copied = sem("ada_copied")
        mod_turned = sem("mod_turned")
        h_ready = sem("h_ready")
        sig_ready = sem("sig_ready")
        z_ready = sem("z_ready")
        act_evac = sem("act_evac")
        qk_sums = sem("qk_sums")
        qk_var = sem("qk_var")
        qk_root = sem("qk_root")
        qk_ready = sem("qk_ready")
        idx_prod = sem("idx_prod")
        idx_relu = sem("idx_relu")
        idx_used = sem("idx_used")
        y_ready = sem("y_ready")
        y_centred = sem("y_centred")
        y_sig = sem("y_sig")
        y_scaled = sem("y_scaled")
        conv_ready = sem("conv_ready")
        gated = sem("gated")
        s_idx_prod = sem("s_idx_prod")
        s_wi = sem("s_wi")
        s_wi_prod = sem("s_wi_prod")
        s_relued = sem("s_relued")
        s_summed = sem("s_summed")
        s_turned = sem("s_turned")
        sel_ready = sem("sel_ready")
        logits = sem("logits")
        biased = sem("biased")
        row_max = sem("row_max")
        exped = sem("exped")
        normed = sem("normed")
        turned = sem("turned")
        turned_copied = sem("turned_copied")
        mixed = sem("mixed")
        mixed_copied = sem("mixed_copied")
        s_sel_ready = sem("s_sel_ready")
        s_selT_prod = sem("s_selT_prod")
        s_logits = sem("s_logits")
        s_biased = sem("s_biased")
        s_rows = sem("s_rows")
        s_rowmax = sem("s_rowmax")
        s_exped = sem("s_exped")
        s_normed = sem("s_normed")
        s_back = sem("s_back")
        s_back_copied = sem("s_back_copied")
        s_mixed = sem("s_mixed")
        s_mixed_copied = sem("s_mixed_copied")
        merged = sem("merged")
        x1_ready = sem("x1_ready")
        h2_ready = sem("h2_ready")
        pscore = sem("pscore")
        pscore_copied = sem("pscore_copied")
        top_max = sem("top_max")
        top_exp = sem("top_exp")
        picks = sem("picks")
        picks_turned = sem("picks_turned")
        picks_copied = sem("picks_copied")
        hot_ready = sem("hot_ready")
        gate_prod = sem("gate_prod")
        gate_copied = sem("gate_copied")
        gelued = sem("gelued")
        weighted = sem("weighted")
        y_out = sem("y_out")
        stored = sem("stored")
        dve_step = sem("dve_step")
        act_step = sem("act_step")

        def seq(v, n=TD):
            return v.rearrange("p (b t) -> p b t", t=n)

        block = ctx.enter_context(nc.Block())

        @block.sync
        def _(sp):
            def load(n, slot):
                sp.dma_start(ring[:, slot, :], a["stream"][n]).then_inc(tile_loaded[slot], 16)

            for n in range(R):
                load(n, n)
            with sp.Fori(0, (NLIN - R) // R) as g:
                for s in range(R):
                    sp.wait_ge(tile_done, g * R + (s + 1))
                    sp.dma_start(ring[:, s, :], a["stream"][bass.ds(g * R + (R + s), 1)].rearrange("o p n -> (o p) n"))\
                        .then_inc(tile_loaded[s], 16)
            for n in range(NLIN - NLIN % R, NLIN):
                sp.wait_ge(tile_done, n - R + 1)
                load(n, n % R)
            for c, base, slot in ((0, 0, U_SLOT[0]), (1, 1, U_SLOT[1]), (0, 2, V_SLOT[0]), (1, 3, V_SLOT[1])):
                sp.wait_ge(tile_done, NLIN + base - R + 1)
                load(NLIN + 2 * c + (slot == V_SLOT[c]), slot)
            with sp.Fori(1, NSUB // 2) as g:
                for c in range(2):
                    sp.wait_ge(u_done, g * 2 + (c - 1))
                    sp.dma_start(ring[:, U_SLOT[c], :],
                                 a["stream"][bass.ds(g * 4 + (NLIN + 2 * c), 1)].rearrange("o p n -> (o p) n"))\
                        .then_inc(tile_loaded[U_SLOT[c]], 16)
                    sp.wait_ge(o_done, g * 2 + (c - 1))
                    sp.dma_start(ring[:, V_SLOT[c], :],
                                 a["stream"][bass.ds(g * 4 + (NLIN + 2 * c + 1), 1)].rearrange("o p n -> (o p) n"))\
                        .then_inc(tile_loaded[V_SLOT[c]], 16)
            sp.wait_ge(y_out, 3 * KC)
            sp.dma_start(a["yT"], h2[:, :, :]).then_inc(stored, 16)
            sp.wait_ge(stored, 16 * 7)

        @block.gpsimd
        def _(pool):
            pool.dma_start(pages[0:1, :], a["pages"]).then_inc(pages_in, 16)
            nc.gpsimd.memset(zp[:, :, 0:LEFT], 0.0).then_inc(zeroed, 1)
            nc.gpsimd.memset(ones[:, :], 1.0).then_inc(zeroed, 1)
            pool.dma_start(v_w, a["v_w"]).then_inc(vw_in, 16)
            for dst, src in ((dist, "dist"), (causal, "causal"), (alibi_past, "alibi_past"),
                             (alibi_new[0:TS], "alibi_new"), (own[0:TS], "own")):
                pool.dma_start(dst, a[src]).then_inc(attn_in, 16)
            pool.wait_ge(pages_in, 16)
            for n in range(NSEQ * NPAGES):
                page = pool.value_load(pages[0:1, n:n + 1], min_val=0, max_val=a["cache_k"].shape[0] - 1)
                one = bass.ds(page, 1)
                pool.dma_start(cache_i[0:ID, n], a["cache_i"][one].rearrange("o p n -> (o p) n")).then_inc(cache_in, 16)
                pool.dma_start(cache_i[ID:P, n], a["cache_i"][one].rearrange("o p n -> (o p) n")).then_inc(cache_in, 16)
                pool.dma_start(cache_k[:, n], a["cache_k"][one].rearrange("o p v n -> (o p) v n")).then_inc(cache_in, 16)
                pool.dma_start(cache_v[:, n], a["cache_v"][one].rearrange("o p n -> (o p) n")).then_inc(cache_in, 16)
            pool.wait_ge(merged, 1)
            for n in range(2):
                pool.dma_start(sk[:, n], a["sub_keys"][n]).then_inc(peer_in, 16)
            pool.wait_ge(h2_ready, KC + 1)
            nc.gpsimd.memset(zeros, 0.0).then_inc(zeroed, 1)

        @block.scalar
        def _(eng):
            steps = [0]

            def chain(ins):
                steps[0] += 1
                ins.then_inc(act_step, 1)
                eng.wait_ge(act_step, steps[0])

            def square_all(src, ready, value):
                eng.wait_ge(*ready)
                nc.scalar.activation(xn[:, :, :], src[:, :, :], ACT.Square).then_inc(squares, 1)
                eng.wait_ge(stat_v, value)
                nc.scalar.activation(rstd, rstd, ACT.Sqrt).then_inc(stat_r, 1)

            eng.dma_start(cT[:, :, :], a["cT"]).then_inc(inputs, 16)
            eng.dma_start(x[:, :, :], a["xT"]).then_inc(inputs, 16)
            for dst, src in ((ident[:, :], "ident"), (iota[:, :], "iota"), (gnorm[:, :, :], "gnorm"),
                             (badaT[:, :], "badaT")):
                eng.dma_start(dst, a[src]).then_inc(consts, 16)
            for dst, src in ((zs[:, :, :, 0:LEFT], "stateT"), (wdw, "wdw"), (cvec, "cvec"), (qkg, "qkg")):
                eng.dma_start(dst, a[src]).then_inc(conv_in, 16)
            eng.wait_ge(inputs, 32)
            nc.scalar.activation(cs[:, :, :], cT[:, :, :], ACT.Sigmoid).then_inc(c_sig, 1)
            square_all(x, (inputs, 32), 1)
            with eng.Fori(0, NADA // R // 2) as g:
                for b in range(2):
                    eng.wait_ge(tile_done, g * (2 * R) + (b + 1) * R)
                    nc.scalar.activation(m_row[:, bass.ds(g * (2 * ADA_COLS) + b * ADA_COLS, ADA_COLS)],
                                         lin[b][0:NG, :], ACT.Copy).then_inc(ada_copied, 1)

            def evac(key, dst, func=ACT.Copy):
                eng.wait_ge(tile_done, TILE[key] + 1)
                nc.scalar.activation(dst, lin[BANK[key]][:, 0:T], func).then_inc(act_evac, 1)

            for k in range(KC):
                eng.wait_ge(tile_done, TILE["conv_g", k] + 1)
                if k >= 2:
                    eng.wait_ge(z_ready, 2 * (k - 1))
                nc.scalar.activation(sig[:, k % 2], lin[BANK["conv_g", k]][:, 0:T], ACT.Sigmoid).then_inc(sig_ready, 1)
            evac(("ki", 0), ki)
            for n in range(4):
                evac(("qi", n), qi[:, n])
            for t in range(NT):
                eng.wait_ge(v_done, t + 1)
                rows = tokens(t)[1]
                nc.scalar.activation(vtok[0:rows, t], lin[BANK["v", t]][0:rows, 0:VW], ACT.Copy).then_inc(act_evac, 1)
            for n, key in enumerate(QK):
                evac(key, (kT[:, key[1]] if key[0] == "k" else q[:, key[1]]))
                evac(key, sq_qk[n], ACT.Square)
            for n in range(KC):
                evac(("gate_a", n), ga[:, n], ACT.Sigmoid)
            eng.wait_ge(qk_var, len(QK))
            nc.scalar.activation(rs_k, rs_k, ACT.Sqrt).then_inc(qk_root, 1)
            nc.scalar.activation(h2[:, :, :], h2[:, :, :], ACT.Sqrt).then_inc(qk_root, 1)
            square_all(y, (y_centred, 1), 2)
            for n in range(KC):
                evac(("gate_b", n), gb[:, n], ACT.Sigmoid)
            eng.wait_ge(y_scaled, KC)
            nc.scalar.activation(xn[:, :, :], y[:, :, :], ACT.Sigmoid).then_inc(y_sig, 1)
            for n in range(NQ * IH):
                keys = P * (n // IH + 1)
                eng.wait_ge(idx_prod, n + 1)
                if n >= 2:
                    eng.wait_ge(idx_used, n - 1)
                nc.scalar.activation(relu[:, n % 2, 0:keys], pa[n % 2][:, 0:keys], ACT.Relu, scale=IDX_SCALE)\
                    .then_inc(idx_relu, 1)
            eng.wait_ge(s_idx_prod, 1)
            for par in range(2):
                cols = slice(par * 128, par * 128 + 128)
                nc.scalar.activation(s_relu[:, :, cols], pa[par][:, 0:256].rearrange("p (m b) -> p m b", m=NPAGES),
                                     ACT.Relu, scale=IDX_SCALE).then_inc(s_relued, 1)
                nc.scalar.activation(n_relu[0:TS, cols], pa[par][0:TS, 256:384], ACT.Relu, scale=IDX_SCALE)\
                    .then_inc(s_relued, 1)
            for n in range(NQ * H + 2):
                if n < NQ * H:
                    keys = P * (n // H + 1)
                    eng.wait_ge(row_max, n + 1)
                    nc.scalar.activation(lg[:, n % 2, 0:keys], lg[:, n % 2, 0:keys], ACT.Exp, bias=stat[:, n, 0:1],
                                         accum_out=stat[:, n, 1:2]).then_inc(exped, 1)
                if 1 <= n <= NQ * H:
                    m = n - 1
                    keys = P * (m // H + 1)
                    eng.wait_ge(turned, m + 1)
                    if m >= 2:
                        eng.wait_ge(mixed, m - 1)
                    nc.scalar.activation(prT[:, m % 2, 0:keys], pa[2][:, 0:keys], ACT.Copy).then_inc(turned_copied, 1)
                if n >= 2:
                    m = n - 2
                    eng.wait_ge(mixed, m + 1)
                    nc.scalar.activation(attn[:, m % H, tokens(m // H)[0]], pa[3][:, 0:P], ACT.Copy)\
                        .then_inc(mixed_copied, 1)
            for g in range(2):
                eng.wait_ge(s_rowmax, g + 1)
                nc.scalar.activation(s_row[:, g], s_row[:, g], ACT.Exp, bias=s_stat[:, g, 0:1],
                                     accum_out=s_stat[:, g, 1:2]).then_inc(s_exped, 1)
            eng.wait_ge(qk_ready, 4)
            eng.dma_start(a["kT"], kT).then_inc(stored, 16)
            eng.dma_start(a["v_prompt"], vtok[:, 0:NQ, 0:KV * P]).then_inc(stored, 16)
            eng.dma_start(a["v_sample"], vtok[0:TS, NQ, 0:KV * P]).then_inc(stored, 16)
            eng.dma_start(a["kiT"], ki[0:ID]).then_inc(stored, 16)
            eng.wait_ge(z_ready, 2 * KC)
            eng.dma_start(a["convpT"], zp[:, :, TP:TP + LEFT]).then_inc(stored, 16)
            eng.dma_start(a["convsT"], zs[:, :, :, TD:TD + LEFT]).then_inc(stored, 16)
            square_all(x, (x1_ready, 3 * KC), 3)
            eng.wait_ge(stored, 16 * 6)
            for n in range(2 * PH):
                evac(("peer_q", n), qh[:, n])
                if n % 4 == 3:
                    for t in range(NT):
                        m = n // 4 * NT + t
                        rows = tokens(t)[1]
                        eng.wait_ge(pscore, m + 1)
                        nc.scalar.activation(sc[0:rows, t, n - 3:n + 1],
                                             pa[m % 4][0:rows, :].rearrange("p (a b) -> p a b", b=NSUB), ACT.Copy)\
                            .then_inc(pscore_copied, 1)
            for t in range(NT):
                rows = tokens(t)[1]
                eng.wait_ge(top_max, t + 1)
                nc.scalar.activation(tv[0:rows, t], tv[0:rows, t], ACT.Exp).then_inc(top_exp, 1)
            for n in range(3):
                eng.wait_ge(picks_turned, n + 1)
                nc.scalar.activation(picked[:, n, :], pa[n][:, 0:T], ACT.Copy).then_inc(picks_copied, 1)
            with eng.Fori(0, T // 8) as g:
                for b in range(2):
                    eng.wait_ge(gate_prod, g * 2 + (b + 1))
                    nc.scalar.activation(gate_mat[:, :, bass.ds(g * 8 + b * 4, 4)],
                                         ps[b][:, :].rearrange("p (t i) -> p i t", t=4), ACT.Copy)\
                        .then_inc(gate_copied, 1)
            for c in range(2):
                eng.wait_ge(u_done, c + 1)
                nc.scalar.activation(act[:, c], ps[5 + c][:, 0:T], ACT.Gelu_apprx_tanh).then_inc(gelued, 1)
            with eng.Fori(1, NSUB // 2) as g:
                for c in range(2):
                    eng.wait_ge(u_done, g * 2 + (c + 1))
                    eng.wait_ge(weighted, g * 2 + (c - 1))
                    nc.scalar.activation(act[:, c], ps[5 + c][:, 0:T], ACT.Gelu_apprx_tanh).then_inc(gelued, 1)

        @block.vector
        def _(dve):
            V = nc.vector
            steps = [0]

            def step(ins):
                steps[0] += 1
                ins.then_inc(dve_step, 1)

            def settle(back=0):
                dve.wait_ge(dve_step, steps[0] - back)

            def inv_root(n, out):
                dve.wait_ge(stats, n)
                V.tensor_scalar(out, stb[:, 0:T], 1.0 / D, EPS, ALU.mult, ALU.add).then_inc(stat_v, 1)

            def root(n):
                dve.wait_ge(stat_r, n)
                step(V.reciprocal(rstd, rstd))
                settle()

            def over_chunks(v):
                return v.unsqueeze(1).to_broadcast([P, KC, T])

            def modulate(src, dst, which, ready):
                step(V.tensor_tensor(xn[:, :, :], src[:, :, :], over_chunks(rstd), ALU.mult))
                settle()
                for k in range(KC):
                    V.tensor_scalar(dst[:, k, 0:TP], xn[:, k, 0:TP], scl[:, which, k, 0:1],
                                    mod[:, 3 * which, k, 0:1], ALU.mult, ALU.add).then_inc(ready, 1)

                def wide(v):
                    return v.unsqueeze(3).to_broadcast([P, KC, NSEQ, TD])

                smp = dst[:, :, TP:T].rearrange("p k (b t) -> p k b t", t=TD)
                step(V.tensor_tensor(smp, xn[:, :, TP:T].rearrange("p k (b t) -> p k b t", t=TD),
                                     wide(scl[:, which, :, 1:NG]), ALU.mult))
                settle()
                V.tensor_tensor(smp, smp, wide(mod[:, 3 * which, :, 1:NG]), ALU.add).then_inc(ready, 1)

            dve.wait_ge(c_sig, 1)
            V.tensor_tensor(cs[:, :, :], cs[:, :, :], cT[:, :, :], ALU.mult).then_inc(c_silu, 1)
            inv_root(1, rstd)
            root(1)
            dve.wait_ge(consts, 64)
            dve.wait_ge(mod_turned, 1)
            flat = mod[:, :, :, :].rearrange("p a k g -> p (a k) g")
            step(V.tensor_tensor(flat, pa[0][:, 0:6 * KC * NG].rearrange("p (a g) -> p a g", g=NG),
                                 badaT[:, :].unsqueeze(2).to_broadcast([P, 6 * KC, NG]), ALU.add))
            settle()
            for w in range(2):
                step(V.tensor_scalar(scl[:, w], mod[:, 3 * w + 1], 1.0, None, ALU.add))
            settle()
            for w in range(2):
                step(V.tensor_tensor(scl[:, w], scl[:, w], gnorm[:, w].unsqueeze(2).to_broadcast([P, KC, NG]),
                                     ALU.mult))
            settle()
            modulate(x, hT, 0, h_ready)

            dve.wait_ge(conv_in, 64)
            dve.wait_ge(zeroed, 2)
            for k in range(KC):
                dve.wait_ge(tile_done, TILE["conv_a", k] + 1)
                dve.wait_ge(sig_ready, k + 1)
                pa_k = lin[BANK["conv_a", k]]
                V.tensor_tensor(zp[:, k, LEFT:], pa_k[:, 0:TP], sig[:, k % 2, 0:TP], ALU.mult).then_inc(z_ready, 1)
                V.tensor_tensor(zs[:, k, :, LEFT:], seq(pa_k[:, TP:T]), seq(sig[:, k % 2, TP:T]), ALU.mult)\
                    .then_inc(z_ready, 1)
                dve.wait_ge(z_ready, 2 * k + 2)
                yp, ys = y[:, k, 0:TP], seq(y[:, k, TP:T])
                for j in range(CW):
                    w = wdw[:, k, j:j + 1]
                    if j == 0:
                        step(V.tensor_scalar(yp, zp[:, k, 0:TP], w, None, ALU.mult))
                        step(V.tensor_scalar(ys, zs[:, k, :, 0:TD], w, None, ALU.mult))
                        continue
                    settle(1)
                    step(V.scalar_tensor_tensor(yp, zp[:, k, j:j + TP], w, yp, ALU.mult, ALU.add))
                    settle(1)
                    step(V.scalar_tensor_tensor(ys, zs[:, k, :, j:j + TD], w, ys, ALU.mult, ALU.add))
                settle()
                V.tensor_scalar(y[:, k], y[:, k], cvec[:, 0, k:k + 1], None, ALU.add).then_inc(y_ready, 1)
            dve.wait_ge(y_ready, KC)
            dve.wait_ge(stats, 2)
            step(V.tensor_scalar(rstd, stb[:, 0:T], 1.0 / D, None, ALU.mult))
            settle()
            V.tensor_tensor(y[:, :, :], y[:, :, :], over_chunks(rstd), ALU.subtract).then_inc(y_centred, 1)
            dve.wait_ge(y_centred, 1)
            for n in range(len(QK)):
                dve.wait_ge(qk_sums, n + 1)
                dst = rs_k[:, n] if n < KV else h2[:, n - KV]
                V.tensor_scalar(dst, pa[n % 2][:, 0:T], 1.0 / P, EPS, ALU.mult, ALU.add).then_inc(qk_var, 1)
            inv_root(3, rstd)
            dve.wait_ge(qk_root, 2)
            step(V.reciprocal(rs_k, rs_k))
            step(V.reciprocal(h2[:, :, :], h2[:, :, :]))
            settle()
            dve.wait_ge(act_evac, ACT_EVAC["q", H - 1])
            step(V.tensor_tensor(kT, kT, rs_k, ALU.mult))
            step(V.tensor_tensor(q, q, h2[:, :, :], ALU.mult))
            settle()
            V.tensor_scalar(kT, kT, qkg[:, 1:2], None, ALU.mult).then_inc(qk_ready, 2)
            V.tensor_scalar(q, q, qkg[:, 0:1], None, ALU.mult).then_inc(qk_ready, 2)
            root(2)
            step(V.tensor_tensor(y[:, :, :], y[:, :, :], over_chunks(rstd), ALU.mult))
            settle()
            for k in range(KC):
                V.tensor_scalar(y[:, k], y[:, k], cvec[:, 1, k:k + 1], cvec[:, 2, k:k + 1], ALU.mult, ALU.add)\
                    .then_inc(y_scaled, 1)

            dve.wait_ge(attn_in, 80)
            for n in range(NQ * IH):
                t, h = divmod(n, IH)
                keys = P * (t + 1)
                dve.wait_ge(idx_relu, n + 1)
                w = vtok[:, t, KV * P + h:KV * P + h + 1]
                acc = isc[:, t, 0:keys]
                if h == 0:
                    ins = V.tensor_scalar(acc, relu[:, n % 2, 0:keys], w, None, ALU.mult)
                else:
                    dve.wait_ge(idx_used, n)
                    ins = V.scalar_tensor_tensor(acc, relu[:, n % 2, 0:keys], w, acc, ALU.mult, ALU.add)
                ins.then_inc(idx_used, 1)
            dve.wait_ge(idx_used, NQ * IH)
            for t in range(NQ):
                keys = P * (t + 1)
                step(V.scalar_tensor_tensor(isc[:, t, 0:keys], isc[:, t, 0:keys], HEAD_SCALE, causal[:, t, 0:keys],
                                            ALU.mult, ALU.add))
            for _ in range(PROMPT_TOPK // 8):
                for t in range(NQ):
                    settle(1)
                    step(V.max(out=max8[:, t], in_=isc[:, t, 0:P * (t + 1)]))
                for t in range(NQ):
                    settle(1)
                    step(V.match_replace(out=isc[:, t, 0:P * (t + 1)], in_to_replace=max8[:, t],
                                         in_values=isc[:, t, 0:P * (t + 1)], imm_value=TAKEN))
            settle()
            for t in range(NQ):
                keys = P * (t + 1)
                step(V.tensor_scalar(selb[:, t, 0:keys], isc[:, t, 0:keys], TAKEN, NEG, ALU.not_equal, ALU.mult))
            settle()
            for t in range(NQ):
                keys = P * (t + 1)
                V.tensor_tensor(selb[:, t, 0:keys], selb[:, t, 0:keys], causal[:, t, 0:keys], ALU.add)\
                    .then_inc(sel_ready, 1)
            dve.wait_ge(y_sig, 1)
            V.tensor_tensor(y[:, :, :], y[:, :, :], xn[:, :, :], ALU.mult).then_inc(conv_ready, 1)

            dve.wait_ge(tile_done, TILE["gate_b", KC - 1] + 1)
            wi = vtok[0:TS, NQ, KV * P:VW].rearrange("p (pair par) -> p par pair", par=2)
            for par in range(2):
                V.tensor_tensor(wi_diag[0:TS, par * 4:par * 4 + 4], wi[:, par].unsqueeze(2).to_broadcast([TS, 4, TS]),
                                ident[0:TS, 0:TS].unsqueeze(1).to_broadcast([TS, 4, TS]), ALU.mult).then_inc(s_wi, 1)
            dve.wait_ge(s_wi_prod, 1)
            step(V.tensor_copy(wi_all, pa[2][:, 0:IH * TS].rearrange("p (a b) -> p a b", b=TS)))
            settle()
            dve.wait_ge(s_relued, 4)
            wi_flat = wi_all.rearrange("p a b -> p (a b)")
            for m in range(NPAGES):
                step(V.tensor_tensor(s_relu[:, m], s_relu[:, m], wi_flat, ALU.mult))
            step(V.tensor_tensor(n_relu[0:TS], n_relu[0:TS], wi_flat[0:TS], ALU.mult))
            settle()
            V.tensor_reduce(s_iscT[:, 0:NPAGES], s_relu.rearrange("p m (a b) -> p m b a", b=TS), AX.X, ALU.add)\
                .then_inc(s_summed, 1)
            V.tensor_reduce(s_iscT[0:TS, NPAGES], n_relu[0:TS].rearrange("p (a b) -> p b a", b=TS), AX.X, ALU.add)\
                .then_inc(s_summed, 1)
            dve.wait_ge(s_turned, 1)
            keys = PAST + TS
            step(V.scalar_tensor_tensor(s_isc[0:TS], pa[3][0:TS, 0:keys], HEAD_SCALE, own[0:TS], ALU.mult, ALU.add))
            for left in range(SAMPLE_TOPK, 0, -8):
                settle()
                step(V.max(out=s_max8[0:TS], in_=s_isc[0:TS]))
                settle()
                if left < 8:
                    step(V.memset(s_max8[0:TS, left:8], TAKEN))
                    settle()
                step(V.match_replace(out=s_isc[0:TS], in_to_replace=s_max8[0:TS], in_values=s_isc[0:TS],
                                     imm_value=TAKEN))
            settle()
            step(V.tensor_scalar(s_sel[0:TS], s_isc[0:TS], TAKEN, NEG, ALU.not_equal, ALU.mult))
            settle()
            V.tensor_tensor(s_sel[0:TS], s_sel[0:TS], own[0:TS], ALU.add).then_inc(s_sel_ready, 1)

            for n in range(KC):
                key = ("conv_out", n)
                dve.wait_ge(tile_done, TILE[key] + 1)
                dve.wait_ge(act_evac, ACT_EVAC["gate_b", n])
                V.tensor_tensor(gb[:, n], lin[BANK[key]][:, 0:T], gb[:, n], ALU.mult).then_inc(gated, 1)

            for n in range(NQ * H + 1):
                if n < NQ * H:
                    t, h = divmod(n, H)
                    keys = P * (t + 1)
                    slope = 2.0 ** (-8.0 * (h + 1) / H)
                    if n == 0:
                        dve.wait_ge(sel_ready, NQ)
                    if n >= 2:
                        dve.wait_ge(turned, n - 1)
                    step(V.scalar_tensor_tensor(bias_h[:, n % 2, 0:keys], dist[:, t, 0:keys], -slope,
                                                selb[:, t, 0:keys], ALU.mult, ALU.add))
                    settle()
                    dve.wait_ge(logits, n + 1)
                    V.scalar_tensor_tensor(lg[:, n % 2, 0:keys], pa[n % 2][:, 0:keys], QK_SCALE,
                                           bias_h[:, n % 2, 0:keys], ALU.mult, ALU.add).then_inc(biased, 1)
                    dve.wait_ge(biased, n + 1)
                    V.tensor_reduce(stat[:, n, 0:1], lg[:, n % 2, 0:keys], AX.X, ALU.max, negate=True)\
                        .then_inc(row_max, 1)
                if n >= 1:
                    m = n - 1
                    keys = P * (m // H + 1)
                    dve.wait_ge(exped, m + 1)
                    step(V.reciprocal(stat[:, m, 2:3], stat[:, m, 1:2]))
                    settle()
                    V.tensor_scalar(lg[:, m % 2, 0:keys], lg[:, m % 2, 0:keys], stat[:, m, 2:3], None, ALU.mult)\
                        .then_inc(normed, 1)

            dve.wait_ge(s_selT_prod, 1)
            step(V.tensor_copy(s_selT[:, 0:NPAGES], pa[2][:, 0:NPAGES * TS].rearrange("p (m b) -> p m b", b=TS)))
            step(V.tensor_copy(s_selT[0:TS, NPAGES], pa[2][0:TS, NPAGES * TS:(NPAGES + 1) * TS]))
            dve.wait_ge(s_logits, 1)
            for m in range(NPAGES):
                step(V.scalar_tensor_tensor(s_lT[:, m], pa[0][:, m * 256:m * 256 + 256], QK_SCALE, alibi_past[:, m],
                                            ALU.mult, ALU.add))
            step(V.scalar_tensor_tensor(s_lT[0:TS, NPAGES], pa[1][0:TS, 0:256], QK_SCALE, alibi_new[0:TS],
                                        ALU.mult, ALU.add))
            settle()
            for m in range(NPAGES + 1):
                rows = P if m < NPAGES else TS
                v = s_lT[0:rows, m].rearrange("p (b h t) -> p b h t", h=H, t=TD)
                V.tensor_tensor(v, v, seq(s_selT[0:rows, m]).unsqueeze(2).to_broadcast([rows, NSEQ, H, TD]), ALU.add)\
                    .then_inc(s_biased, 1)
            for g in range(2):
                dve.wait_ge(s_rows, g + 1)
                step(V.tensor_copy(s_row[:, g], pa[2 + g][:, 0:PAST + TS]))
                settle()
                V.tensor_reduce(s_stat[:, g, 0:1], s_row[:, g], AX.X, ALU.max, negate=True).then_inc(s_rowmax, 1)
            for g in range(2):
                dve.wait_ge(s_exped, g + 1)
                step(V.reciprocal(s_stat[:, g, 2:3], s_stat[:, g, 1:2]))
                settle()
                V.tensor_scalar(s_row[:, g], s_row[:, g], s_stat[:, g, 2:3], None, ALU.mult).then_inc(s_normed, 1)
            dve.wait_ge(s_back, 1)
            V.tensor_copy(s_prT[:, 0:NPAGES], pa[0][:, :].rearrange("p (m r) -> p m r", m=NPAGES))\
                .then_inc(s_back_copied, 1)
            V.tensor_copy(s_prT[0:TS, NPAGES], pa[1][0:TS, 0:256]).then_inc(s_back_copied, 1)
            dve.wait_ge(s_mixed, 1)
            V.tensor_copy(attn[:, :, TP:T].rearrange("p h (b t) -> p b h t", t=TD),
                          pa[2][:, 0:256].rearrange("p (b h t) -> p b h t", h=H, t=TD)).then_inc(s_mixed_copied, 1)

            for n in range(KC):
                key = ("attn_out", n)
                dve.wait_ge(tile_done, TILE[key] + 1)
                V.tensor_tensor(ga[:, n], lin[BANK[key]][:, 0:T], ga[:, n], ALU.mult).then_inc(gated, 1)
            dve.wait_ge(gated, 2 * KC)
            V.tensor_tensor(ga[:, :, :], ga[:, :, :], gb[:, :, :], ALU.add).then_inc(merged, 1)

            def residual(k, src, which, dst, done):
                V.scalar_tensor_tensor(dst[:, k, 0:TP], src[0], mod[:, which, k, 0:1], x[:, k, 0:TP],
                                       ALU.mult, ALU.add).then_inc(done, 1)
                tmp = dtmp_early if which == 2 else dtmp
                V.tensor_tensor(seq(tmp), seq(src[1]), mod[:, which, k, 1:NG].unsqueeze(2).to_broadcast([P, NSEQ, TD]),
                                ALU.mult).then_inc(done, 1)
                dve.wait_ge(done, 3 * k + 2)
                V.tensor_tensor(dst[:, k, TP:T], tmp, x[:, k, TP:T], ALU.add).then_inc(done, 1)
                dve.wait_ge(done, 3 * k + 3)

            dtmp_early = sig[:, 0, 0:TS]
            for n in range(KC):
                key = ("out", n)
                dve.wait_ge(tile_done, TILE[key] + 1)
                bank = lin[BANK[key]]
                residual(n, (bank[:, 0:TP], bank[:, TP:T]), 2, x, x1_ready)
            inv_root(4, rstd)
            root(3)
            modulate(x, h2, 1, h2_ready)

            for grp in range(4):
                dve.wait_ge(pscore_copied, (grp + 1) * NT)
                units = [(t, n) for t in range(NT) for n in range(4 * grp, 4 * grp + 4)]
                nu = len(units)

                def each(fn):
                    for t, n in units:
                        rows = tokens(t)[1]
                        settle(nu - 1)
                        step(fn(rows, t, n))

                each(lambda r, t, n: V.max(out=va[0:r, t, n, 0:8], in_=sc[0:r, t, n]))
                each(lambda r, t, n: V.max_index(out=ix[0:r, t, n, 0:8], in_max=va[0:r, t, n, 0:8],
                                                 in_values=sc[0:r, t, n]))
                each(lambda r, t, n: V.match_replace(out=scw[0:r, t, n], in_to_replace=va[0:r, t, n, 0:8],
                                                     in_values=sc[0:r, t, n], imm_value=TAKEN))
                each(lambda r, t, n: V.max(out=va[0:r, t, n, 8:16], in_=scw[0:r, t, n]))
                each(lambda r, t, n: V.max_index(out=ix[0:r, t, n, 8:16], in_max=va[0:r, t, n, 8:16],
                                                 in_values=scw[0:r, t, n]))
                settle()
                units = [(t, h) for t in range(NT) for h in (2 * grp, 2 * grp + 1)]
                nu = len(units)
                each(lambda r, t, h: V.tensor_tensor(
                    cand[0:r, t, h].rearrange("p (a b) -> p a b", b=PTOP),
                    va[0:r, t, 2 * h].unsqueeze(2).to_broadcast([r, PTOP, PTOP]),
                    va[0:r, t, 2 * h + 1].unsqueeze(1).to_broadcast([r, PTOP, PTOP]), ALU.add))
                each(lambda r, t, h: V.max(out=tv[0:r, t, h, 0:8], in_=cand[0:r, t, h]))
                each(lambda r, t, h: V.max_index(out=tj[0:r, t, h, 0:8], in_max=tv[0:r, t, h, 0:8],
                                                 in_values=cand[0:r, t, h]))
                each(lambda r, t, h: V.match_replace(out=cand[0:r, t, h], in_to_replace=tv[0:r, t, h, 0:8],
                                                     in_values=cand[0:r, t, h], imm_value=TAKEN))
                each(lambda r, t, h: V.max(out=tv[0:r, t, h, 8:16], in_=cand[0:r, t, h]))
                each(lambda r, t, h: V.max_index(out=tj[0:r, t, h, 8:16], in_max=tv[0:r, t, h, 8:16],
                                                 in_values=cand[0:r, t, h]))
                settle()
            for t in range(NT):
                r = tokens(t)[1]
                step(V.tensor_copy(gsum[0:r, t, :, 0], tv[0:r, t, :, 0]))
            settle()
            for t in range(NT):
                r = tokens(t)[1]
                V.tensor_tensor(tv[0:r, t], tv[0:r, t], gsum[0:r, t, :, 0].unsqueeze(2)
                                .to_broadcast([r, PH, PTOP]), ALU.subtract).then_inc(top_max, 1)
            for t in range(NT):
                r = tokens(t)[1]
                flat_j = tj[0:r, t].rearrange("p h k -> p (h k)")
                step(V.tensor_single_scalar(tab_u[0:r, 0, t], flat_j, 4, ALU.logical_shift_right))
                step(V.tensor_single_scalar(tab_u[0:r, 1, t], flat_j, PTOP - 1, ALU.bitwise_and))
                step(V.tensor_copy(ixf[0:r, t], ix[0:r, t]))
            settle()
            for t in range(NT):
                r = tokens(t)[1]
                for w in range(2):
                    step(V.tensor_copy(tab[0:r, w, t], tab_u[0:r, w, t]))
            settle()
            for t in range(NT):
                r = tokens(t)[1]
                for w in range(2):
                    step(V.tensor_tensor(eq[0:r], tab[0:r, w, t].unsqueeze(2).to_broadcast([r, PH * PTOP, PTOP]),
                                         iota[0:r, 0:PTOP].unsqueeze(1).to_broadcast([r, PH * PTOP, PTOP]),
                                         ALU.is_equal))
                    settle()
                    eq4 = eq[0:r].rearrange("p (h k) a -> p h k a", k=PTOP)
                    idx = ixf[0:r, t].rearrange("p (h w) a -> p w h a", w=2)[:, w]
                    step(V.tensor_tensor(eq4, eq4, idx.unsqueeze(2).to_broadcast([r, PH, PTOP, PTOP]), ALU.mult))
                    settle()
                    step(V.tensor_reduce(tsel[0:r, t, w], eq[0:r], AX.X, ALU.add))
                    settle()
            dve.wait_ge(top_exp, NT)
            for t in range(NT):
                r = tokens(t)[1]
                step(V.tensor_reduce(gsum[0:r, t, :, 1], tv[0:r, t], AX.X, ALU.add))
            settle()
            for t in range(NT):
                r = tokens(t)[1]
                step(V.reciprocal(gsum[0:r, t, :, 1], gsum[0:r, t, :, 1]))
            settle()
            for t in range(NT):
                r = tokens(t)[1]
                V.tensor_tensor(tsel[0:r, t, 2].rearrange("p (h k) -> p h k", k=PTOP), tv[0:r, t],
                                gsum[0:r, t, :, 1].unsqueeze(2).to_broadcast([r, PH, PTOP]), ALU.mult)\
                    .then_inc(picks, 1)

            dve.wait_ge(picks_copied, 3)

            def one_hot(base, slot, first):
                for j in range(4):
                    col = base + j if isinstance(base, int) else base + j
                    V.tensor_scalar(hot2[:, slot + j], iota[:, :], picked[:, 1, bass.ds(col, 1)], None, ALU.is_equal)\
                        .then_inc(hot_ready, 1)
                    V.tensor_scalar(hot1[:, slot + j], iota[:, :], picked[:, 0, bass.ds(col, 1)],
                                    picked[:, 2, bass.ds(col, 1)], ALU.is_equal, ALU.mult).then_inc(hot_ready, 1)

            for b in range(2):
                one_hot(4 * b, 4 * b, True)
            with dve.Fori(1, T // NH) as g:
                for b in range(2):
                    dve.wait_ge(gate_prod, g * 2 + (b - 1))
                    one_hot(g * NH + 4 * b, 4 * b, False)

            dve.wait_ge(gate_copied, T // 4)
            for c in range(2):
                dve.wait_ge(gelued, c + 1)
                V.tensor_tensor(wgt[:, c], act[:, c], gate_mat[:, c], ALU.mult).then_inc(weighted, 1)
            with dve.Fori(1, NSUB // 2) as g:
                for c in range(2):
                    dve.wait_ge(gelued, g * 2 + (c + 1))
                    dve.wait_ge(o_done, g * 2 + (c - 1))
                    V.tensor_tensor(wgt[:, c], act[:, c],
                                    gate_mat[:, bass.ds(g * 2 + c, 1)].rearrange("p o t -> p (o t)"), ALU.mult)\
                        .then_inc(weighted, 1)
            dve.wait_ge(o_done, NSUB)
            for k in range(KC):
                src = (ps[k // 2][:, (k % 2) * TP:(k % 2 + 1) * TP], ps[4][:, k * TS:(k + 1) * TS])
                residual(k, src, 5, h2, y_out)

        @block.tensor
        def _(pe):
            MM = nc.tensor.matmul

            def sums(src, out, n):
                for k in range(n):
                    last = MM(out[:, 0:T], ones[:, :], src[:, k], start=(k == 0), stop=(k == n - 1))
                return last

            def linear(key, rhs):
                n = BANKED.index(key)
                free(n)
                pe.wait_ge(tile_loaded[TILE[key] % R], 16 * (TILE[key] // R + 1))
                w = ring[:, TILE[key] % R, :].rearrange("p (k m) -> p k m", m=P)
                for k in range(KC):
                    last = MM(lin[n % NBANK][:, 0:T], w[:, k], rhs[:, k], start=(k == 0), stop=(k == KC - 1))
                last.then_inc(tile_done, 1)

            def free(n):
                if n < NBANK:
                    return
                kind, m = key = BANKED[n - NBANK]
                if kind == "conv_a":
                    pe.wait_ge(z_ready, 2 * m + 2)
                elif kind == "conv_g":
                    pe.wait_ge(sig_ready, m + 1)
                elif kind in ("conv_out", "attn_out"):
                    pe.wait_ge(gated, m + 1 + (KC if kind == "attn_out" else 0))
                elif kind == "out":
                    pe.wait_ge(x1_ready, 3 * m + 2)
                else:
                    pe.wait_ge(act_evac, ACT_EVAC[key])

            pe.wait_ge(zeroed, 2)
            pe.wait_ge(squares, 1)
            sums(xn, stb, KC).then_inc(stats, 1)
            pe.wait_ge(c_silu, 1)

            def ada_columns(g):
                for b in range(2):
                    for s in range(R):
                        pe.wait_ge(tile_loaded[s], g * 32 + 16 * (b + 1))
                        w = ring[:, s, :].rearrange("p (k m) -> p k m", m=ADA_COLS)
                        for j in range(2):
                            k = 2 * s + j
                            last = MM(lin[b][0:NG, :], cs[:, k], w[:, j], start=(k == 0), stop=(k == KC - 1))
                        last.then_inc(tile_done, 1)

            ada_columns(0)
            with pe.Fori(1, NADA // R // 2) as g:
                pe.wait_ge(ada_copied, g * 2)
                ada_columns(g)
            pe.wait_ge(ada_copied, NADA // R)
            pe.wait_ge(consts, 64)
            for n in range(6 * KC):
                last = nc.tensor.transpose(pa[0][:, n * NG:(n + 1) * NG], m_row[:, n * P:(n + 1) * P],
                                           ident[0:NG, 0:NG])
            last.then_inc(mod_turned, 1)

            pe.wait_ge(h_ready, KC + 1)
            for k in range(KC):
                linear(("conv_a", k), hT)
                linear(("conv_g", k), hT)
            linear(("ki", 0), hT)
            for n in range(4):
                linear(("qi", n), hT)
            pe.wait_ge(vw_in, 16)
            for t in range(NT):
                n = BANKED.index(("v", t))
                free(n)
                cols, rows = tokens(t)
                for k in range(KC):
                    last = MM(lin[n % NBANK][0:rows, 0:VW], hT[:, k, cols], v_w[:, k], start=(k == 0),
                              stop=(k == KC - 1))
                last.then_inc(v_done, 1)
            for key in QK:
                linear(key, hT)
            for n in range(KC):
                linear(("gate_a", n), hT)
            pe.wait_ge(y_ready, KC)
            sums(y, stb, KC).then_inc(stats, 1)
            for n, key in enumerate(QK):
                pe.wait_ge(act_evac, ACT_EVAC[key])
                if n >= 2:
                    pe.wait_ge(qk_var, n - 1)
                MM(pa[n % 2][:, 0:T], ones[:, :], sq_qk[n], start=True, stop=True).then_inc(qk_sums, 1)
            pe.wait_ge(squares, 2)
            sums(xn, stb, KC).then_inc(stats, 1)
            for n in range(KC):
                linear(("gate_b", n), hT)
            pe.wait_ge(qk_var, len(QK))
            for n in range(NQ * IH):
                t, h = divmod(n, IH)
                half = slice(ID * (h % 2), ID * (h % 2) + ID)
                if n >= 2:
                    pe.wait_ge(idx_relu, n - 1)
                MM(pa[n % 2][:, 0:P * (t + 1)], qi[half, h // 2, tokens(t)[0]], ki[half, 0:P * (t + 1)],
                   start=True, stop=True).then_inc(idx_prod, 1)
            pe.wait_ge(idx_relu, NQ * IH)
            pe.wait_ge(cache_in, 16 * 4 * NSEQ * NPAGES)
            for m in range(NPAGES):
                for par in range(2):
                    half = slice(ID * par, ID * par + ID)
                    for b in range(NSEQ):
                        out = pa[par][:, m * 128:m * 128 + 128]\
                            .rearrange("p (pair s) -> p pair s", s=TS)[:, :, b * TD:b * TD + TD]
                        MM(out, cache_i[half, b * NPAGES + m], qi[half, :, TP + b * TD:TP + b * TD + TD],
                           start=True, stop=True)
            for par in range(2):
                half = slice(ID * par, ID * par + ID)
                last = MM(pa[par][0:TS, 256:384].rearrange("p (a b) -> p a b", b=TS),
                          ki[half, TP:T], qi[half, :, TP:T], start=True, stop=True)
            last.then_inc(s_idx_prod, 1)
            pe.wait_ge(s_wi, 2)
            MM(pa[2][:, 0:IH * TS], ones[0:TS, :], wi_diag[0:TS].rearrange("p a b -> p (a b)"), start=True, stop=True)\
                .then_inc(s_wi_prod, 1)
            pe.wait_ge(s_summed, 2)
            for m in range(NPAGES):
                nc.tensor.transpose(pa[3][0:TS, m * P:(m + 1) * P], s_iscT[:, m], ident[:, :])
            nc.tensor.transpose(pa[3][0:TS, PAST:PAST + TS], s_iscT[0:TS, NPAGES], ident[0:TS, 0:TS])\
                .then_inc(s_turned, 1)
            pe.wait_ge(conv_ready, 1)
            for n in range(KC):
                linear(("conv_out", n), y)
            pe.wait_ge(qk_ready, 4)
            pe.wait_ge(s_relued, 4)
            pe.wait_ge(s_sel_ready, 1)
            for n in range(NQ * H + 2):
                if n < NQ * H:
                    t, h = divmod(n, H)
                    if n >= 2:
                        pe.wait_ge(biased, n - 1)
                    MM(pa[n % 2][:, 0:P * (t + 1)], q[:, h, tokens(t)[0]], kT[:, h // HG, 0:P * (t + 1)],
                       start=True, stop=True).then_inc(logits, 1)
                if 1 <= n <= NQ * H:
                    m = n - 1
                    pe.wait_ge(normed, m + 1)
                    if m >= 1:
                        pe.wait_ge(turned_copied, m)
                    for blk in range(m // H + 1):
                        last = nc.tensor.transpose(pa[2][:, blk * P:(blk + 1) * P],
                                                   lg[:, m % 2, blk * P:(blk + 1) * P], ident[:, :])
                    last.then_inc(turned, 1)
                if n >= 2:
                    m = n - 2
                    t, h = divmod(m, H)
                    pe.wait_ge(turned_copied, m + 1)
                    if m >= 1:
                        pe.wait_ge(mixed_copied, m)
                    kv = h // HG
                    for blk in range(t + 1):
                        last = MM(pa[3][:, 0:P], vtok[:, blk, kv * P:(kv + 1) * P], prT[:, m % 2, blk * P:(blk + 1) * P],
                                  start=(blk == 0), stop=(blk == t))
                    last.then_inc(mixed, 1)
            pe.wait_ge(turned_copied, NQ * H)
            for m in range(NPAGES):
                nc.tensor.transpose(pa[2][:, m * TS:(m + 1) * TS], s_sel[0:TS, m * P:(m + 1) * P], ident[0:TS, 0:TS])
            nc.tensor.transpose(pa[2][0:TS, NPAGES * TS:(NPAGES + 1) * TS], s_sel[0:TS, PAST:PAST + TS],
                                ident[0:TS, 0:TS]).then_inc(s_selT_prod, 1)
            pe.wait_ge(biased, NQ * H)
            for m in range(NPAGES):
                for b in range(NSEQ):
                    for kv in range(KV):
                        at = m * 256 + b * H * TD + kv * HG * TD
                        MM(pa[0][:, at:at + HG * TD].rearrange("p (h t) -> p h t", t=TD),
                           cache_k[:, b * NPAGES + m, kv],
                           q[:, kv * HG:(kv + 1) * HG, TP + b * TD:TP + b * TD + TD], start=True, stop=True)
            for kv in range(KV):
                out = pa[1][0:TS, 0:256].rearrange("p (b h t) -> p h b t", h=H, t=TD)[:, kv * HG:(kv + 1) * HG]
                last = MM(out, kT[:, kv, TP:T],
                          q[:, kv * HG:(kv + 1) * HG, TP:T].rearrange("p h (b t) -> p h b t", t=TD),
                          start=True, stop=True)
            last.then_inc(s_logits, 1)
            pe.wait_ge(s_biased, NPAGES + 1)
            pe.wait_ge(mixed_copied, NQ * H)
            for g in range(2):
                for m in range(NPAGES):
                    nc.tensor.transpose(pa[2 + g][:, m * P:(m + 1) * P], s_lT[:, m, g * P:(g + 1) * P], ident[:, :])
                nc.tensor.transpose(pa[2 + g][:, PAST:PAST + TS], s_lT[0:TS, NPAGES, g * P:(g + 1) * P],
                                    ident[0:TS, 0:TS]).then_inc(s_rows, 1)
            pe.wait_ge(s_normed, 2)
            for g in range(2):
                for m in range(NPAGES):
                    nc.tensor.transpose(pa[0][:, m * 256 + g * P:m * 256 + (g + 1) * P],
                                        s_row[:, g, m * P:(m + 1) * P], ident[:, :])
                last = nc.tensor.transpose(pa[1][0:TS, g * P:(g + 1) * P], s_row[:, g, PAST:PAST + TS], ident[:, :])
            last.then_inc(s_back, 1)
            pe.wait_ge(s_back_copied, 2)
            for b in range(NSEQ):
                for kv in range(KV):
                    at = b * H * TD + kv * HG * TD
                    cols = slice(kv * P, (kv + 1) * P)
                    for m in range(NPAGES):
                        MM(pa[2][:, at:at + HG * TD], cache_v[:, b * NPAGES + m, cols], s_prT[:, m, at:at + HG * TD],
                           start=(m == 0), stop=False)
                    last = MM(pa[2][:, at:at + HG * TD], vtok[0:TS, NQ, cols], s_prT[0:TS, NPAGES, at:at + HG * TD],
                              start=False, stop=True)
            last.then_inc(s_mixed, 1)
            pe.wait_ge(s_mixed_copied, 1)
            for n in range(KC):
                linear(("attn_out", n), attn)
            pe.wait_ge(merged, 1)
            for n in range(KC):
                linear(("out", n), ga)
            pe.wait_ge(squares, 3)
            sums(xn, stb, KC).then_inc(stats, 1)
            pe.wait_ge(h2_ready, KC + 1)
            pe.wait_ge(peer_in, 32)
            for n in range(2 * PH):
                linear(("peer_q", n), h2)
                if n % 4 == 3:
                    pe.wait_ge(act_evac, ACT_EVAC["peer_q", n])
                    for t in range(NT):
                        m = n // 4 * NT + t
                        cols, rows = tokens(t)
                        if m >= 4:
                            pe.wait_ge(pscore_copied, m - 3)
                        for j in range(4):
                            last = MM(pa[m % 4][0:rows, j * P:(j + 1) * P], qh[:, n - 3 + j, cols], sk[:, j % 2],
                                      start=True, stop=True)
                        last.then_inc(pscore, 1)
            pe.wait_ge(pscore_copied, 4 * NT)
            pe.wait_ge(picks, NT)
            for n in range(3):
                for t in range(NT):
                    cols, rows = tokens(t)
                    last = nc.tensor.transpose(pa[n][:, cols], tsel[0:rows, t, n], ident[0:rows, 0:rows])
                last.then_inc(picks_turned, 1)
            pe.wait_ge(act_evac, ACT_EVAC["peer_q", 2 * PH - 1])

            def gate_tokens(b):
                for j in range(4):
                    last = MM(ps[b][:, j * P:(j + 1) * P], hot2[:, 4 * b + j], hot1[:, 4 * b + j], start=True, stop=True)
                last.then_inc(gate_prod, 1)

            for b in range(2):
                pe.wait_ge(hot_ready, 8 * (b + 1))
                gate_tokens(b)
            with pe.Fori(1, T // NH) as g:
                for b in range(2):
                    pe.wait_ge(hot_ready, g * 16 + 8 * (b + 1))
                    pe.wait_ge(gate_copied, g * 2 + (b - 1))
                    gate_tokens(b)

            def scores(c, loaded):
                pe.wait_ge(tile_loaded[U_SLOT[c]], loaded)
                u = ring[:, U_SLOT[c], :].rearrange("p (k m) -> p k m", m=P)
                for k in range(KC):
                    last = MM(ps[5 + c][:, 0:T], u[:, k], h2[:, k], start=(k == 0), stop=(k == KC - 1))
                last.then_inc(u_done, 1)

            def outputs(c, loaded, value):
                pe.wait_ge(tile_loaded[V_SLOT[c]], loaded)
                pe.wait_ge(weighted, value)
                v = ring[:, V_SLOT[c], :].rearrange("p (k m) -> p k m", m=P)
                for k in range(KC):
                    MM(ps[k // 2][:, (k % 2) * TP:(k % 2 + 1) * TP], v[:, k], wgt[:, c, 0:TP], start=False,
                       stop=False, skip_group_check=True)
                    last = MM(ps[4][:, k * TS:(k + 1) * TS], v[:, k], wgt[:, c, TP:T], start=False,
                              stop=False, skip_group_check=True)
                last.then_inc(o_done, 1)

            def use(slot):
                return (NLIN + R - 1 - slot) // R

            u0, v0 = [16 * use(s) for s in U_SLOT], [16 * use(s) for s in V_SLOT]
            pe.wait_ge(gate_copied, T // 4)
            pe.wait_ge(picks_copied, 3)
            pe.wait_ge(zeroed, 3)
            for b in range(5):
                MM(ps[b][:, :], zeros[:, 0:P], zeros, start=True, stop=False, skip_group_check=True)
            scores(0, u0[0] + 16)
            scores(1, u0[1] + 16)
            outputs(0, v0[0] + 16, 1)
            pe.wait_ge(gelued, 1)
            scores(0, u0[0] + 32)
            outputs(1, v0[1] + 16, 2)
            with pe.Fori(1, NSUB // 2 - 1) as g:
                pe.wait_ge(gelued, g * 2)
                scores(1, g * 16 + (u0[1] + 16))
                outputs(0, g * 16 + (v0[0] + 16), g * 2 + 1)
                pe.wait_ge(gelued, g * 2 + 1)
                scores(0, g * 16 + (u0[0] + 32))
                outputs(1, g * 16 + (v0[1] + 16), g * 2 + 2)
            half = NSUB // 2
            pe.wait_ge(gelued, NSUB - 2)
            scores(1, u0[1] + 16 * half)
            outputs(0, v0[0] + 16 * half, NSUB - 1)
            outputs(1, v0[1] + 16 * half, NSUB)


def constants():
    p, s = np.arange(P), np.arange(TP)
    pos = (np.arange(NQ)[None, :] * P + p[:, None])[:, :, None]
    dist = (pos - s).astype(np.float32)
    slope = 2.0 ** (-8.0 * np.arange(1, H + 1) / H)
    t4 = np.arange(TD)
    key = np.arange(NPAGES)[None, :] * P + p[:, None]
    past = -slope[:, None] * (PAST + t4 - key[:, :, None, None])
    past = np.broadcast_to(past[:, :, None], (P, NPAGES, NSEQ, H, TD))
    ts = np.arange(TS)
    new = -slope[:, None] * (t4 - (ts % TD)[:, None, None])
    new = np.broadcast_to(new[:, None], (TS, NSEQ, H, TD))
    own = np.zeros((TS, PAST + TS))
    same = (ts[:, None] // TD == ts // TD) & (ts <= ts[:, None])
    own[:, PAST:] = np.where(same, 0.0, NEG)
    made = {
        "ident": np.eye(P), "iota": np.broadcast_to(p, (P, P)), "dist": dist,
        "causal": np.where(dist >= 0, 0.0, NEG), "alibi_past": past.reshape(P, NPAGES, -1),
        "alibi_new": new.reshape(TS, -1), "own": own,
    }
    return {n: np.ascontiguousarray(v, dtype=np.float32) for n, v in made.items()}


def layouts(v):
    def chunks(m):
        return m.reshape(-1, m.shape[-1] // P, P).transpose(2, 1, 0)

    def cut(w):
        return w.reshape(KC, P, -1, P).transpose(2, 1, 0, 3).reshape(-1, P, D)

    w_in = v["w_in"]
    edges = np.cumsum([H * P, KV * P, KV * P, IH * ID, ID, IH, 2 * D, 2 * D])
    w_q, w_k, w_v, w_qi, w_ki, w_wi, w_conv, w_gate = (
        w_in[:, lo:hi] for lo, hi in zip([0, *edges[:-1]], edges))
    tiles = {"conv_a": cut(w_conv[:, :D]), "conv_g": cut(w_conv[:, D:]), "ki": cut(np.concatenate([w_ki, w_ki], 1)),
             "qi": cut(w_qi), "k": cut(w_k), "q": cut(w_q), "gate_a": cut(w_gate[:, :D]), "gate_b": cut(w_gate[:, D:]),
             "conv_out": cut(v["w_conv_out"]), "attn_out": cut(v["w_o_attn"]), "out": cut(v["w_out"]),
             "peer_q": cut(v["w_q_peer"])}
    stream = np.empty((NTILES, P, D), np.float32)
    stream[:NADA] = v["w_ada"].reshape(R, 2, P, -1, ADA_COLS).transpose(3, 0, 2, 1, 4).reshape(NADA, P, D)
    for key, n in TILE.items():
        stream[n] = tiles[key[0]][key[1]]
    stream[NLIN::2] = v["u_emb"].reshape(NSUB, P, KC, P).transpose(0, 3, 2, 1).reshape(NSUB, P, D)
    stream[NLIN + 1::2] = v["v_emb"].reshape(NSUB, P, D)
    xs = np.concatenate([v["x_prompt"].reshape(TP, D), v["x_sample"].reshape(TS, D)])
    cond = np.concatenate([v["c_prompt"], v["c_sample"]])
    vw = np.concatenate([w_v, w_wi], 1)
    pool = v["cache_k"].shape[0]
    made = {
        "stream": stream, "xT": chunks(xs), "cT": chunks(cond), "badaT": v["b_ada"].reshape(-1, P).T,
        "gnorm": chunks(np.stack([v["g_norm1"], v["g_norm2"]])).transpose(0, 2, 1),
        "v_w": vw.reshape(KC, P, VW).transpose(1, 0, 2),
        "stateT": v["state_conv"].reshape(NSEQ, LEFT, KC, P).transpose(3, 2, 0, 1),
        "wdw": v["w_dw"].reshape(CW, KC, P).transpose(2, 1, 0),
        "cvec": chunks(np.stack([v["b_dw"], v["ln_g"], v["ln_b"]])).transpose(0, 2, 1),
        "qkg": np.stack([v["g_q"], v["g_k"]], 1),
        "cache_k": v["cache_k"].transpose(0, 3, 2, 1), "cache_v": v["cache_v"].reshape(pool, PAGE, KV * P),
        "cache_i": v["cache_idx_k"].transpose(0, 2, 1), "pages": v["page_table"].reshape(1, -1),
        "sub_keys": np.stack([v["sub_keys1"].T, v["sub_keys2"].T]),
    }
    return {n: np.ascontiguousarray(m) for n, m in made.items()} | constants()


OUTS = {"yT": (P, KC, T), "kT": (P, KV, T), "v_prompt": (P, NQ, KV * P), "v_sample": (TS, KV * P), "kiT": (ID, T),
        "convpT": (P, KC, LEFT), "convsT": (P, KC, NSEQ, LEFT)}


def kernel(**inputs):
    import concourse.bacc as bacc
    from concourse.bass_utils import run_bass_kernel_spmd

    arrays = layouts({n: np.asarray(v) for n, v in inputs.items()})
    nc = bacc.Bacc("TRN2", target_bir_lowering=False, num_devices=1)
    aps = {}
    for name, m in arrays.items():
        aps[name] = nc.dram_tensor(f"in_{name}", m.shape, mybir.dt.from_np(m.dtype), kind="ExternalInput").ap()
    for name, shape in OUTS.items():
        aps[name] = nc.dram_tensor(f"out_{name}", shape, mybir.dt.float32, kind="ExternalOutput").ap()
    build(nc, aps)
    got = run_bass_kernel_spmd(nc, [{f"in_{n}": m for n, m in arrays.items()}], core_ids=[0]).results[0]
    out = {n: got[f"out_{n}"] for n in OUTS}
    y = out["yT"].transpose(2, 1, 0).reshape(T, D)
    k = out["kT"].transpose(2, 1, 0)
    ki = out["kiT"].T
    return (y[:TP].reshape(1, TP, D), y[TP:].reshape(NSEQ, TD, D),
            k[:TP].reshape(1, TP, KV, P), out["v_prompt"].transpose(1, 0, 2).reshape(1, TP, KV, P),
            ki[:TP].reshape(1, TP, ID), out["convpT"].transpose(2, 1, 0).reshape(1, LEFT, D),
            k[TP:].reshape(NSEQ, TD, KV, P), out["v_sample"].reshape(NSEQ, TD, KV, P),
            ki[TP:].reshape(NSEQ, TD, ID), out["convsT"].transpose(2, 3, 1, 0).reshape(NSEQ, LEFT, D))
```

```python
from contextlib import ExitStack

import numpy as np

import concourse.bass as bass
from concourse import mybir

P = 128
D = 1024
KC = D // P
TP, NSEQ, TD = 256, 8, 4
TS = NSEQ * TD
T = TP + TS
NQ = TP // P
NT = NQ + 1
NG = 1 + NSEQ
H, KV = 8, 2
HG = H // KV
IH, ID = 8, 64
CW = 31
LEFT = CW - 1
PAGE, NPAGES = 128, 2
PAST = PAGE * NPAGES
PROMPT_TOPK = TP // 4
SAMPLE_TOPK = (PAST + TD) // 4
NSUB, PH, PTOP = 128, 8, 16
EPS = 1e-6
NEG = -1e30
TAKEN = -3e38
R = 4
ADA_COLS = 512
NGRP = 6 * D // ADA_COLS
NFIRST = 2 * D // ADA_COLS
CG = ADA_COLS // P
QK_SCALE = P ** -0.5
IDX_SCALE = ID ** -0.5
HEAD_SCALE = IH ** -0.5
VW = KV * P + IH

CONV = [(kind, k) for k in range(KC) for kind in ("conv_a", "conv_g")]
LINEAR = (CONV[:12] + [("ki", 0)] + [("qi", n) for n in range(4)] + CONV[12:]
          + [("k", n) for n in range(KV)] + [("q", n) for n in range(H)]
          + [("gate_a", n) for n in range(KC)] + [("gate_b", n) for n in range(KC)]
          + [("conv_out", n) for n in range(KC)] + [("ada", g) for g in range(NFIRST, NGRP)]
          + [("attn_out", n) for n in range(KC)]
          + [("out", n) for n in range(KC)] + [("peer_q", n) for n in range(2 * PH)])
TILE, NLIN = {}, NFIRST * R
for key in LINEAR:
    TILE[key] = NLIN
    NLIN += R if key[0] == "ada" else 1
NTILES = NLIN + 2 * NSUB
MIXED = T // 4
BEFORE = 36
AFTER = NSUB - MIXED - BEFORE
assert BEFORE % R == 0 and MIXED % R == 0 and AFTER % R == 0 and NSUB % R == 0


def slot_of(c):
    return (NLIN + c) % R


def loads_before(c):
    return (NLIN + c) // R


BANKED = []
for key in LINEAR:
    if key[0] == "conv_a":
        continue
    if key == ("k", 0):
        BANKED += [("v", t) for t in range(NT)]
    BANKED.append(key)
NBANK = 3
BANK = {key: n % NBANK for n, key in enumerate(BANKED)}
ACT_EVAC, n_evac = {}, 0
for key in BANKED:
    if key[0] in ("ki", "qi", "v", "gate_a", "gate_b", "ada", "peer_q"):
        n_evac += 1
        ACT_EVAC[key] = n_evac
    if key[0] in ("k", "q"):
        n_evac += 2
        ACT_EVAC[key] = n_evac
QK = [("k", n) for n in range(KV)] + [("q", n) for n in range(H)]


def tokens(t):
    return (slice(t * P, t * P + P), P) if t < NQ else (slice(TP, T), TS)


def build(nc, a):
    f32, f32r, bf16 = mybir.dt.float32, mybir.dt.float32r, mybir.dt.bfloat16
    i32, u32 = mybir.dt.int32, mybir.dt.uint32
    ALU, ACT, AX = mybir.AluOpType, mybir.ActivationFunctionType, mybir.AxisListType

    with ExitStack() as ctx:
        def sb(name, *shape, dt=f32):
            return ctx.enter_context(nc.sbuf_tensor(name, [P] + list(shape), dt))

        def sem(name):
            return ctx.enter_context(nc.semaphore(name))

        x = sb("x", KC, T)
        mod = sb("mod", 6, KC, NG)
        scl = sb("scl", 2, KC, NG)
        ident = sb("ident", P)
        ones = sb("ones", P)
        iota = sb("iota", P, dt=bf16)
        gnorm = sb("gnorm", 2, KC)
        ring = sb("ring", R, D)
        split = sb("split", 2, 2, D, dt=f32r)
        h2r = sb("h2r", 2, KC * T, dt=f32r)
        pages = sb("pages", NSEQ * NPAGES, dt=i32)
        NBIG = NSUB * T
        big = sb("big", NBIG)
        gate_mat = big[:, :].rearrange("p (i t) -> p i t", t=T)

        class Region:

            def __init__(self, tensor, size):
                self.tensor, self.size, self.at = tensor, size, 0

            def take(self, *shape, dt=None):
                n = int(np.prod(shape))
                v = self.tensor[:, self.at:self.at + n]
                self.at += n
                assert self.at <= self.size, (self.at, self.size)
                if dt is not None:
                    v = v.bitcast(dt)
                names = "abcd"[:len(shape)]
                if len(shape) > 1:
                    v = v.rearrange(f"p ({' '.join(names)}) -> p {' '.join(names)}",
                                    **{c: s for c, s in zip(names[1:], shape[1:])})
                return v

        early = Region(big, NBIG)
        hT = early.take(KC, T)
        cT = hT[:, 0, 0:KC * NG].rearrange("p (k g) -> p k g", g=NG)
        iota_f = hT[:, 3, 0:P]
        xn = early.take(KC, T)
        q = early.take(H, T)
        kT = early.take(KV, T)
        qi = early.take(4, T)
        ki = early.take(T)
        vtok = early.take(NT, VW)
        z_at = early.at
        zp = early.take(KC, LEFT + TP)
        zs = early.take(KC, NSEQ, LEFT + TD)
        m_at = early.at
        y = early.take(KC, T)
        ga = early.take(KC, T)
        gb = early.take(KC, T)
        attn = early.take(KC, T)
        m_row = big[0:NG, m_at:m_at + NFIRST * ADA_COLS]
        m_row2 = big[0:NG, 0:2 * ADA_COLS].rearrange("p (s c) -> p s c", s=2)
        v_w = attn[:, :, 0:VW]
        cache_k = early.take(NSEQ * NPAGES, KV, PAGE)
        cache_v = early.take(NSEQ * NPAGES, KV * P)
        i_at = early.at
        cache_i = early.take(NSEQ * NPAGES, PAGE)
        wdw = early.take(KC, CW)
        cvec = early.take(3, KC)
        qkg = early.take(2)
        dist_w = early.take(TP)
        causal_w = early.take(TP)
        dist = [dist_w[:, TP - P * (t + 1):] for t in range(NQ)]
        causal = [causal_w[:, TP - P * (t + 1):] for t in range(NQ)]
        sq_qk = [gb[:, n] for n in range(KV)] + [attn[:, n] for n in range(H)]
        rz = Region(big, m_at)
        rz.at = z_at
        alibi_past = rz.take(NPAGES, NSEQ * H * TD)
        alibi_new = rz.take(NSEQ * H * TD)
        own = rz.take(PAST + TS)
        s_relu = rz.take(NPAGES, IH * TS)
        n_relu = rz.take(IH * TS)
        wi_all = rz.take(IH, TS)
        wi_diag = rz.take(IH, TS)
        s_iscT = rz.take(NPAGES + 1, TS)
        s_isc = rz.take(PAST + TS)
        s_sel = rz.take(PAST + TS)
        s_max8 = rz.take(8)
        r1 = Region(big, 2 * KC * T)
        r1.at = KC * T
        s_selT = r1.take(NPAGES + 1, TS)
        s_lT = r1.take(NPAGES + 1, NSEQ * H * TD)
        s_row = r1.take(2, PAST + TS)
        s_prT = s_lT
        s_stat = r1.take(2, 4)

        rstd = early.take(T)
        relu = early.take(2, TP)
        eps = early.take(1)
        cs = early.take(KC, NG)
        badaT = early.take(6 * KC)
        tap = early.take(3, NSEQ, TD)
        isc = early.take(NQ, TP)
        selb = early.take(NQ, TP)
        max8 = early.take(NQ, 8)
        stat = early.take(NQ * H, 3)
        sig = xn
        ri = Region(big, i_at + NSEQ * NPAGES * PAGE)
        ri.at = i_at
        bias_h = ri.take(2, TP)
        lg = ri.take(2, TP)
        prT = ri.take(2, TP)
        dtmp_early = ri.take(TS)


        late = Region(big, NBIG)
        h2 = late.take(KC, T)
        assert late.at == KC * T
        late.take(KC * T)
        qh = late.take(2 * PH, T)
        sk = late.take(2, NSUB)
        sc = late.take(NT, 2 * PH, NSUB)
        scw = late.take(NT, 2 * PH, NSUB)
        va = late.take(NT, 2 * PH, PTOP)
        ix = late.take(NT, 2 * PH, PTOP, dt=u32)
        ixf = late.take(NT, 2 * PH, PTOP)
        cand = sc.rearrange("p t (h c) k -> p t h (c k)", c=2)
        tv = late.take(NT, PH, PTOP)
        tj = late.take(NT, PH, PTOP, dt=u32)
        tab_u = late.take(2, NT, PH * PTOP, dt=u32)
        tab = late.take(2, NT, PH * PTOP)
        tsel = late.take(NT, 3, PH * PTOP)
        gsum = late.take(NT, PH, 2)
        eq = late.take(PH * PTOP, PTOP)
        parts = late.take(2 + 3, T)

        late_x = x[:, :, :].rearrange("p k t -> p (k t)")
        picked = late_x[:, 0:5 * T // 2].bitcast(bf16).rearrange("p (a t) -> p a t", t=T)
        NPARTS = 3
        NHOT = 4
        at = 5 * T // 2
        hot2 = sb("hot2", NHOT, P, dt=bf16)
        hot1 = late_x[:, at:at + NHOT * NPARTS * P // 2].bitcast(bf16)\
            .rearrange("p (s a i) -> p s a i", a=NPARTS, i=P)
        at += NHOT * NPARTS * P // 2
        act = late_x[:, at:at + 2 * T].rearrange("p (s t) -> p s t", t=T)
        assert at + 2 * T <= KC * T
        act_b = late_x[:, 0:R * T].rearrange("p (s t) -> p s t", t=T)
        wr = h2r[:, :, :].rearrange("p a n -> p (a n)")[:, 0:4 * T].rearrange("p (s a t) -> p s a t", a=2, t=T)
        end = Region(big, NBIG)
        xe = end.take(KC, T)
        ye = end.take(KC, T)
        dtmp = end.take(TS)
        act_dram = nc.dram_tensor("act_dram", [NSUB, P, T], f32, kind="Internal").ap()
        x_dram = nc.dram_tensor("x_dram", [P, KC, T], f32, kind="Internal").ap()

        ps = [ctx.enter_context(nc.psum_tensor(f"ps{b}", [P, 512], f32)) for b in range(8)]
        lin, stb, pa = ps[0:NBANK], ps[3], ps[4:8]

        tile_loaded = [sem(f"tile_loaded{s}") for s in range(R)]
        tile_done = sem("tile_done")
        v_done = sem("v_done")
        u_done = sem("u_done")
        o_done = sem("o_done")
        hi_ready = sem("hi_ready")
        lo_ready = sem("lo_ready")
        hi_used = sem("hi_used")
        act_stored = [sem(f"act_stored{s}") for s in range(2)]
        act_loaded = [sem(f"act_loaded{s}") for s in range(R)]
        x_stored = sem("x_stored")
        x_loaded = sem("x_loaded")
        h2_hi = sem("h2_hi")
        h2_lo = sem("h2_lo")
        hot_used = sem("hot_used")
        w_hi = sem("w_hi")
        w_lo = sem("w_lo")
        parts_ready = sem("parts_ready")
        conv_stored = sem("conv_stored")
        mask_in = sem("mask_in")
        inputs = sem("inputs")
        consts = sem("consts")
        conv_in = sem("conv_in")
        vw_in = sem("vw_in")
        pages_in = sem("pages_in")
        cache_in = sem("cache_in")
        attn_in = sem("attn_in")
        peer_in = sem("peer_in")
        zeroed = sem("zeroed")
        squares = sem("squares")
        stats = sem("stats")
        stat_r = sem("stat_r")
        c_sig = sem("c_sig")
        c_silu = sem("c_silu")
        ada_copied = sem("ada_copied")
        mod_turned = sem("mod_turned")
        h_ready = sem("h_ready")
        sig_ready = sem("sig_ready")
        z_ready = sem("z_ready")
        act_evac = sem("act_evac")
        qk_sums = sem("qk_sums")
        qk_root = sem("qk_root")
        qk_ready = sem("qk_ready")
        idx_prod = sem("idx_prod")
        idx_relu = sem("idx_relu")
        idx_used = sem("idx_used")
        y_prompt = sem("y_prompt")
        y_sample = sem("y_sample")
        y_centred = sem("y_centred")
        y_sig = sem("y_sig")
        y_scaled = sem("y_scaled")
        conv_ready = sem("conv_ready")
        gated = sem("gated")
        s_idx_prod = sem("s_idx_prod")
        s_wi = sem("s_wi")
        s_wi_prod = sem("s_wi_prod")
        s_relued = sem("s_relued")
        s_summed = sem("s_summed")
        s_turned = sem("s_turned")
        sel_ready = sem("sel_ready")
        logits = sem("logits")
        biased = sem("biased")
        row_max = sem("row_max")
        exped = sem("exped")
        normed = sem("normed")
        turned = sem("turned")
        turned_copied = sem("turned_copied")
        mixed = sem("mixed")
        mixed_copied = sem("mixed_copied")
        s_sel_ready = sem("s_sel_ready")
        s_selT_prod = sem("s_selT_prod")
        s_logits = sem("s_logits")
        s_scaled = sem("s_scaled")
        s_biased = sem("s_biased")
        s_rows = sem("s_rows")
        s_rowmax = sem("s_rowmax")
        s_exped = sem("s_exped")
        s_normed = sem("s_normed")
        s_back = sem("s_back")
        s_back_copied = sem("s_back_copied")
        s_mixed = sem("s_mixed")
        s_mixed_copied = sem("s_mixed_copied")
        merged = sem("merged")
        x1_ready = sem("x1_ready")
        h2_ready = sem("h2_ready")
        pscore = sem("pscore")
        pscore_copied = sem("pscore_copied")
        top_max = sem("top_max")
        top_exp = sem("top_exp")
        picks = sem("picks")
        picks_turned = sem("picks_turned")
        picks_copied = sem("picks_copied")
        hot_ready = sem("hot_ready")
        gate_copied = sem("gate_copied")
        gelued = sem("gelued")
        weighted = sem("weighted")
        y_out = sem("y_out")
        stored = sem("stored")
        dve_step = sem("dve_step")
        pool_step = sem("pool_step")

        def seq(v, n=TD):
            return v.rearrange("p (b t) -> p b t", t=n)

        block = ctx.enter_context(nc.Block())

        @block.sync
        def _(sp):
            def load(n, slot):
                sp.dma_start(ring[:, slot, :], a["stream"][n]).then_inc(tile_loaded[slot], 16)

            for n in range(R):
                load(n, n)
            with sp.Fori(0, (NLIN - R) // R) as g:
                for s in range(R):
                    sp.wait_ge(tile_done, g * R + (s + 1))
                    sp.dma_start(ring[:, s, :], a["stream"][bass.ds(g * R + (R + s), 1)].rearrange("o p n -> (o p) n"))\
                        .then_inc(tile_loaded[s], 16)
            for n in range(NLIN - NLIN % R, NLIN):
                sp.wait_ge(tile_done, n - R + 1)
                load(n, n % R)
            for c in range(R):
                sp.wait_ge(tile_done, NLIN + c - R + 1)
                load(NLIN + c, slot_of(c))

            def load_expert(c, n):
                sp.wait_ge(hi_ready, c + 1)
                sp.wait_ge(lo_ready, c + 1)
                sp.dma_start(ring[:, slot_of(n), :],
                             a["stream"][bass.ds(c + (NLIN + R), 1)].rearrange("o p n -> (o p) n"))\
                    .then_inc(tile_loaded[slot_of(n)], 16)

            with sp.Fori(0, NSUB // R) as g:
                for n in range(R):
                    load_expert(g * R + n, n)
                    sp.wait_ge(gelued, g * R + (n + 1))
                    sp.dma_start(act_dram[bass.ds(g * R + n, 1)].rearrange("o p t -> (o p) t"), act[:, n % 2])\
                        .then_inc(act_stored[n % 2], 16)
            for s in range(2):
                sp.wait_ge(act_stored[s], 16 * NSUB // 2)
            sp.wait_ge(gate_copied, T // 4)
            for n in range(R):
                sp.dma_start(act_b[:, n], act_dram[n]).then_inc(act_loaded[n], 16)
            with sp.Fori(0, NSUB // R - 1) as g:
                for n in range(R):
                    load_expert(g * R + (NSUB + n), n)
                    sp.wait_ge(w_lo, g * R + (n + 1))
                    sp.dma_start(act_b[:, n], act_dram[bass.ds(g * R + (n + R), 1)].rearrange("o p t -> (o p) t"))\
                        .then_inc(act_loaded[n], 16)
            sp.wait_ge(w_lo, NSUB)
            sp.dma_start(xe, x_dram).then_inc(x_loaded, 16)
            sp.wait_ge(y_out, 3 * KC)
            sp.dma_start(a["yT"], ye).then_inc(stored, 16)
            sp.wait_ge(stored, 16 * 5)

        @block.gpsimd
        def _(pool):
            pool.dma_start(pages[0:1, :], a["pages"]).then_inc(pages_in, 16)
            nc.gpsimd.memset(zp[:, :, 0:LEFT], 0.0).then_inc(zeroed, 1)
            nc.gpsimd.memset(ones[:, :], 1.0).then_inc(zeroed, 1)
            nc.gpsimd.memset(eps, EPS).then_inc(zeroed, 1)
            pool.dma_start(v_w, a["v_w"]).then_inc(vw_in, 16)
            for dst, src in ((dist_w, "dist"), (causal_w, "causal")):
                pool.dma_start(dst, a[src]).then_inc(mask_in, 16)
            pool.wait_ge(pages_in, 16)
            for n in range(NSEQ * NPAGES):
                page = pool.value_load(pages[0:1, n:n + 1], min_val=0, max_val=a["cache_k"].shape[0] - 1)
                one = bass.ds(page, 1)
                pool.dma_start(cache_i[0:ID, n], a["cache_i"][one].rearrange("o p n -> (o p) n")).then_inc(cache_in, 16)
                pool.dma_start(cache_i[ID:P, n], a["cache_i"][one].rearrange("o p n -> (o p) n")).then_inc(cache_in, 16)
                pool.dma_start(cache_k[:, n], a["cache_k"][one].rearrange("o p v n -> (o p) v n")).then_inc(cache_in, 16)
                pool.dma_start(cache_v[:, n], a["cache_v"][one].rearrange("o p n -> (o p) n")).then_inc(cache_in, 16)
            pool.wait_ge(conv_in, 64)
            taps = 0
            for k in range(KC):
                pool.wait_ge(z_ready, 2 * k + 2)
                if k:
                    pool.wait_ge(y_sample, k)
                ys = seq(y[:, k, TP:T])
                nc.gpsimd.tensor_scalar(ys, zs[:, k, :, 0:TD], wdw[:, k, 0:1], cvec[:, 0, k:k + 1],
                                        ALU.mult, ALU.add).then_inc(pool_step, 1)
                nc.gpsimd.tensor_scalar(tap[:, 1], zs[:, k, :, 1:1 + TD], wdw[:, k, 1:2], None, ALU.mult)\
                    .then_inc(pool_step, 1)
                taps += 2
                for j in range(1, CW):
                    if j < CW - 1:
                        nc.gpsimd.tensor_scalar(tap[:, (j + 1) % 3], zs[:, k, :, j + 1:j + 1 + TD],
                                                wdw[:, k, j + 1:j + 2], None, ALU.mult).then_inc(pool_step, 1)
                        taps += 1
                    pool.wait_ge(pool_step, taps - (j < CW - 1))
                    ins = nc.gpsimd.tensor_tensor(ys, ys, tap[:, j % 3], ALU.add)
                    if j < CW - 1:
                        taps += 1
                        ins.then_inc(pool_step, 1)
                    else:
                        ins.then_inc(y_sample, 1)
            pool.wait_ge(y_prompt, KC)
            pool.wait_ge(y_sample, KC)
            pool.wait_ge(conv_stored, 32)
            for dst, src in ((alibi_past, "alibi_past"), (alibi_new[0:TS], "alibi_new"), (own[0:TS], "own")):
                pool.dma_start(dst, a[src]).then_inc(attn_in, 16)
            pool.wait_ge(merged, 1)
            pool.wait_ge(stored, 16 * 4)
            for n in range(2):
                pool.dma_start(sk[:, n], a["sub_keys"][n]).then_inc(peer_in, 16)

            def cut_low(c, n, used, value=None):
                pool.wait_ge(hi_ready, c + 1)
                if value is not None:
                    pool.wait_ge(used, value)
                nc.gpsimd.tensor_tensor(split[:, n % 2, 1], ring[:, slot_of(n), :], split[:, n % 2, 0].bitcast(f32),
                                        ALU.subtract).then_inc(lo_ready, 1)

            for n in range(R):
                cut_low(n, n, u_done, n - 1 if n >= 2 else None)
            with pool.Fori(1, NSUB // R) as g:
                for n in range(R):
                    cut_low(g * R + n, n, u_done, g * R + (n - 1))
            for n in range(R):
                cut_low(NSUB + n, n, *((u_done, NSUB + n - 1) if n < 2 else (o_done, n - 1)))
            with pool.Fori(1, NSUB // R) as g:
                for n in range(R):
                    cut_low(g * R + (NSUB + n), n, o_done, g * R + (n - 1))

        @block.scalar
        def _(eng):
            def square_all(src, *ready):
                eng.wait_ge(*ready)
                nc.scalar.activation(xn[:, :, :], src[:, :, :], ACT.Square).then_inc(squares, 1)

            def root(value):
                eng.wait_ge(stats, value)
                nc.scalar.activation(rstd, stb[:, 0:T], ACT.Sqrt, bias=eps, scale=1.0 / D).then_inc(stat_r, 1)

            eng.dma_start(cT, a["cT"]).then_inc(inputs, 16)
            eng.dma_start(x[:, :, :], a["xT"]).then_inc(inputs, 16)
            for dst, src in ((ident[:, :], "ident"), (iota_f, "iota"), (gnorm[:, :, :], "gnorm"), (badaT, "badaT")):
                eng.dma_start(dst, a[src]).then_inc(consts, 16)
            for dst, src in ((zs[:, :, :, 0:LEFT], "stateT"), (wdw, "wdw"), (cvec, "cvec"), (qkg, "qkg")):
                eng.dma_start(dst, a[src]).then_inc(conv_in, 16)
            eng.wait_ge(inputs, 32)
            nc.scalar.activation(cs, cT, ACT.Sigmoid).then_inc(c_sig, 1)
            square_all(x, inputs, 32)
            eng.wait_ge(zeroed, 3)
            root(1)
            with eng.Fori(0, NFIRST // 2) as g:
                for b in range(2):
                    eng.wait_ge(tile_done, g * (2 * R) + (b + 1) * R)
                    nc.scalar.activation(m_row[:, bass.ds(g * (2 * ADA_COLS) + b * ADA_COLS, ADA_COLS)],
                                         lin[b][0:NG, :], ACT.Copy).then_inc(ada_copied, 1)

            def evac(key, dst, func=ACT.Copy):
                eng.wait_ge(tile_done, TILE[key] + 1)
                nc.scalar.activation(dst, lin[BANK[key]][:, 0:T], func).then_inc(act_evac, 1)

            def qk_root_of(n):
                eng.wait_ge(qk_sums, n + 1)
                nc.scalar.activation(sq_qk[n], stb[:, 0:T], ACT.Sqrt, bias=eps, scale=1.0 / P).then_inc(qk_root, 1)

            for key in BANKED[:BANKED.index(("gate_a", 0))]:
                kind, m = key
                if kind == "conv_g":
                    eng.wait_ge(tile_done, TILE[key] + 1)
                    nc.scalar.activation(sig[:, m], lin[BANK[key]][:, 0:T], ACT.Sigmoid).then_inc(sig_ready, 1)
                elif kind == "ki":
                    evac(key, ki)
                elif kind == "qi":
                    evac(key, qi[:, m])
                elif kind == "v":
                    eng.wait_ge(v_done, m + 1)
                    rows = tokens(m)[1]
                    nc.scalar.activation(vtok[0:rows, m], lin[BANK[key]][0:rows, 0:VW], ACT.Copy)\
                        .then_inc(act_evac, 1)
                else:
                    n = QK.index(key)
                    evac(key, kT[:, m] if kind == "k" else q[:, m])
                    evac(key, sq_qk[n], ACT.Square)
                    if n:
                        qk_root_of(n - 1)
            qk_root_of(len(QK) - 1)
            eng.wait_ge(z_ready, 2 * KC)
            eng.dma_start(a["convpT"], zp[:, :, TP:TP + LEFT]).then_inc(conv_stored, 16)
            eng.dma_start(a["convsT"], zs[:, :, :, TD:TD + LEFT]).then_inc(conv_stored, 16)
            for n in range(NQ * IH):
                if n == 6:
                    square_all(y, y_centred, 1)
                if n == 12:
                    root(3)
                if n % 2 == 0:
                    evac(("gate_a", n // 2), ga[:, n // 2], ACT.Sigmoid)
                keys = P * (n // IH + 1)
                eng.wait_ge(idx_prod, n + 1)
                if n >= 2:
                    eng.wait_ge(idx_used, n - 1)
                nc.scalar.activation(relu[:, n % 2, 0:keys], pa[n % 2][:, 0:keys], ACT.Relu, scale=IDX_SCALE)\
                    .then_inc(idx_relu, 1)
            eng.wait_ge(s_idx_prod, 1)
            eng.wait_ge(y_prompt, KC)
            eng.wait_ge(y_sample, KC)
            eng.wait_ge(conv_stored, 32)
            for par in range(2):
                cols = slice(par * 128, par * 128 + 128)
                nc.scalar.activation(s_relu[:, :, cols], pa[par][:, 0:256].rearrange("p (m b) -> p m b", m=NPAGES),
                                     ACT.Relu, scale=IDX_SCALE).then_inc(s_relued, 1)
                nc.scalar.activation(n_relu[0:TS, cols], pa[par][0:TS, 256:384], ACT.Relu, scale=IDX_SCALE)\
                    .then_inc(s_relued, 1)
            eng.wait_ge(qk_ready, 2)
            for n in range(KC):
                evac(("gate_b", n), gb[:, n], ACT.Sigmoid)
                if n == 1:
                    eng.wait_ge(y_scaled, KC)
                    nc.scalar.activation(xn[:, :, :], y[:, :, :], ACT.Sigmoid).then_inc(y_sig, 1)
            for n in range(NQ * H + 2):
                if n < NQ * H:
                    keys = P * (n // H + 1)
                    eng.wait_ge(row_max, n + 1)
                    nc.scalar.activation(lg[:, n % 2, 0:keys], lg[:, n % 2, 0:keys], ACT.Exp, bias=stat[:, n, 0:1],
                                         accum_out=stat[:, n, 1:2]).then_inc(exped, 1)
                if 1 <= n <= NQ * H:
                    m = n - 1
                    keys = P * (m // H + 1)
                    eng.wait_ge(turned, m + 1)
                    if m >= 2:
                        eng.wait_ge(mixed, m - 1)
                    nc.scalar.activation(prT[:, m % 2, 0:keys], pa[2][:, 0:keys], ACT.Copy).then_inc(turned_copied, 1)
                if n >= 2:
                    m = n - 2
                    eng.wait_ge(mixed, m + 1)
                    nc.scalar.activation(attn[:, m % H, tokens(m // H)[0]], pa[3][:, 0:P], ACT.Copy)\
                        .then_inc(mixed_copied, 1)
                if n % 2 == 1 and n < NQ * H:
                    g = n // 2
                    key = ("ada", NFIRST + g)
                    eng.wait_ge(tile_done, TILE[key] + R)
                    if g >= 2:
                        eng.wait_ge(mod_turned, g)
                    nc.scalar.activation(m_row2[:, g % 2], lin[BANK[key]][0:NG, :], ACT.Copy).then_inc(act_evac, 1)
            for g in range(2):
                eng.wait_ge(s_rowmax, g + 1)
                nc.scalar.activation(s_row[:, g], s_row[:, g], ACT.Exp, bias=s_stat[:, g, 0:1],
                                     accum_out=s_stat[:, g, 1:2]).then_inc(s_exped, 1)
            eng.wait_ge(qk_ready, 4)
            eng.dma_start(a["kT"], kT).then_inc(stored, 16)
            eng.dma_start(a["v_prompt"], vtok[:, 0:NQ, 0:KV * P]).then_inc(stored, 16)
            eng.dma_start(a["v_sample"], vtok[0:TS, NQ, 0:KV * P]).then_inc(stored, 16)
            eng.dma_start(a["kiT"], ki[0:ID]).then_inc(stored, 16)
            eng.wait_ge(x1_ready, 3 * KC)
            eng.dma_start(x_dram, x[:, :, :]).then_inc(x_stored, 16)
            square_all(x, x1_ready, 3 * KC)
            root(4)
            eng.wait_ge(h2_ready, KC + 1)
            nc.scalar.activation(h2r[:, 0], h2.rearrange("p k t -> p (k t)"), ACT.Copy).then_inc(h2_hi, 1)
            eng.wait_ge(stored, 16 * 4)
            for n in range(2 * PH):
                evac(("peer_q", n), qh[:, n])
                if n % 4 == 3:
                    for t in range(NT):
                        m = n // 4 * NT + t
                        rows = tokens(t)[1]
                        eng.wait_ge(pscore, m + 1)
                        nc.scalar.activation(sc[0:rows, t, n - 3:n + 1],
                                             pa[m % 4][0:rows, :].rearrange("p (a b) -> p a b", b=NSUB), ACT.Copy)\
                            .then_inc(pscore_copied, 1)

            def cut_high(c, n, loaded, first=False):
                eng.wait_ge(tile_loaded[slot_of(n)], loaded)
                if not first:
                    eng.wait_ge(hi_used, c - 1)
                    eng.wait_ge(lo_ready, c - 1)
                nc.scalar.activation(split[:, n % 2, 0], ring[:, slot_of(n), :], ACT.Copy).then_inc(hi_ready, 1)

            def gelu(c, n, first=False):
                eng.wait_ge(u_done, c + 1)
                if not first:
                    eng.wait_ge(act_stored[n % 2], 16 * (c // 2))
                nc.scalar.activation(act[:, n % 2], ps[n % 2][:, 0:T], ACT.Gelu_apprx_tanh).then_inc(gelued, 1)

            def first_of(n):
                return 16 * (loads_before(n) + 1)

            eng.wait_ge(x_stored, 16)
            cut_high(0, 0, first_of(0), True)
            for c in range(R):
                cut_high(c + 1, (c + 1) % R, first_of((c + 1) % R) + 16 * ((c + 1) // R), c == 0)
                gelu(c, c, c < 2)

            def turn(g, tokens4):
                for n in range(R):
                    m = (n + 1) % R
                    cut_high(g * R + (n + 1), m, g * 16 + (first_of(m) + 16 * ((n + 1) // R)))
                    eng.wait_ge(u_done, g * R + (n + 1))
                    eng.wait_ge(act_stored[n % 2], g * 32 + 16 * (n // 2))
                    nc.scalar.activation(act[:, n % 2], ps[n % 2][:, 0:T], ACT.Gelu_apprx_tanh).then_inc(gelued, 1)
                    if tokens4:
                        eng.wait_ge(hot_used, g * (2 * R) + 2 * (n + 1 - BEFORE))
                        nc.scalar.activation(gate_mat[:, :, bass.ds(g * (4 * R) + 4 * (n - BEFORE), 4)],
                                             ps[2 + n % 2][:, :].rearrange("p (t i) -> p i t", t=4), ACT.Copy)\
                            .then_inc(gate_copied, 1)

            with eng.Fori(1, BEFORE // R) as g:
                turn(g, False)
            for t in range(NT):
                rows = tokens(t)[1]
                eng.wait_ge(top_max, t + 1)
                nc.scalar.activation(tv[0:rows, t], tv[0:rows, t], ACT.Exp).then_inc(top_exp, 1)
            for n in range(3):
                eng.wait_ge(picks_turned, n + 1)
                nc.scalar.activation(parts[:, n], pa[n][:, 0:T], ACT.Copy).then_inc(picks_copied, 1)
            eng.wait_ge(parts_ready, 5)
            with eng.Fori(BEFORE // R, (BEFORE + MIXED) // R) as g:
                turn(g, True)
            with eng.Fori((BEFORE + MIXED) // R, NSUB // R) as g:
                turn(g, False)
            def v_turn(g, first=False, last=False):
                for n in range(R):
                    eng.wait_ge(weighted, g * R + (n + 1))
                    if not first or n >= 2:
                        eng.wait_ge(o_done, g * R + (n - 1))
                    nc.scalar.activation(wr[:, n % 2, 0], act_b[:, n], ACT.Copy).then_inc(w_hi, 1)
                    m = (n + 1) % R
                    if not (last and n == R - 1):
                        cut_high(g * R + (NSUB + n + 1), m, g * 16 + (first_of(m) + 16 * (NSUB // R + (n + 1) // R)))

            eng.wait_ge(u_done, NSUB)
            v_turn(0, first=True)
            with eng.Fori(1, NSUB // R - 1) as g:
                v_turn(g)
            v_turn(NSUB // R - 1, last=True)

        @block.vector
        def _(dve):
            V = nc.vector
            steps = [0]

            def step(ins):
                steps[0] += 1
                ins.then_inc(dve_step, 1)

            def settle(back=0):
                dve.wait_ge(dve_step, steps[0] - back)

            def root(n):
                dve.wait_ge(stat_r, n)
                step(V.reciprocal(rstd, rstd))
                settle()

            def over_chunks(v):
                return v.unsqueeze(1).to_broadcast([P, KC, T])

            def modulate(src, dst, which, ready):
                step(V.tensor_tensor(xn[:, :, :], src[:, :, :], over_chunks(rstd), ALU.mult))
                settle()
                for k in range(KC):
                    V.tensor_scalar(dst[:, k, 0:TP], xn[:, k, 0:TP], scl[:, which, k, 0:1],
                                    mod[:, 3 * which, k, 0:1], ALU.mult, ALU.add).then_inc(ready, 1)

                def wide(v):
                    return v.unsqueeze(3).to_broadcast([P, KC, NSEQ, TD])

                smp = dst[:, :, TP:T].rearrange("p k (b t) -> p k b t", t=TD)
                step(V.tensor_tensor(smp, xn[:, :, TP:T].rearrange("p k (b t) -> p k b t", t=TD),
                                     wide(scl[:, which, :, 1:NG]), ALU.mult))
                settle()
                V.tensor_tensor(smp, smp, wide(mod[:, 3 * which, :, 1:NG]), ALU.add).then_inc(ready, 1)

            dve.wait_ge(c_sig, 1)
            V.tensor_tensor(cs, cs, cT, ALU.mult).then_inc(c_silu, 1)
            root(1)
            dve.wait_ge(consts, 64)
            step(V.tensor_copy(iota[:, :], iota_f))
            dve.wait_ge(mod_turned, 1)

            def modulation(turned_rows, lo, hi, w):
                n = (hi - lo) * KC
                step(V.tensor_tensor(mod[:, lo:hi].rearrange("p a k g -> p (a k) g"),
                                     turned_rows[:, 0:n * NG].rearrange("p (a g) -> p a g", g=NG),
                                     badaT[:, lo * KC:hi * KC].unsqueeze(2).to_broadcast([P, n, NG]), ALU.add))
                settle()
                step(V.tensor_scalar(scl[:, w], mod[:, 3 * w + 1], 1.0, None, ALU.add))
                settle()
                step(V.tensor_tensor(scl[:, w], scl[:, w], gnorm[:, w].unsqueeze(2).to_broadcast([P, KC, NG]),
                                     ALU.mult))
                settle()

            modulation(pa[0], 0, 2, 0)
            modulate(x, hT, 0, h_ready)

            dve.wait_ge(conv_in, 64)
            dve.wait_ge(zeroed, 3)
            for pair in range(KC // 2):
                for k in (2 * pair, 2 * pair + 1):
                    dve.wait_ge(tile_done, TILE["conv_a", k] + 1)
                    dve.wait_ge(sig_ready, k + 1)
                    V.tensor_tensor(zp[:, k, LEFT:], pa[k % 4][:, 0:TP], sig[:, k, 0:TP], ALU.mult)\
                        .then_inc(z_ready, 1)
                    V.tensor_tensor(zs[:, k, :, LEFT:], seq(pa[k % 4][:, TP:T]), seq(sig[:, k, TP:T]), ALU.mult)\
                        .then_inc(z_ready, 1)
                dve.wait_ge(z_ready, 4 * pair + 4)
                for j in range(CW):
                    for k in (2 * pair, 2 * pair + 1):
                        yp, w = y[:, k, 0:TP], wdw[:, k, j:j + 1]
                        if j == 0:
                            ins = V.tensor_scalar(yp, zp[:, k, 0:TP], w, cvec[:, 0, k:k + 1], ALU.mult, ALU.add)
                        else:
                            settle(1 if j < CW - 1 or k % 2 == 0 else 0)
                            ins = V.scalar_tensor_tensor(yp, zp[:, k, j:j + TP], w, yp, ALU.mult, ALU.add)
                        if j < CW - 1:
                            step(ins)
                        else:
                            ins.then_inc(y_prompt, 1)
            dve.wait_ge(qk_root, len(QK))
            step(V.reciprocal(gb[:, 0:KV], gb[:, 0:KV]))
            step(V.reciprocal(attn[:, 0:H], attn[:, 0:H]))
            settle()
            step(V.tensor_tensor(kT, kT, gb[:, 0:KV], ALU.mult))
            step(V.tensor_tensor(q, q, attn[:, 0:H], ALU.mult))
            settle()
            V.tensor_scalar(kT, kT, qkg[:, 1:2], None, ALU.mult).then_inc(qk_ready, 2)
            V.tensor_scalar(q, q, qkg[:, 0:1], None, ALU.mult).then_inc(qk_ready, 2)
            dve.wait_ge(y_prompt, KC)
            dve.wait_ge(y_sample, KC)
            dve.wait_ge(conv_stored, 32)
            wi = vtok[0:TS, NQ, KV * P:VW].rearrange("p (pair par) -> p par pair", par=2)
            for par in range(2):
                V.tensor_tensor(wi_diag[0:TS, par * 4:par * 4 + 4], wi[:, par].unsqueeze(2).to_broadcast([TS, 4, TS]),
                                ident[0:TS, 0:TS].unsqueeze(1).to_broadcast([TS, 4, TS]), ALU.mult).then_inc(s_wi, 1)
            dve.wait_ge(stats, 2)
            step(V.tensor_scalar(rstd, stb[:, 0:T], 1.0 / D, None, ALU.mult))
            settle()
            V.tensor_tensor(y[:, :, :], y[:, :, :], over_chunks(rstd), ALU.subtract).then_inc(y_centred, 1)

            dve.wait_ge(mask_in, 32)
            for n in range(NQ * IH):
                t, h = divmod(n, IH)
                keys = P * (t + 1)
                dve.wait_ge(idx_relu, n + 1)
                w = vtok[:, t, KV * P + h:KV * P + h + 1]
                acc = isc[:, t, 0:keys]
                if h == 0:
                    ins = V.tensor_scalar(acc, relu[:, n % 2, 0:keys], w, None, ALU.mult)
                else:
                    dve.wait_ge(idx_used, n)
                    ins = V.scalar_tensor_tensor(acc, relu[:, n % 2, 0:keys], w, acc, ALU.mult, ALU.add)
                ins.then_inc(idx_used, 1)
            dve.wait_ge(idx_used, NQ * IH)
            for t in range(NQ):
                keys = P * (t + 1)
                step(V.scalar_tensor_tensor(isc[:, t, 0:keys], isc[:, t, 0:keys], HEAD_SCALE, causal[t],
                                            ALU.mult, ALU.add))

            dve.wait_ge(attn_in, 48)
            dve.wait_ge(s_wi_prod, 1)
            step(V.tensor_copy(wi_all, pa[2][:, 0:IH * TS].rearrange("p (a b) -> p a b", b=TS)))
            settle()
            dve.wait_ge(s_relued, 4)
            wi_flat = wi_all.rearrange("p a b -> p (a b)")
            for m in range(NPAGES):
                step(V.tensor_tensor(s_relu[:, m], s_relu[:, m], wi_flat, ALU.mult))
            step(V.tensor_tensor(n_relu[0:TS], n_relu[0:TS], wi_flat[0:TS], ALU.mult))
            settle()
            V.tensor_reduce(s_iscT[:, 0:NPAGES], s_relu.rearrange("p m (a b) -> p m b a", b=TS), AX.X, ALU.add)\
                .then_inc(s_summed, 1)
            V.tensor_reduce(s_iscT[0:TS, NPAGES], n_relu[0:TS].rearrange("p (a b) -> p b a", b=TS), AX.X, ALU.add)\
                .then_inc(s_summed, 1)
            dve.wait_ge(y_centred, 1)
            root(2)
            step(V.tensor_tensor(y[:, :, :], y[:, :, :], over_chunks(rstd), ALU.mult))
            settle()
            for k in range(KC):
                V.tensor_scalar(y[:, k], y[:, k], cvec[:, 1, k:k + 1], cvec[:, 2, k:k + 1], ALU.mult, ALU.add)\
                    .then_inc(y_scaled, 1)
            dve.wait_ge(s_turned, 1)
            keys = PAST + TS
            step(V.scalar_tensor_tensor(s_isc[0:TS], pa[3][0:TS, 0:keys], HEAD_SCALE, own[0:TS], ALU.mult, ALU.add))
            lists = [(isc[:, t, 0:P * (t + 1)], max8[:, t]) for t in range(NQ)] + [(s_isc[0:TS], s_max8[0:TS])]
            for taken in range(0, SAMPLE_TOPK, 8):
                left = SAMPLE_TOPK - taken
                now = lists if taken < PROMPT_TOPK else lists[NQ:]
                for scores, best in now:
                    settle(len(now) - 1)
                    step(V.max(out=best, in_=scores))
                if left < 8:
                    settle()
                    step(V.memset(s_max8[0:TS, left:8], TAKEN))
                for scores, best in now:
                    settle(len(now) - 1)
                    step(V.match_replace(out=scores, in_to_replace=best, in_values=scores, imm_value=TAKEN))
                if taken == 8:
                    dve.wait_ge(y_sig, 1)
                    V.tensor_tensor(y[:, :, :], y[:, :, :], xn[:, :, :], ALU.mult).then_inc(conv_ready, 1)
            settle()
            for t in range(NQ):
                keys = P * (t + 1)
                step(V.tensor_scalar(selb[:, t, 0:keys], isc[:, t, 0:keys], TAKEN, NEG, ALU.not_equal, ALU.mult))
            step(V.tensor_scalar(s_sel[0:TS], s_isc[0:TS], TAKEN, NEG, ALU.not_equal, ALU.mult))
            settle()
            for t in range(NQ):
                keys = P * (t + 1)
                V.tensor_tensor(selb[:, t, 0:keys], selb[:, t, 0:keys], causal[t], ALU.add)\
                    .then_inc(sel_ready, 1)
            V.tensor_tensor(s_sel[0:TS], s_sel[0:TS], own[0:TS], ALU.add).then_inc(s_sel_ready, 1)
            dve.wait_ge(s_logits, 1)
            for m in range(NPAGES):
                step(V.scalar_tensor_tensor(s_lT[:, m], pa[0][:, m * 256:m * 256 + 256], QK_SCALE, alibi_past[:, m],
                                            ALU.mult, ALU.add))
            V.scalar_tensor_tensor(s_lT[0:TS, NPAGES], pa[1][0:TS, 0:256], QK_SCALE, alibi_new[0:TS],
                                   ALU.mult, ALU.add).then_inc(s_scaled, 1)

            for n in range(KC):
                key = ("conv_out", n)
                dve.wait_ge(tile_done, TILE[key] + 1)
                dve.wait_ge(act_evac, ACT_EVAC["gate_b", n])
                V.tensor_tensor(gb[:, n], lin[BANK[key]][:, 0:T], gb[:, n], ALU.mult).then_inc(gated, 1)

            for n in range(NQ * H + 1):
                if n < NQ * H:
                    t, h = divmod(n, H)
                    keys = P * (t + 1)
                    slope = 2.0 ** (-8.0 * (h + 1) / H)
                    if n == 0:
                        dve.wait_ge(sel_ready, NQ)
                    if n >= 2:
                        dve.wait_ge(turned, n - 1)
                    step(V.scalar_tensor_tensor(bias_h[:, n % 2, 0:keys], dist[t], -slope,
                                                selb[:, t, 0:keys], ALU.mult, ALU.add))
                    settle()
                    dve.wait_ge(logits, n + 1)
                    V.scalar_tensor_tensor(lg[:, n % 2, 0:keys], pa[n % 2][:, 0:keys], QK_SCALE,
                                           bias_h[:, n % 2, 0:keys], ALU.mult, ALU.add).then_inc(biased, 1)
                    dve.wait_ge(biased, n + 1)
                    V.tensor_reduce(stat[:, n, 0:1], lg[:, n % 2, 0:keys], AX.X, ALU.max, negate=True)\
                        .then_inc(row_max, 1)
                if n >= 1:
                    m = n - 1
                    keys = P * (m // H + 1)
                    dve.wait_ge(exped, m + 1)
                    step(V.reciprocal(stat[:, m, 2:3], stat[:, m, 1:2]))
                    settle()
                    V.tensor_scalar(lg[:, m % 2, 0:keys], lg[:, m % 2, 0:keys], stat[:, m, 2:3], None, ALU.mult)\
                        .then_inc(normed, 1)

            dve.wait_ge(s_selT_prod, 1)
            step(V.tensor_copy(s_selT[:, 0:NPAGES], pa[2][:, 0:NPAGES * TS].rearrange("p (m b) -> p m b", b=TS)))
            step(V.tensor_copy(s_selT[0:TS, NPAGES], pa[2][0:TS, NPAGES * TS:(NPAGES + 1) * TS]))
            settle()
            for m in range(NPAGES + 1):
                rows = P if m < NPAGES else TS
                v = s_lT[0:rows, m].rearrange("p (b h t) -> p b h t", h=H, t=TD)
                V.tensor_tensor(v, v, seq(s_selT[0:rows, m]).unsqueeze(2).to_broadcast([rows, NSEQ, H, TD]), ALU.add)\
                    .then_inc(s_biased, 1)
            for g in range(2):
                dve.wait_ge(s_rows, g + 1)
                step(V.tensor_copy(s_row[:, g], pa[2 + g][:, 0:PAST + TS]))
                settle()
                V.tensor_reduce(s_stat[:, g, 0:1], s_row[:, g], AX.X, ALU.max, negate=True).then_inc(s_rowmax, 1)
            for g in range(2):
                dve.wait_ge(s_exped, g + 1)
                step(V.reciprocal(s_stat[:, g, 2:3], s_stat[:, g, 1:2]))
                settle()
                V.tensor_scalar(s_row[:, g], s_row[:, g], s_stat[:, g, 2:3], None, ALU.mult).then_inc(s_normed, 1)
            dve.wait_ge(s_back, 1)
            V.tensor_copy(s_prT[:, 0:NPAGES], pa[0][:, :].rearrange("p (m r) -> p m r", m=NPAGES))\
                .then_inc(s_back_copied, 1)
            V.tensor_copy(s_prT[0:TS, NPAGES], pa[1][0:TS, 0:256]).then_inc(s_back_copied, 1)
            dve.wait_ge(s_mixed, 1)
            V.tensor_copy(attn[:, :, TP:T].rearrange("p h (b t) -> p b h t", t=TD),
                          pa[2][:, 0:256].rearrange("p (b h t) -> p b h t", h=H, t=TD)).then_inc(s_mixed_copied, 1)

            for n in range(KC):
                key = ("attn_out", n)
                dve.wait_ge(tile_done, TILE[key] + 1)
                V.tensor_tensor(ga[:, n], lin[BANK[key]][:, 0:T], ga[:, n], ALU.mult).then_inc(gated, 1)
            dve.wait_ge(gated, 2 * KC)
            V.tensor_tensor(ga[:, :, :], ga[:, :, :], gb[:, :, :], ALU.add).then_inc(merged, 1)

            dve.wait_ge(mod_turned, 1 + NGRP - NFIRST)
            modulation(stb, 2, 6, 1)

            def residual(k, src, which, xin, dst, tmp, done):
                V.scalar_tensor_tensor(dst[:, k, 0:TP], src[0], mod[:, which, k, 0:1], xin[:, k, 0:TP],
                                       ALU.mult, ALU.add).then_inc(done, 1)
                V.tensor_tensor(seq(tmp), seq(src[1]), mod[:, which, k, 1:NG].unsqueeze(2).to_broadcast([P, NSEQ, TD]),
                                ALU.mult).then_inc(done, 1)
                dve.wait_ge(done, 3 * k + 2)
                V.tensor_tensor(dst[:, k, TP:T], tmp, xin[:, k, TP:T], ALU.add).then_inc(done, 1)
                dve.wait_ge(done, 3 * k + 3)

            for n in range(KC):
                key = ("out", n)
                dve.wait_ge(tile_done, TILE[key] + 1)
                bank = lin[BANK[key]]
                residual(n, (bank[:, 0:TP], bank[:, TP:T]), 2, x, x, dtmp_early, x1_ready)
            root(3)
            modulate(x, h2, 1, h2_ready)
            dve.wait_ge(h2_hi, 1)
            V.tensor_tensor(h2r[:, 1], h2.rearrange("p k t -> p (k t)"), h2r[:, 0].bitcast(f32), ALU.subtract)\
                .then_inc(h2_lo, 1)

            for grp in range(4):
                dve.wait_ge(pscore_copied, (grp + 1) * NT)
                units = [(t, n) for t in range(NT) for n in range(4 * grp, 4 * grp + 4)]
                nu = len(units)

                def each(fn):
                    for t, n in units:
                        rows = tokens(t)[1]
                        settle(nu - 1)
                        step(fn(rows, t, n))

                each(lambda r, t, n: V.max(out=va[0:r, t, n, 0:8], in_=sc[0:r, t, n]))
                each(lambda r, t, n: V.max_index(out=ix[0:r, t, n, 0:8], in_max=va[0:r, t, n, 0:8],
                                                 in_values=sc[0:r, t, n]))
                each(lambda r, t, n: V.match_replace(out=scw[0:r, t, n], in_to_replace=va[0:r, t, n, 0:8],
                                                     in_values=sc[0:r, t, n], imm_value=TAKEN))
                each(lambda r, t, n: V.max(out=va[0:r, t, n, 8:16], in_=scw[0:r, t, n]))
                each(lambda r, t, n: V.max_index(out=ix[0:r, t, n, 8:16], in_max=va[0:r, t, n, 8:16],
                                                 in_values=scw[0:r, t, n]))
                settle()
                units = [(t, h) for t in range(NT) for h in (2 * grp, 2 * grp + 1)]
                nu = len(units)
                each(lambda r, t, h: V.tensor_tensor(
                    cand[0:r, t, h].rearrange("p (a b) -> p a b", b=PTOP),
                    va[0:r, t, 2 * h].unsqueeze(2).to_broadcast([r, PTOP, PTOP]),
                    va[0:r, t, 2 * h + 1].unsqueeze(1).to_broadcast([r, PTOP, PTOP]), ALU.add))
                each(lambda r, t, h: V.max(out=tv[0:r, t, h, 0:8], in_=cand[0:r, t, h]))
                each(lambda r, t, h: V.max_index(out=tj[0:r, t, h, 0:8], in_max=tv[0:r, t, h, 0:8],
                                                 in_values=cand[0:r, t, h]))
                each(lambda r, t, h: V.match_replace(out=cand[0:r, t, h], in_to_replace=tv[0:r, t, h, 0:8],
                                                     in_values=cand[0:r, t, h], imm_value=TAKEN))
                each(lambda r, t, h: V.max(out=tv[0:r, t, h, 8:16], in_=cand[0:r, t, h]))
                each(lambda r, t, h: V.max_index(out=tj[0:r, t, h, 8:16], in_max=tv[0:r, t, h, 8:16],
                                                 in_values=cand[0:r, t, h]))
                settle()
            for t in range(NT):
                r = tokens(t)[1]
                step(V.tensor_copy(gsum[0:r, t, :, 0], tv[0:r, t, :, 0]))
            settle()
            for t in range(NT):
                r = tokens(t)[1]
                V.tensor_tensor(tv[0:r, t], tv[0:r, t], gsum[0:r, t, :, 0].unsqueeze(2)
                                .to_broadcast([r, PH, PTOP]), ALU.subtract).then_inc(top_max, 1)
            for t in range(NT):
                r = tokens(t)[1]
                flat_j = tj[0:r, t].rearrange("p h k -> p (h k)")
                step(V.tensor_single_scalar(tab_u[0:r, 0, t], flat_j, 4, ALU.logical_shift_right))
                step(V.tensor_single_scalar(tab_u[0:r, 1, t], flat_j, PTOP - 1, ALU.bitwise_and))
                step(V.tensor_copy(ixf[0:r, t], ix[0:r, t]))
            settle()
            for t in range(NT):
                r = tokens(t)[1]
                for w in range(2):
                    step(V.tensor_copy(tab[0:r, w, t], tab_u[0:r, w, t]))
            settle()
            for t in range(NT):
                r = tokens(t)[1]
                for w in range(2):
                    step(V.tensor_tensor(eq[0:r], tab[0:r, w, t].unsqueeze(2).to_broadcast([r, PH * PTOP, PTOP]),
                                         iota[0:r, 0:PTOP].unsqueeze(1).to_broadcast([r, PH * PTOP, PTOP]),
                                         ALU.is_equal))
                    settle()
                    eq4 = eq[0:r].rearrange("p (h k) a -> p h k a", k=PTOP)
                    idx = ixf[0:r, t].rearrange("p (h w) a -> p w h a", w=2)[:, w]
                    step(V.tensor_tensor(eq4, eq4, idx.unsqueeze(2).to_broadcast([r, PH, PTOP, PTOP]), ALU.mult))
                    settle()
                    step(V.tensor_reduce(tsel[0:r, t, w], eq[0:r], AX.X, ALU.add))
                    settle()
            dve.wait_ge(top_exp, NT)
            for t in range(NT):
                r = tokens(t)[1]
                step(V.tensor_reduce(gsum[0:r, t, :, 1], tv[0:r, t], AX.X, ALU.add))
            settle()
            for t in range(NT):
                r = tokens(t)[1]
                step(V.reciprocal(gsum[0:r, t, :, 1], gsum[0:r, t, :, 1]))
            settle()
            for t in range(NT):
                r = tokens(t)[1]
                V.tensor_tensor(tsel[0:r, t, 2].rearrange("p (h k) -> p h k", k=PTOP), tv[0:r, t],
                                gsum[0:r, t, :, 1].unsqueeze(2).to_broadcast([r, PH, PTOP]), ALU.mult)\
                    .then_inc(picks, 1)

            dve.wait_ge(picks_copied, 3)
            for n in range(2):
                V.tensor_copy(picked[:, n], parts[:, n]).then_inc(parts_ready, 1)
            rest = parts[:, 2]
            for n in range(NPARTS):
                V.tensor_copy(picked[:, 2 + n], rest).then_inc(parts_ready, 1)
                if n < NPARTS - 1:
                    dve.wait_ge(parts_ready, 3 + n)
                    step(V.tensor_tensor(parts[:, 3 + n], rest, picked[:, 2 + n], ALU.subtract))
                    settle()
                    rest = parts[:, 3 + n]
            dve.wait_ge(parts_ready, 5)

            def one_hot(token, slot):
                col = bass.ds(token, 1)
                V.tensor_scalar(hot2[:, slot], iota[:, :], picked[:, 1, col], None, ALU.is_equal)
                for n in range(NPARTS):
                    last = V.tensor_scalar(hot1[:, slot, n], iota[:, :], picked[:, 0, col], picked[:, 2 + n, col],
                                           ALU.is_equal, ALU.mult)
                return last

            def token_pairs(g, first=False):
                for pair in range(2):
                    if not first:
                        dve.wait_ge(hot_used, g * 2 + (pair - 1))
                    for j in range(2):
                        last = one_hot(g * 4 + (2 * pair + j), 2 * pair + j)
                    last.then_inc(hot_ready, 1)

            token_pairs(0, True)
            with dve.Fori(1, MIXED) as g:
                token_pairs(g)

            dve.wait_ge(gate_copied, MIXED)
            dve.wait_ge(u_done, NSUB)

            def weights(g, behind):
                for n in range(R):
                    dve.wait_ge(act_loaded[n], g * 16 + 16)
                    V.tensor_tensor(act_b[:, n], act_b[:, n],
                                    gate_mat[:, bass.ds(g * R + n, 1)].rearrange("p o t -> p (o t)"), ALU.mult)\
                        .then_inc(weighted, 1)
                    if n or behind:
                        low(g * R + (n - 1), (n - 1) % R)

            def low(c, n):
                dve.wait_ge(w_hi, c + 1)
                V.tensor_tensor(wr[:, n % 2, 1], act_b[:, n], wr[:, n % 2, 0].bitcast(f32), ALU.subtract)\
                    .then_inc(w_lo, 1)

            weights(0, False)
            with dve.Fori(1, NSUB // R) as g:
                weights(g, True)
            low(NSUB - 1, R - 1)
            dve.wait_ge(o_done, NSUB)
            dve.wait_ge(x_loaded, 16)
            for k in range(KC):
                residual(k, (ps[k][:, 0:TP], ps[k][:, TP:T]), 5, xe, ye, dtmp, y_out)

        @block.tensor
        def _(pe):
            MM = nc.tensor.matmul

            def sums(src, out, n):
                for k in range(n):
                    last = MM(out[:, 0:T], ones[:, :], src[:, k], start=(k == 0), stop=(k == n - 1))
                return last

            def linear(key, rhs):
                if key[0] == "conv_a":
                    bank = pa[key[1] % 4]
                    if key[1] >= 4:
                        pe.wait_ge(z_ready, 2 * (key[1] - 4) + 2)
                else:
                    bank = lin[BANK[key]]
                    free(BANKED.index(key))
                pe.wait_ge(tile_loaded[TILE[key] % R], 16 * (TILE[key] // R + 1))
                w = ring[:, TILE[key] % R, :].rearrange("p (k m) -> p k m", m=P)
                for k in range(KC):
                    last = MM(bank[:, 0:T], w[:, k], rhs[:, k], start=(k == 0), stop=(k == KC - 1))
                last.then_inc(tile_done, 1)

            def free(n):
                if n < NBANK:
                    return
                kind, m = key = BANKED[n - NBANK]
                if kind == "conv_g":
                    pe.wait_ge(sig_ready, m + 1)
                elif kind in ("conv_out", "attn_out"):
                    pe.wait_ge(gated, m + 1 + (KC if kind == "attn_out" else 0))
                elif kind == "out":
                    pe.wait_ge(x1_ready, 3 * m + 2)
                else:
                    pe.wait_ge(act_evac, ACT_EVAC[key])

            pe.wait_ge(zeroed, 3)
            pe.wait_ge(squares, 1)
            sums(xn, stb, KC).then_inc(stats, 1)
            pe.wait_ge(c_silu, 1)

            def ada_columns(g):
                for b in range(2):
                    for s in range(R):
                        pe.wait_ge(tile_loaded[s], g * 32 + 16 * (b + 1))
                        w = ring[:, s, :].rearrange("p (k m) -> p k m", m=ADA_COLS)
                        for j in range(2):
                            k = 2 * s + j
                            last = MM(lin[b][0:NG, :], cs[:, k], w[:, j], start=(k == 0), stop=(k == KC - 1))
                        last.then_inc(tile_done, 1)

            ada_columns(0)
            with pe.Fori(1, NFIRST // 2) as g:
                pe.wait_ge(ada_copied, g * 2)
                ada_columns(g)
            pe.wait_ge(ada_copied, NFIRST)
            pe.wait_ge(consts, 64)
            for n in range(2 * KC):
                last = nc.tensor.transpose(pa[0][:, n * NG:(n + 1) * NG], m_row[:, n * P:(n + 1) * P],
                                           ident[0:NG, 0:NG])
            last.then_inc(mod_turned, 1)

            pe.wait_ge(h_ready, KC + 1)
            pe.wait_ge(vw_in, 16)

            def qk_sum(n):
                pe.wait_ge(act_evac, ACT_EVAC[QK[n]])
                if n:
                    pe.wait_ge(qk_root, n)
                MM(stb[:, 0:T], ones[:, :], sq_qk[n], start=True, stop=True).then_inc(qk_sums, 1)

            for key in LINEAR[:LINEAR.index(("gate_a", 0))]:
                if key == ("k", 0):
                    for t in range(NT):
                        n = BANKED.index(("v", t))
                        free(n)
                        cols, rows = tokens(t)
                        for k in range(KC):
                            last = MM(lin[n % NBANK][0:rows, 0:VW], hT[:, k, cols], v_w[:, k], start=(k == 0),
                                      stop=(k == KC - 1))
                        last.then_inc(v_done, 1)
                linear(key, hT)
                if key in QK[1:]:
                    qk_sum(QK.index(key) - 1)
            pe.wait_ge(z_ready, 2 * KC)
            for n in range(NQ * IH):
                if n % 2 == 0:
                    linear(("gate_a", n // 2), hT)
                if n == 0:
                    qk_sum(len(QK) - 1)
                if n == 2:
                    pe.wait_ge(y_prompt, KC)
                    pe.wait_ge(y_sample, KC)
                    pe.wait_ge(qk_root, len(QK))
                    sums(y, stb, KC).then_inc(stats, 1)
                if n == 10:
                    pe.wait_ge(squares, 2)
                    sums(xn, stb, KC).then_inc(stats, 1)
                t, h = divmod(n, IH)
                half = slice(ID * (h % 2), ID * (h % 2) + ID)
                if n >= 2:
                    pe.wait_ge(idx_relu, n - 1)
                MM(pa[n % 2][:, 0:P * (t + 1)], qi[half, h // 2, tokens(t)[0]], ki[half, 0:P * (t + 1)],
                   start=True, stop=True).then_inc(idx_prod, 1)
            pe.wait_ge(idx_relu, NQ * IH)
            pe.wait_ge(cache_in, 16 * 4 * NSEQ * NPAGES)
            for m in range(NPAGES):
                for par in range(2):
                    half = slice(ID * par, ID * par + ID)
                    for b in range(NSEQ):
                        out = pa[par][:, m * 128:m * 128 + 128]\
                            .rearrange("p (pair s) -> p pair s", s=TS)[:, :, b * TD:b * TD + TD]
                        MM(out, cache_i[half, b * NPAGES + m], qi[half, :, TP + b * TD:TP + b * TD + TD],
                           start=True, stop=True)
            for par in range(2):
                half = slice(ID * par, ID * par + ID)
                last = MM(pa[par][0:TS, 256:384].rearrange("p (a b) -> p a b", b=TS),
                          ki[half, TP:T], qi[half, :, TP:T], start=True, stop=True)
            last.then_inc(s_idx_prod, 1)
            pe.wait_ge(s_wi, 2)
            MM(pa[2][:, 0:IH * TS], ones[0:TS, :], wi_diag[0:TS].rearrange("p a b -> p (a b)"), start=True, stop=True)\
                .then_inc(s_wi_prod, 1)
            for n in range(KC):
                linear(("gate_b", n), hT)
                if n == 1:
                    pe.wait_ge(s_summed, 2)
                    for m in range(NPAGES):
                        nc.tensor.transpose(pa[3][0:TS, m * P:(m + 1) * P], s_iscT[:, m], ident[:, :])
                    nc.tensor.transpose(pa[3][0:TS, PAST:PAST + TS], s_iscT[0:TS, NPAGES], ident[0:TS, 0:TS])\
                        .then_inc(s_turned, 1)
            pe.wait_ge(qk_ready, 4)
            pe.wait_ge(s_relued, 4)
            for m in range(NPAGES):
                for b in range(NSEQ):
                    for kv in range(KV):
                        at = m * 256 + b * H * TD + kv * HG * TD
                        MM(pa[0][:, at:at + HG * TD].rearrange("p (h t) -> p h t", t=TD),
                           cache_k[:, b * NPAGES + m, kv],
                           q[:, kv * HG:(kv + 1) * HG, TP + b * TD:TP + b * TD + TD], start=True, stop=True)
            for kv in range(KV):
                out = pa[1][0:TS, 0:256].rearrange("p (b h t) -> p h b t", h=H, t=TD)[:, kv * HG:(kv + 1) * HG]
                last = MM(out, kT[:, kv, TP:T],
                          q[:, kv * HG:(kv + 1) * HG, TP:T].rearrange("p h (b t) -> p h b t", t=TD),
                          start=True, stop=True)
            last.then_inc(s_logits, 1)
            pe.wait_ge(conv_ready, 1)
            for n in range(KC):
                linear(("conv_out", n), y)
            def ada_half(g, part):
                key = ("ada", NFIRST + g)
                if part == 0:
                    free(BANKED.index(key))
                for s in (2 * part, 2 * part + 1):
                    n = TILE[key] + s
                    pe.wait_ge(tile_loaded[n % R], 16 * (n // R + 1))
                    w = ring[:, n % R, :].rearrange("p (k m) -> p k m", m=ADA_COLS)
                    for j in range(2):
                        k = 2 * s + j
                        last = MM(lin[BANK[key]][0:NG, :], cs[:, k], w[:, j], start=(k == 0), stop=(k == KC - 1))
                    last.then_inc(tile_done, 1)

            def ada_turn(g):
                pe.wait_ge(act_evac, ACT_EVAC["ada", NFIRST + g])
                for j in range(CG):
                    at = (g * CG + j) * NG
                    last = nc.tensor.transpose(stb[:, at:at + NG], m_row2[:, g % 2, j * P:(j + 1) * P],
                                               ident[0:NG, 0:NG])
                last.then_inc(mod_turned, 1)

            pe.wait_ge(s_scaled, 1)
            for n in range(NQ * H + 2):
                if n < NQ * H:
                    t, h = divmod(n, H)
                    if n >= 2:
                        pe.wait_ge(biased, n - 1)
                    MM(pa[n % 2][:, 0:P * (t + 1)], q[:, h, tokens(t)[0]], kT[:, h // HG, 0:P * (t + 1)],
                       start=True, stop=True).then_inc(logits, 1)
                    ada_half(n // 2, n % 2)
                if 1 <= n <= NQ * H:
                    m = n - 1
                    pe.wait_ge(normed, m + 1)
                    if m >= 1:
                        pe.wait_ge(turned_copied, m)
                    for blk in range(m // H + 1):
                        last = nc.tensor.transpose(pa[2][:, blk * P:(blk + 1) * P],
                                                   lg[:, m % 2, blk * P:(blk + 1) * P], ident[:, :])
                    last.then_inc(turned, 1)
                if n >= 2:
                    m = n - 2
                    t, h = divmod(m, H)
                    pe.wait_ge(turned_copied, m + 1)
                    if m >= 1:
                        pe.wait_ge(mixed_copied, m)
                    kv = h // HG
                    for blk in range(t + 1):
                        last = MM(pa[3][:, 0:P], vtok[:, blk, kv * P:(kv + 1) * P], prT[:, m % 2, blk * P:(blk + 1) * P],
                                  start=(blk == 0), stop=(blk == t))
                    last.then_inc(mixed, 1)
                    if n % 2 == 0:
                        ada_turn(n // 2 - 1)
            pe.wait_ge(turned_copied, NQ * H)
            for m in range(NPAGES):
                nc.tensor.transpose(pa[2][:, m * TS:(m + 1) * TS], s_sel[0:TS, m * P:(m + 1) * P], ident[0:TS, 0:TS])
            nc.tensor.transpose(pa[2][0:TS, NPAGES * TS:(NPAGES + 1) * TS], s_sel[0:TS, PAST:PAST + TS],
                                ident[0:TS, 0:TS]).then_inc(s_selT_prod, 1)
            pe.wait_ge(s_biased, NPAGES + 1)
            pe.wait_ge(mixed_copied, NQ * H)
            for g in range(2):
                for m in range(NPAGES):
                    nc.tensor.transpose(pa[2 + g][:, m * P:(m + 1) * P], s_lT[:, m, g * P:(g + 1) * P], ident[:, :])
                nc.tensor.transpose(pa[2 + g][:, PAST:PAST + TS], s_lT[0:TS, NPAGES, g * P:(g + 1) * P],
                                    ident[0:TS, 0:TS]).then_inc(s_rows, 1)
            pe.wait_ge(s_normed, 2)
            for g in range(2):
                for m in range(NPAGES):
                    nc.tensor.transpose(pa[0][:, m * 256 + g * P:m * 256 + (g + 1) * P],
                                        s_row[:, g, m * P:(m + 1) * P], ident[:, :])
                last = nc.tensor.transpose(pa[1][0:TS, g * P:(g + 1) * P], s_row[:, g, PAST:PAST + TS], ident[:, :])
            last.then_inc(s_back, 1)
            pe.wait_ge(s_back_copied, 2)
            for b in range(NSEQ):
                for kv in range(KV):
                    at = b * H * TD + kv * HG * TD
                    cols = slice(kv * P, (kv + 1) * P)
                    for m in range(NPAGES):
                        MM(pa[2][:, at:at + HG * TD], cache_v[:, b * NPAGES + m, cols], s_prT[:, m, at:at + HG * TD],
                           start=(m == 0), stop=False)
                    last = MM(pa[2][:, at:at + HG * TD], vtok[0:TS, NQ, cols], s_prT[0:TS, NPAGES, at:at + HG * TD],
                              start=False, stop=True)
            last.then_inc(s_mixed, 1)
            pe.wait_ge(s_mixed_copied, 1)
            for n in range(KC):
                linear(("attn_out", n), attn)
            pe.wait_ge(merged, 1)
            for n in range(KC):
                linear(("out", n), ga)
            pe.wait_ge(squares, 3)
            sums(xn, stb, KC).then_inc(stats, 1)
            pe.wait_ge(h2_ready, KC + 1)
            pe.wait_ge(peer_in, 32)
            for n in range(2 * PH):
                linear(("peer_q", n), h2)
                if n % 4 == 3:
                    pe.wait_ge(act_evac, ACT_EVAC["peer_q", n])
                    for t in range(NT):
                        m = n // 4 * NT + t
                        cols, rows = tokens(t)
                        if m >= 4:
                            pe.wait_ge(pscore_copied, m - 3)
                        for j in range(4):
                            last = MM(pa[m % 4][0:rows, j * P:(j + 1) * P], qh[:, n - 3 + j, cols], sk[:, j % 2],
                                      start=True, stop=True)
                        last.then_inc(pscore, 1)
            pe.wait_ge(pscore_copied, 4 * NT)
            pe.wait_ge(h2_lo, 1)
            h_hi, h_lo = (h2r[:, part].rearrange("p (k t) -> p k t", t=T) for part in range(2))

            def scores(c, n, first=False):
                pe.wait_ge(hi_ready, c + 1)
                if not first:
                    pe.wait_ge(gelued, c - 1)
                u_hi, u_lo = (split[:, n % 2, part].rearrange("p (k m) -> p k m", m=P) for part in range(2))
                out = ps[n % 2][:, 0:T]
                for k in range(KC):
                    MM(out, u_hi[:, k], h_hi[:, k], start=(k == 0), stop=False)
                    last = MM(out, u_hi[:, k], h_lo[:, k], start=False, stop=False)
                last.then_inc(hi_used, 1)
                pe.wait_ge(lo_ready, c + 1)
                for k in range(KC):
                    last = MM(out, u_lo[:, k], h_hi[:, k], start=False, stop=(k == KC - 1))
                last.then_inc(u_done, 1)

            for c in range(R):
                scores(c, c, c < 2)
            with pe.Fori(1, BEFORE // R) as g:
                for n in range(R):
                    scores(g * R + n, n)
            pe.wait_ge(picks, NT)
            for n in range(3):
                for t in range(NT):
                    cols, rows = tokens(t)
                    last = nc.tensor.transpose(pa[n][:, cols], tsel[0:rows, t, n], ident[0:rows, 0:rows])
                last.then_inc(picks_turned, 1)

            def gate_tokens(q, n, first=False):
                if not first:
                    pe.wait_ge(gate_copied, q - 1)
                for pair in range(2):
                    pe.wait_ge(hot_ready, q * 2 + (pair + 1))
                    for j in range(2):
                        s = 2 * pair + j
                        for part in range(NPARTS):
                            last = MM(ps[2 + n % 2][:, s * P:(s + 1) * P], hot2[:, s], hot1[:, s, part],
                                      start=(part == 0), stop=(part == NPARTS - 1))
                    last.then_inc(hot_used, 1)

            for n in range(R):
                scores(BEFORE + n, n)
                gate_tokens(n, n, n < 2)
            with pe.Fori(1, MIXED // R) as g:
                for n in range(R):
                    scores(g * R + (BEFORE + n), n)
                    gate_tokens(g * R + n, n)
            with pe.Fori((BEFORE + MIXED) // R, NSUB // R) as g:
                for n in range(R):
                    scores(g * R + n, n)

            def outputs(c, n, first=False, last=False):
                v = [split[:, n % 2, part].rearrange("p (k m) -> p k m", m=P) for part in range(2)]

                def product(v_part, w_part, start=False, stop=False):
                    for k in range(KC):
                        ins = MM(ps[k][:, 0:T], v[v_part][:, k], wr[:, n % 2, w_part], start=start, stop=stop)
                    return ins

                pe.wait_ge(hi_ready, c + (NSUB + 1))
                pe.wait_ge(w_hi, c + 1)
                product(0, 0, start=first)
                pe.wait_ge(w_lo, c + 1)
                product(0, 1).then_inc(hi_used, 1)
                pe.wait_ge(lo_ready, c + (NSUB + 1))
                product(1, 0, stop=last).then_inc(o_done, 1)

            pe.wait_ge(gelued, NSUB)
            pe.wait_ge(gate_copied, MIXED)
            for n in range(R):
                outputs(n, n, first=n == 0)
            with pe.Fori(1, NSUB // R - 1) as g:
                for n in range(R):
                    outputs(g * R + n, n)
            for n in range(R):
                outputs(NSUB - R + n, n, last=n == R - 1)


def constants():
    p, s = np.arange(P), np.arange(TP)
    pos = (np.arange(NQ)[None, :] * P + p[:, None])[:, :, None]
    dist = (pos - s).astype(np.float32)[:, NQ - 1]
    slope = 2.0 ** (-8.0 * np.arange(1, H + 1) / H)
    t4 = np.arange(TD)
    key = np.arange(NPAGES)[None, :] * P + p[:, None]
    past = -slope[:, None] * (PAST + t4 - key[:, :, None, None])
    past = np.broadcast_to(past[:, :, None], (P, NPAGES, NSEQ, H, TD))
    ts = np.arange(TS)
    new = -slope[:, None] * (t4 - (ts % TD)[:, None, None])
    new = np.broadcast_to(new[:, None], (TS, NSEQ, H, TD))
    own = np.zeros((TS, PAST + TS))
    same = (ts[:, None] // TD == ts // TD) & (ts <= ts[:, None])
    own[:, PAST:] = np.where(same, 0.0, NEG)
    made = {
        "ident": np.eye(P), "iota": np.broadcast_to(p, (P, P)), "dist": dist,
        "causal": np.where(dist >= 0, 0.0, NEG), "alibi_past": past.reshape(P, NPAGES, -1),
        "alibi_new": new.reshape(TS, -1), "own": own,
    }
    return {n: np.ascontiguousarray(v, dtype=np.float32) for n, v in made.items()}


def layouts(v):
    def chunks(m):
        return m.reshape(-1, m.shape[-1] // P, P).transpose(2, 1, 0)

    def cut(w):
        return w.reshape(KC, P, -1, P).transpose(2, 1, 0, 3).reshape(-1, P, D)

    w_in = v["w_in"]
    edges = np.cumsum([H * P, KV * P, KV * P, IH * ID, ID, IH, 2 * D, 2 * D])
    w_q, w_k, w_v, w_qi, w_ki, w_wi, w_conv, w_gate = (
        w_in[:, lo:hi] for lo, hi in zip([0, *edges[:-1]], edges))
    tiles = {"conv_a": cut(w_conv[:, :D]), "conv_g": cut(w_conv[:, D:]), "ki": cut(np.concatenate([w_ki, w_ki], 1)),
             "qi": cut(w_qi), "k": cut(w_k), "q": cut(w_q), "gate_a": cut(w_gate[:, :D]), "gate_b": cut(w_gate[:, D:]),
             "conv_out": cut(v["w_conv_out"]), "attn_out": cut(v["w_o_attn"]), "out": cut(v["w_out"]),
             "peer_q": cut(v["w_q_peer"])}
    stream = np.empty((NTILES, P, D), np.float32)
    ada = v["w_ada"].reshape(R, 2, P, NGRP, ADA_COLS).transpose(3, 0, 2, 1, 4).reshape(NGRP, R, P, D)
    stream[:NFIRST * R] = ada[:NFIRST].reshape(-1, P, D)
    for key, n in TILE.items():
        if key[0] == "ada":
            stream[n:n + R] = ada[key[1]]
        else:
            stream[n] = tiles[key[0]][key[1]]
    stream[NLIN:NLIN + NSUB] = v["u_emb"].reshape(NSUB, P, KC, P).transpose(0, 3, 2, 1).reshape(NSUB, P, D)
    stream[NLIN + NSUB:] = v["v_emb"].reshape(NSUB, P, D)
    xs = np.concatenate([v["x_prompt"].reshape(TP, D), v["x_sample"].reshape(TS, D)])
    cond = np.concatenate([v["c_prompt"], v["c_sample"]])
    vw = np.concatenate([w_v, w_wi], 1)
    pool = v["cache_k"].shape[0]
    made = {
        "stream": stream, "xT": chunks(xs), "cT": chunks(cond), "badaT": v["b_ada"].reshape(-1, P).T,
        "gnorm": chunks(np.stack([v["g_norm1"], v["g_norm2"]])).transpose(0, 2, 1),
        "v_w": vw.reshape(KC, P, VW).transpose(1, 0, 2),
        "stateT": v["state_conv"].reshape(NSEQ, LEFT, KC, P).transpose(3, 2, 0, 1),
        "wdw": v["w_dw"].reshape(CW, KC, P).transpose(2, 1, 0),
        "cvec": chunks(np.stack([v["b_dw"], v["ln_g"], v["ln_b"]])).transpose(0, 2, 1),
        "qkg": np.stack([v["g_q"], v["g_k"]], 1),
        "cache_k": v["cache_k"].transpose(0, 3, 2, 1), "cache_v": v["cache_v"].reshape(pool, PAGE, KV * P),
        "cache_i": v["cache_idx_k"].transpose(0, 2, 1), "pages": v["page_table"].reshape(1, -1),
        "sub_keys": np.stack([v["sub_keys1"].T, v["sub_keys2"].T]),
    }
    return {n: np.ascontiguousarray(m) for n, m in made.items()} | constants()


OUTS = {"yT": (P, KC, T), "kT": (P, KV, T), "v_prompt": (P, NQ, KV * P), "v_sample": (TS, KV * P), "kiT": (ID, T),
        "convpT": (P, KC, LEFT), "convsT": (P, KC, NSEQ, LEFT)}


def kernel(**inputs):
    import concourse.bacc as bacc
    from concourse.bass_utils import run_bass_kernel_spmd

    arrays = layouts({n: np.asarray(v) for n, v in inputs.items()})
    nc = bacc.Bacc("TRN2", target_bir_lowering=False, num_devices=1)
    aps = {}
    for name, m in arrays.items():
        aps[name] = nc.dram_tensor(f"in_{name}", m.shape, mybir.dt.from_np(m.dtype), kind="ExternalInput").ap()
    for name, shape in OUTS.items():
        aps[name] = nc.dram_tensor(f"out_{name}", shape, mybir.dt.float32, kind="ExternalOutput").ap()
    build(nc, aps)
    got = run_bass_kernel_spmd(nc, [{f"in_{n}": m for n, m in arrays.items()}], core_ids=[0]).results[0]
    out = {n: got[f"out_{n}"] for n in OUTS}
    y = out["yT"].transpose(2, 1, 0).reshape(T, D)
    k = out["kT"].transpose(2, 1, 0)
    ki = out["kiT"].T
    return (y[:TP].reshape(1, TP, D), y[TP:].reshape(NSEQ, TD, D),
            k[:TP].reshape(1, TP, KV, P), out["v_prompt"].transpose(1, 0, 2).reshape(1, TP, KV, P),
            ki[:TP].reshape(1, TP, ID), out["convpT"].transpose(2, 1, 0).reshape(1, LEFT, D),
            k[TP:].reshape(NSEQ, TD, KV, P), out["v_sample"].reshape(NSEQ, TD, KV, P),
            ki[TP:].reshape(NSEQ, TD, ID), out["convsT"].transpose(2, 3, 1, 0).reshape(NSEQ, LEFT, D))
```

```python
from contextlib import ExitStack

import numpy as np

import concourse.bass as bass
from concourse import mybir

P = 128
D = 1024
KC = D // P
TP, NSEQ, TD = 256, 8, 4
TS = NSEQ * TD
T = TP + TS
NQ = TP // P
NT = NQ + 1
NG = 1 + NSEQ
H, KV = 8, 2
HG = H // KV
IH, ID = 8, 64
CW = 31
LEFT = CW - 1
PAGE, NPAGES = 128, 2
PAST = PAGE * NPAGES
PROMPT_TOPK = TP // 4
SAMPLE_TOPK = (PAST + TD) // 4
NSUB, PH, PTOP = 128, 8, 16
EPS = 1e-6
NEG = -1e30
TAKEN = -3e38
R = 4
ADA_COLS = 512
NGRP = 6 * D // ADA_COLS
NFIRST = 2 * D // ADA_COLS
CG = ADA_COLS // P
QK_SCALE = P ** -0.5
IDX_SCALE = ID ** -0.5
HEAD_SCALE = IH ** -0.5
VW = KV * P + IH

CONV = [(kind, k) for k in range(KC) for kind in ("conv_a", "conv_g")]
LINEAR = (CONV[:12] + [("ki", 0)] + [("qi", n) for n in range(4)] + CONV[12:]
          + [("k", n) for n in range(KV)] + [("q", n) for n in range(H)]
          + [("gate_a", n) for n in range(KC)] + [("gate_b", n) for n in range(KC)]
          + [("conv_out", n) for n in range(KC)] + [("ada", g) for g in range(NFIRST, NGRP)]
          + [("attn_out", n) for n in range(KC)]
          + [("out", n) for n in range(KC)] + [("peer_q", n) for n in range(2 * PH)])
TILE, NLIN = {}, NFIRST * R
for key in LINEAR:
    TILE[key] = NLIN
    NLIN += R if key[0] == "ada" else 1
NTILES = NLIN + 2 * NSUB
MIXED = T // 4
BEFORE = 36
SOFTMAX = 20
TURN = BEFORE - R
AFTER = NSUB - MIXED - BEFORE
assert BEFORE % R == 0 and MIXED % R == 0 and AFTER % R == 0 and NSUB % R == 0


def slot_of(c):
    return (NLIN + c) % R


def loads_before(c):
    return (NLIN + c) // R


BANKED = []
for key in LINEAR:
    if key[0] == "conv_a":
        continue
    if key == ("k", 0):
        BANKED += [("v", t) for t in range(NT)]
    BANKED.append(key)
NBANK = 3
BANK = {key: n % NBANK for n, key in enumerate(BANKED)}
ACT_EVAC, n_evac = {}, 0
for key in BANKED:
    if key[0] in ("ki", "qi", "v", "gate_a", "gate_b", "ada", "peer_q"):
        n_evac += 1
        ACT_EVAC[key] = n_evac
    if key[0] in ("k", "q"):
        n_evac += 2
        ACT_EVAC[key] = n_evac
STAGES = [("gate_a", "gate_b"), ("conv_out",), ("attn_out",), ("out",), ("peer_q",)]
CUT = [key for key in LINEAR if any(key[0] in kinds for kinds in STAGES)]
QK = [("k", n) for n in range(KV)] + [("q", n) for n in range(H)]


def tokens(t):
    return (slice(t * P, t * P + P), P) if t < NQ else (slice(TP, T), TS)


def build(nc, a):
    f32, f32r, bf16 = mybir.dt.float32, mybir.dt.float32r, mybir.dt.bfloat16
    i32, u32 = mybir.dt.int32, mybir.dt.uint32
    ALU, ACT, AX = mybir.AluOpType, mybir.ActivationFunctionType, mybir.AxisListType

    with ExitStack() as ctx:
        def sb(name, *shape, dt=f32):
            return ctx.enter_context(nc.sbuf_tensor(name, [P] + list(shape), dt))

        def sem(name):
            return ctx.enter_context(nc.semaphore(name))

        x = sb("x", KC, T)
        mod = sb("mod", 6, KC, NG)
        scl = sb("scl", 2, KC, NG)
        ident = sb("ident", P)
        ones = sb("ones", P)
        iota = sb("iota", P, dt=bf16)
        gnorm = sb("gnorm", 2, KC)
        ring = sb("ring", R, D)
        split = sb("split", 2, 2, D, dt=f32r)
        rhs_parts = sb("h2r", 2, KC * T, dt=f32r)
        pages = sb("pages", NSEQ * NPAGES, dt=i32)
        NBIG = NSUB * T
        big = sb("big", NBIG)
        gate_mat = big[:, :].rearrange("p (i t) -> p i t", t=T)

        class Region:

            def __init__(self, tensor, size):
                self.tensor, self.size, self.at = tensor, size, 0

            def take(self, *shape, dt=None):
                n = int(np.prod(shape))
                v = self.tensor[:, self.at:self.at + n]
                self.at += n
                assert self.at <= self.size, (self.at, self.size)
                if dt is not None:
                    v = v.bitcast(dt)
                names = "abcd"[:len(shape)]
                if len(shape) > 1:
                    v = v.rearrange(f"p ({' '.join(names)}) -> p {' '.join(names)}",
                                    **{c: s for c, s in zip(names[1:], shape[1:])})
                return v

        early = Region(big, NBIG)
        hT = early.take(KC, T)
        cT = hT[:, 0, 0:KC * NG].rearrange("p (k g) -> p k g", g=NG)
        iota_f = hT[:, 3, 0:P]
        xn = early.take(KC, T)
        q = early.take(H, T)
        kT = early.take(KV, T)
        qi = early.take(4, T)
        ki = early.take(T)
        vtok = early.take(NT, VW)
        z_at = early.at
        zp = early.take(KC, LEFT + TP)
        zs = early.take(KC, NSEQ, LEFT + TD)
        m_at = early.at
        y = early.take(KC, T)
        ga = early.take(KC, T)
        gb = early.take(KC, T)
        attn = early.take(KC, T)
        m_row = big[0:NG, m_at:m_at + NFIRST * ADA_COLS]
        m_row2 = big[0:NG, 0:2 * ADA_COLS].rearrange("p (s c) -> p s c", s=2)
        v_w = attn[:, :, 0:VW]
        cache_k = early.take(NSEQ * NPAGES, KV, PAGE)
        cache_v = early.take(NSEQ * NPAGES, KV * P)
        i_at = early.at
        cache_i = early.take(NSEQ * NPAGES, PAGE)
        wdw = early.take(KC, CW)
        cvec = early.take(3, KC)
        qkg = early.take(2)
        dist_w = early.take(TP)
        causal_w = early.take(TP)
        dist = [dist_w[:, TP - P * (t + 1):] for t in range(NQ)]
        causal = [causal_w[:, TP - P * (t + 1):] for t in range(NQ)]
        sq_qk = [gb[:, n] for n in range(KV)] + [attn[:, n] for n in range(H)]
        rz = Region(big, m_at)
        rz.at = z_at
        alibi_past = rz.take(NPAGES, NSEQ * H * TD)
        alibi_new = rz.take(NSEQ * H * TD)
        own = rz.take(PAST + TS)
        s_relu = rz.take(NPAGES, IH * TS)
        n_relu = rz.take(IH * TS)
        wi_all = rz.take(IH, TS)
        wi_diag = rz.take(IH, TS)
        s_iscT = rz.take(NPAGES + 1, TS)
        s_isc = rz.take(PAST + TS)
        s_sel = rz.take(PAST + TS)
        s_max8 = rz.take(8)
        r1 = Region(big, 2 * KC * T)
        r1.at = KC * T
        s_selT = r1.take(NPAGES + 1, TS)
        s_lT = r1.take(NPAGES + 1, NSEQ * H * TD)
        s_row = r1.take(2, PAST + TS)
        s_prT = s_lT
        s_stat = r1.take(2, 4)
        s_out = r1.take(2, KV * P)

        rstd = early.take(T)
        relu = early.take(2, TP)
        eps = early.take(1)
        cs = early.take(KC, NG)
        badaT = early.take(6 * KC)
        tap = early.take(3, 2, NSEQ, TD)
        isc = early.take(NQ, TP)
        selb = early.take(NQ, TP)
        max8 = early.take(NQ, 8)
        stat = early.take(NQ * H, 3)
        sig = xn
        ri = Region(big, i_at + NSEQ * NPAGES * PAGE)
        ri.at = i_at
        bias_h = ri.take(2, TP)
        lg = ri.take(2, TP)
        prT = ri.take(2, TP)
        dtmp_early = ri.take(TS)

        late = Region(big, NBIG)
        h2 = late.take(KC, T)
        assert late.at == KC * T
        late.take(KC * T)
        qh = late.take(2 * PH, T)
        sk = late.take(2, NSUB)
        sc = late.take(NT, 2 * PH, NSUB)
        scw = late.take(NT, 2 * PH, NSUB)
        va = late.take(NT, 2 * PH, PTOP)
        ix = late.take(NT, 2 * PH, PTOP, dt=u32)
        ixf = late.take(NT, 2 * PH, PTOP)
        cand = sc.rearrange("p t (h c) k -> p t h (c k)", c=2)
        tv = late.take(NT, PH, PTOP)
        tj = late.take(NT, PH, PTOP, dt=u32)
        tab_u = late.take(2, NT, PH * PTOP, dt=u32)
        tab = late.take(2, NT, PH * PTOP)
        tsel = late.take(NT, 3, PH * PTOP)
        gsum = late.take(NT, PH, 2)
        eq = late.take(PH * PTOP, PTOP)
        parts = late.take(2 + 3, T)

        late_x = x[:, :, :].rearrange("p k t -> p (k t)")
        picked = late_x[:, 0:5 * T // 2].bitcast(bf16).rearrange("p (a t) -> p a t", t=T)
        NPARTS = 3
        NHOT = 4
        at = 5 * T // 2
        hot2 = sb("hot2", NHOT, P, dt=bf16)
        hot1 = late_x[:, at:at + NHOT * NPARTS * P // 2].bitcast(bf16)\
            .rearrange("p (s a i) -> p s a i", a=NPARTS, i=P)
        at += NHOT * NPARTS * P // 2
        act = late_x[:, at:at + 2 * T].rearrange("p (s t) -> p s t", t=T)
        assert at + 2 * T <= KC * T
        act_b = late_x[:, 0:R * T].rearrange("p (s t) -> p s t", t=T)
        wr = rhs_parts[:, :, :].rearrange("p a n -> p (a n)")[:, 0:4 * T].rearrange("p (s a t) -> p s a t", a=2, t=T)
        end = Region(big, NBIG)
        xe = end.take(KC, T)
        ye = end.take(KC, T)
        dtmp = end.take(TS)
        act_dram = nc.dram_tensor("act_dram", [NSUB, P, T], f32, kind="Internal").ap()
        x_dram = nc.dram_tensor("x_dram", [P, KC, T], f32, kind="Internal").ap()

        ps = [ctx.enter_context(nc.psum_tensor(f"ps{b}", [P, 512], f32)) for b in range(8)]
        lin, stb, pa = ps[0:NBANK], ps[3], ps[4:8]

        tile_loaded = [sem(f"tile_loaded{s}") for s in range(R)]
        tile_done = sem("tile_done")
        v_done = sem("v_done")
        u_done = sem("u_done")
        bank_done = sem("bank_done")
        o_done = sem("o_done")
        hi_ready = sem("hi_ready")
        lo_ready = sem("lo_ready")
        hi_used = sem("hi_used")
        act_stored = [sem(f"act_stored{s}") for s in range(2)]
        act_loaded = [sem(f"act_loaded{s}") for s in range(R)]
        x_stored = sem("x_stored")
        x_loaded = sem("x_loaded")
        rhs_hi = sem("rhs_hi")
        rhs_lo = sem("rhs_lo")
        lin_hi = sem("lin_hi")
        lin_hi_used = sem("lin_hi_used")
        lin_lo = sem("lin_lo")
        hot_used = sem("hot_used")
        w_hi = sem("w_hi")
        w_lo = sem("w_lo")
        parts_ready = sem("parts_ready")
        conv_stored = sem("conv_stored")
        mask_in = sem("mask_in")
        inputs = sem("inputs")
        consts = sem("consts")
        conv_in = sem("conv_in")
        vw_in = sem("vw_in")
        pages_in = sem("pages_in")
        cache_in = sem("cache_in")
        attn_in = sem("attn_in")
        peer_in = sem("peer_in")
        zeroed = sem("zeroed")
        squares2 = sem("squares2")
        squares = sem("squares")
        stats = sem("stats")
        stat_r = sem("stat_r")
        c_sig = sem("c_sig")
        c_silu = sem("c_silu")
        ada_copied = sem("ada_copied")
        mod_turned = sem("mod_turned")
        h_ready = sem("h_ready")
        sig_ready = sem("sig_ready")
        z_ready = sem("z_ready")
        act_evac = sem("act_evac")
        qk_sums = sem("qk_sums")
        qk_root = sem("qk_root")
        qk_ready = sem("qk_ready")
        idx_prod = sem("idx_prod")
        idx_relu = sem("idx_relu")
        idx_used = sem("idx_used")
        y_prompt = sem("y_prompt")
        y_sample = sem("y_sample")
        y_centred = sem("y_centred")
        y_sig = sem("y_sig")
        y_scaled = sem("y_scaled")
        conv_ready = sem("conv_ready")
        gated = sem("gated")
        s_idx_prod = sem("s_idx_prod")
        s_wi = sem("s_wi")
        s_wi_prod = sem("s_wi_prod")
        s_relued = sem("s_relued")
        s_summed = sem("s_summed")
        s_turned = sem("s_turned")
        sel_ready = sem("sel_ready")
        logits = sem("logits")
        biased = sem("biased")
        row_max = sem("row_max")
        exped = sem("exped")
        normed = sem("normed")
        turned = sem("turned")
        turned_copied = sem("turned_copied")
        mixed = sem("mixed")
        mixed_copied = sem("mixed_copied")
        s_sel_ready = sem("s_sel_ready")
        s_selT_prod = sem("s_selT_prod")
        s_logits = sem("s_logits")
        s_scaled = sem("s_scaled")
        s_biased = sem("s_biased")
        s_rows = sem("s_rows")
        s_rowmax = sem("s_rowmax")
        s_exped = sem("s_exped")
        s_normed = sem("s_normed")
        s_back = sem("s_back")
        s_back_copied = sem("s_back_copied")
        s_mixed = sem("s_mixed")
        s_out_copied = sem("s_out_copied")
        s_out_turned = sem("s_out_turned")
        s_mixed_copied = sem("s_mixed_copied")
        merged = sem("merged")
        x1_ready = sem("x1_ready")
        h2_ready = sem("h2_ready")
        pscore = sem("pscore")
        pscore_copied = sem("pscore_copied")
        top_max = sem("top_max")
        top_exp = sem("top_exp")
        picks = sem("picks")
        picks_turned = sem("picks_turned")
        picks_copied = sem("picks_copied")
        hot_ready = sem("hot_ready")
        gate_copied = sem("gate_copied")
        gelued = sem("gelued")
        weighted = sem("weighted")
        y_out = sem("y_out")
        stored = sem("stored")
        dve_step = sem("dve_step")
        pool_step = sem("pool_step")

        def seq(v, n=TD):
            return v.rearrange("p (b t) -> p b t", t=n)

        block = ctx.enter_context(nc.Block())

        @block.sync
        def _(sp):
            def load(n, slot):
                sp.dma_start(ring[:, slot, :], a["stream"][n]).then_inc(tile_loaded[slot], 16)

            for n in range(R):
                load(n, n)
            def turn(g):
                for s in range(R):
                    sp.wait_ge(tile_done, g * R + (s + 1))
                    sp.dma_start(ring[:, s, :], a["stream"][bass.ds(g * R + (R + s), 1)].rearrange("o p n -> (o p) n"))\
                        .then_inc(tile_loaded[s], 16)

            with sp.Fori(0, (NLIN - R) // R) as g:
                turn(g)
            for n in range(NLIN - NLIN % R, NLIN):
                sp.wait_ge(tile_done, n - R + 1)
                load(n, n % R)
            for c in range(R):
                sp.wait_ge(tile_done, NLIN + c - R + 1)
                load(NLIN + c, slot_of(c))

            def load_expert(c, n):
                sp.wait_ge(hi_ready, c + 1)
                sp.wait_ge(lo_ready, c + 1)
                sp.dma_start(ring[:, slot_of(n), :],
                             a["stream"][bass.ds(c + (NLIN + R), 1)].rearrange("o p n -> (o p) n"))\
                    .then_inc(tile_loaded[slot_of(n)], 16)

            def u_turn(g):
                for n in range(R):
                    load_expert(g * R + n, n)
                    sp.wait_ge(gelued, g * R + (n + 1))
                    sp.dma_start(act_dram[bass.ds(g * R + n, 1)].rearrange("o p t -> (o p) t"), act[:, n % 2])\
                        .then_inc(act_stored[n % 2], 16)

            with sp.Fori(0, NSUB // R - 2) as g:
                u_turn(g)
            sp.wait_ge(gate_copied, MIXED)
            for s in range(2):
                sp.wait_ge(act_stored[s], 16 * (NSUB // 2 - R))
            for n in range(R):
                sp.dma_start(act_b[:, n], act_dram[n]).then_inc(act_loaded[n], 16)
            with sp.Fori(NSUB // R - 2, NSUB // R) as g:
                u_turn(g)
            for s in range(2):
                sp.wait_ge(act_stored[s], 16 * NSUB // 2)
            with sp.Fori(0, NSUB // R - 1) as g:
                for n in range(R):
                    load_expert(g * R + (NSUB + n), n)
                    sp.wait_ge(w_lo, g * R + (n + 1))
                    sp.dma_start(act_b[:, n], act_dram[bass.ds(g * R + (n + R), 1)].rearrange("o p t -> (o p) t"))\
                        .then_inc(act_loaded[n], 16)
            sp.wait_ge(w_lo, NSUB)
            sp.dma_start(xe, x_dram).then_inc(x_loaded, 16)
            for half in range(2):
                ks = slice(half * KC // 2, (half + 1) * KC // 2)
                sp.wait_ge(y_out, 3 * ks.stop)
                sp.dma_start(a["yT"][:, ks], ye[:, ks]).then_inc(stored, 16)
            sp.wait_ge(stored, 16 * 6)

        @block.gpsimd
        def _(pool):
            pool.dma_start(pages[0:1, :], a["pages"]).then_inc(pages_in, 16)
            nc.gpsimd.memset(zp[:, :, 0:LEFT], 0.0).then_inc(zeroed, 1)
            nc.gpsimd.memset(ones[:, :], 1.0).then_inc(zeroed, 1)
            nc.gpsimd.memset(eps, EPS).then_inc(zeroed, 1)
            pool.wait_ge(mod_turned, 1)
            pool.dma_start(v_w, a["v_w"]).then_inc(vw_in, 16)
            for dst, src in ((dist_w, "dist"), (causal_w, "causal")):
                pool.dma_start(dst, a[src]).then_inc(mask_in, 16)
            pool.wait_ge(conv_in, 64)
            taps = 0
            for pair in range(KC // 2):
                ks = slice(2 * pair, 2 * pair + 2)

                def wide(v):
                    return v.unsqueeze(2).unsqueeze(3).to_broadcast([P, 2, NSEQ, TD])

                pool.wait_ge(z_ready, 4 * pair + 4)
                if pair == KC // 2 - 1:
                    pool.dma_start(a["convpT"], zp[:, :, TP:TP + LEFT]).then_inc(conv_stored, 16)
                    pool.dma_start(a["convsT"], zs[:, :, :, TD:TD + LEFT]).then_inc(conv_stored, 16)
                ys = y[:, ks, TP:T].rearrange("p k (b t) -> p k b t", t=TD)
                if pair:
                    pool.wait_ge(y_sample, pair)
                nc.gpsimd.tensor_tensor(ys, zs[:, ks, :, 0:TD], wide(wdw[:, ks, 0]), ALU.mult).then_inc(pool_step, 1)
                nc.gpsimd.tensor_tensor(tap[:, 1], zs[:, ks, :, 1:1 + TD], wide(wdw[:, ks, 1]), ALU.mult)\
                    .then_inc(pool_step, 1)
                taps += 2
                for j in range(1, CW):
                    if j < CW - 1:
                        nc.gpsimd.tensor_tensor(tap[:, (j + 1) % 3], zs[:, ks, :, j + 1:j + 1 + TD],
                                                wide(wdw[:, ks, j + 1]), ALU.mult).then_inc(pool_step, 1)
                        taps += 1
                    pool.wait_ge(pool_step, taps - (j < CW - 1))
                    nc.gpsimd.tensor_tensor(ys, ys, tap[:, j % 3], ALU.add).then_inc(pool_step, 1)
                    taps += 1
                pool.wait_ge(pool_step, taps)
                nc.gpsimd.tensor_tensor(ys, ys, wide(cvec[:, 0, ks]), ALU.add).then_inc(y_sample, 1)
            pool.wait_ge(rhs_hi, KC)
            nc.gpsimd.tensor_tensor(rhs_parts[:, 1], hT[:, :, :].rearrange("p k t -> p (k t)"),
                                    rhs_parts[:, 0].bitcast(f32), ALU.subtract).then_inc(rhs_lo, KC)
            pool.wait_ge(y_prompt, KC)
            pool.wait_ge(y_sample, KC // 2)
            pool.wait_ge(conv_stored, 32)

            def low_tiles(kinds):
                for n, key in enumerate(CUT):
                    if key[0] in kinds:
                        pool.wait_ge(lin_hi, n + 1)
                        if n >= 2:
                            pool.wait_ge(tile_done, TILE[CUT[n - 2]] + 1)
                        nc.gpsimd.tensor_tensor(split[:, n % 2, 1], ring[:, TILE[key] % R, :],
                                                split[:, n % 2, 0].bitcast(f32), ALU.subtract).then_inc(lin_lo, 1)

            low_tiles(("gate_a",))
            for dst, src in ((alibi_past, "alibi_past"), (alibi_new[0:TS], "alibi_new"), (own[0:TS], "own")):
                pool.dma_start(dst, a[src]).then_inc(attn_in, 16)
            low_tiles(("gate_b",))
            for k in range(KC):
                pool.wait_ge(rhs_hi, KC + k + 1)
                nc.gpsimd.tensor_tensor(rhs_parts[:, 1, k * T:(k + 1) * T], y[:, k],
                                        rhs_parts[:, 0, k * T:(k + 1) * T].bitcast(f32), ALU.subtract)\
                    .then_inc(rhs_lo, 1)
            for kind in ("conv_out", "attn_out", "out"):
                low_tiles((kind,))
            pool.wait_ge(merged, KC)
            pool.wait_ge(stored, 16 * 4)
            for n in range(2):
                pool.dma_start(sk[:, n], a["sub_keys"][n]).then_inc(peer_in, 16)

            low_tiles(("peer_q",))
            pool.wait_ge(tile_done, NLIN)

            def cut_low(c, n, used, value=None):
                pool.wait_ge(hi_ready, c + 1)
                if value is not None:
                    pool.wait_ge(used, value)
                nc.gpsimd.tensor_tensor(split[:, n % 2, 1], ring[:, slot_of(n), :], split[:, n % 2, 0].bitcast(f32),
                                        ALU.subtract).then_inc(lo_ready, 1)

            for n in range(R):
                cut_low(n, n, u_done, n - 1 if n >= 2 else None)
            with pool.Fori(1, NSUB // R) as g:
                for n in range(R):
                    cut_low(g * R + n, n, u_done, g * R + (n - 1))
            for n in range(R):
                cut_low(NSUB + n, n, *((u_done, NSUB + n - 1) if n < 2 else (o_done, n - 1)))
            with pool.Fori(1, NSUB // R) as g:
                for n in range(R):
                    cut_low(g * R + (NSUB + n), n, o_done, g * R + (n - 1))

        @block.scalar
        def _(eng):
            def square_all(src, *ready):
                eng.wait_ge(*ready)
                nc.scalar.activation(xn[:, :, :], src[:, :, :], ACT.Square).then_inc(squares, 1)

            def root(value):
                eng.wait_ge(stats, value)
                nc.scalar.activation(rstd, stb[:, 0:T], ACT.Sqrt, bias=eps, scale=1.0 / D).then_inc(stat_r, 1)

            eng.dma_start(cT, a["cT"]).then_inc(inputs, 16)
            eng.dma_start(x[:, :, :], a["xT"]).then_inc(inputs, 16)
            for dst, src in ((ident[:, :], "ident"), (iota_f, "iota"), (gnorm[:, :, :], "gnorm"), (badaT, "badaT")):
                eng.dma_start(dst, a[src]).then_inc(consts, 16)
            for dst, src in ((zs[:, :, :, 0:LEFT], "stateT"), (wdw, "wdw"), (cvec, "cvec"), (qkg, "qkg")):
                eng.dma_start(dst, a[src]).then_inc(conv_in, 16)
            eng.wait_ge(inputs, 32)
            nc.scalar.activation(cs, cT, ACT.Sigmoid).then_inc(c_sig, 1)
            square_all(x, inputs, 32)
            eng.wait_ge(zeroed, 3)
            root(1)
            with eng.Fori(0, NFIRST // 2) as g:
                for b in range(2):
                    eng.wait_ge(tile_done, g * (2 * R) + (b + 1) * R)
                    nc.scalar.activation(m_row[:, bass.ds(g * (2 * ADA_COLS) + b * ADA_COLS, ADA_COLS)],
                                         lin[b][0:NG, :], ACT.Copy).then_inc(ada_copied, 1)

            def evac(key, dst, func=ACT.Copy):
                eng.wait_ge(tile_done, TILE[key] + 1)
                nc.scalar.activation(dst, lin[BANK[key]][:, 0:T], func).then_inc(act_evac, 1)

            def cut_tile(key):
                n, at = CUT.index(key), TILE[key]
                eng.wait_ge(tile_loaded[at % R], 16 * (at // R + 1))
                if n >= 2:
                    eng.wait_ge(lin_hi_used, n - 1)
                    eng.wait_ge(lin_lo, n - 1)
                nc.scalar.activation(split[:, n % 2, 0], ring[:, at % R, :], ACT.Copy).then_inc(lin_hi, 1)

            def cut_rhs(src, ready, each):
                for k in range(KC):
                    if k == 0 or each:
                        eng.wait_ge(ready, max(1, each * (k + 1)))
                    nc.scalar.activation(rhs_parts[:, 0, k * T:(k + 1) * T], src[:, k], ACT.Copy).then_inc(rhs_hi, 1)

            cut_rhs(hT, h_ready, 3)

            def load_page(n):
                page = eng.value_load(pages[0:1, n:n + 1], min_val=0, max_val=a["cache_k"].shape[0] - 1)
                for dst, src in ((cache_i[0:ID, n], "cache_i"), (cache_i[ID:P, n], "cache_i"),
                                 (cache_k[:, n].rearrange("p v n -> p (v n)"), "cache_k"), (cache_v[:, n], "cache_v")):
                    eng.dma_start(dst, a[src][bass.ds(page, 1)].rearrange("o p n -> (o p) n")).then_inc(cache_in, 16)

            def qk_root_of(n):
                eng.wait_ge(qk_sums, n + 1)
                nc.scalar.activation(sq_qk[n], stb[:, 0:T], ACT.Sqrt, bias=eps, scale=1.0 / P).then_inc(qk_root, 1)

            for key in BANKED[:BANKED.index(("gate_a", 0))]:
                kind, m = key
                if kind == "conv_g":
                    eng.wait_ge(tile_done, TILE[key] + 1)
                    nc.scalar.activation(sig[:, m], lin[BANK[key]][:, 0:T], ACT.Sigmoid).then_inc(sig_ready, 1)
                    eng.wait_ge(pages_in, 16)
                    for n in (2 * m, 2 * m + 1):
                        load_page(n)
                elif kind == "ki":
                    evac(key, ki)
                elif kind == "qi":
                    evac(key, qi[:, m])
                elif kind == "v":
                    eng.wait_ge(v_done, m + 1)
                    rows = tokens(m)[1]
                    nc.scalar.activation(vtok[0:rows, m], lin[BANK[key]][0:rows, 0:VW], ACT.Copy)\
                        .then_inc(act_evac, 1)
                else:
                    n = QK.index(key)
                    if n == len(QK) - 1:
                        cut_tile(("gate_a", 0))
                    evac(key, kT[:, m] if kind == "k" else q[:, m])
                    evac(key, sq_qk[n], ACT.Square)
                    if n:
                        qk_root_of(n - 1)
            cut_tile(("gate_a", 1))
            qk_root_of(len(QK) - 1)
            for n in range(NQ * IH):
                if n == 6:
                    square_all(y, y_centred, 1)
                if n == 12:
                    root(3)
                if n % 2 == 0:
                    if n:
                        cut_tile(CUT[n // 2 + 1])
                    evac(("gate_a", n // 2), ga[:, n // 2], ACT.Sigmoid)
                keys = P * (n // IH + 1)
                eng.wait_ge(idx_prod, n + 1)
                if n >= 2:
                    eng.wait_ge(idx_used, n - 1)
                nc.scalar.activation(relu[:, n % 2, 0:keys], pa[n % 2][:, 0:keys], ACT.Relu, scale=IDX_SCALE)\
                    .then_inc(idx_relu, 1)
            eng.wait_ge(s_idx_prod, 1)
            eng.wait_ge(y_prompt, KC)
            eng.wait_ge(y_sample, KC // 2)
            eng.wait_ge(conv_stored, 32)
            for par in range(2):
                cols = slice(par * 128, par * 128 + 128)
                nc.scalar.activation(s_relu[:, :, cols], pa[par][:, 0:256].rearrange("p (m b) -> p m b", m=NPAGES),
                                     ACT.Relu, scale=IDX_SCALE).then_inc(s_relued, 1)
                nc.scalar.activation(n_relu[0:TS, cols], pa[par][0:TS, 256:384], ACT.Relu, scale=IDX_SCALE)\
                    .then_inc(s_relued, 1)
            eng.wait_ge(qk_ready, KV)
            for n in range(KC):
                cut_tile(CUT[KC + n + 1])
                evac(("gate_b", n), gb[:, n], ACT.Sigmoid)
                if n == 1:
                    eng.wait_ge(y_scaled, KC)
                    nc.scalar.activation(xn[:, :, :], y[:, :, :], ACT.Sigmoid).then_inc(y_sig, 1)
            eng.wait_ge(tile_done, TILE["gate_b", KC - 1] + 1)
            cut_rhs(y, conv_ready, 0)
            for n in range(1, KC):
                cut_tile(("conv_out", n))
            for n in range(NQ * H + 2):
                if n < NQ * H:
                    keys = P * (n // H + 1)
                    eng.wait_ge(row_max, n + 1)
                    nc.scalar.activation(lg[:, n % 2, 0:keys], lg[:, n % 2, 0:keys], ACT.Exp, bias=stat[:, n, 0:1],
                                         accum_out=stat[:, n, 1:2]).then_inc(exped, 1)
                if 1 <= n <= NQ * H:
                    m = n - 1
                    keys = P * (m // H + 1)
                    eng.wait_ge(turned, m + 1)
                    if m >= 2:
                        eng.wait_ge(mixed, m - 1)
                    nc.scalar.activation(prT[:, m % 2, 0:keys], pa[2][:, 0:keys], ACT.Copy).then_inc(turned_copied, 1)
                if n >= 2:
                    m = n - 2
                    eng.wait_ge(mixed, m + 1)
                    nc.scalar.activation(attn[:, m % H, tokens(m // H)[0]], pa[3][:, 0:P], ACT.Copy)\
                        .then_inc(mixed_copied, 1)
                if n % 2 == 1 and n < NQ * H:
                    g = n // 2
                    key = ("ada", NFIRST + g)
                    eng.wait_ge(tile_done, TILE[key] + R)
                    if g >= 2:
                        eng.wait_ge(mod_turned, g)
                    nc.scalar.activation(m_row2[:, g % 2], lin[BANK[key]][0:NG, :], ACT.Copy).then_inc(act_evac, 1)
            for g in range(2):
                eng.wait_ge(s_rowmax, g + 1)
                nc.scalar.activation(s_row[:, g], s_row[:, g], ACT.Exp, bias=s_stat[:, g, 0:1],
                                     accum_out=s_stat[:, g, 1:2]).then_inc(s_exped, 1)
            eng.wait_ge(qk_ready, len(QK))
            eng.dma_start(a["kT"], kT).then_inc(stored, 16)
            eng.dma_start(a["v_prompt"], vtok[:, 0:NQ, 0:KV * P]).then_inc(stored, 16)
            eng.dma_start(a["v_sample"], vtok[0:TS, NQ, 0:KV * P]).then_inc(stored, 16)
            eng.dma_start(a["kiT"], ki[0:ID]).then_inc(stored, 16)
            for n in range(2):
                cut_tile(("attn_out", n))
            eng.wait_ge(tile_done, TILE["conv_out", KC - 1] + 1)
            eng.wait_ge(s_mixed_copied, 4)
            cut_rhs(attn, s_mixed_copied, 0)
            for n in range(2, KC):
                cut_tile(("attn_out", n))
            for n in range(2):
                cut_tile(("out", n))
            eng.wait_ge(tile_done, TILE["attn_out", KC - 1] + 1)
            cut_rhs(ga, merged, 1)
            for k in range(KC):
                if k + 2 < KC:
                    cut_tile(("out", k + 2))
                eng.wait_ge(x1_ready, 3 * k + 3)
                nc.scalar.activation(xn[:, k], x[:, k], ACT.Square).then_inc(squares2, 1)
            eng.wait_ge(x1_ready, 3 * KC)
            eng.dma_start(x_dram, x[:, :, :]).then_inc(x_stored, 16)
            root(4)
            cut_tile(("peer_q", 0))
            eng.wait_ge(tile_done, TILE["out", KC - 1] + 1)
            cut_rhs(h2, h2_ready, 3)
            eng.wait_ge(stored, 16 * 4)
            for n in range(2 * PH):
                if n + 1 < 2 * PH:
                    cut_tile(("peer_q", n + 1))
                evac(("peer_q", n), qh[:, n])
                if n % 4 == 3:
                    for t in range(NT):
                        m = n // 4 * NT + t
                        rows = tokens(t)[1]
                        eng.wait_ge(pscore, m + 1)
                        nc.scalar.activation(sc[0:rows, t, n - 3:n + 1],
                                             pa[m % 4][0:rows, :].rearrange("p (a b) -> p a b", b=NSUB), ACT.Copy)\
                            .then_inc(pscore_copied, 1)

            def cut_high(c, n, loaded, first=False):
                eng.wait_ge(tile_loaded[slot_of(n)], loaded)
                if not first:
                    eng.wait_ge(hi_used, c - 1)
                    eng.wait_ge(lo_ready, c - 1)
                nc.scalar.activation(split[:, n % 2, 0], ring[:, slot_of(n), :], ACT.Copy).then_inc(hi_ready, 1)

            def gelu(c, n, first=False):
                eng.wait_ge(u_done, c + 1)
                if not first:
                    eng.wait_ge(act_stored[n % 2], 16 * (c // 2))
                nc.scalar.activation(act[:, n % 2], ps[n % 2][:, 0:T], ACT.Gelu_apprx_tanh).then_inc(gelued, 1)

            def first_of(n):
                return 16 * (loads_before(n) + 1)

            eng.wait_ge(x_stored, 16)
            eng.wait_ge(tile_done, NLIN)
            cut_high(0, 0, first_of(0), True)
            for c in range(R):
                cut_high(c + 1, (c + 1) % R, first_of((c + 1) % R) + 16 * ((c + 1) // R), c == 0)
                gelu(c, c, c < 2)

            def turn(g, tokens4):
                for n in range(R):
                    m = (n + 1) % R
                    cut_high(g * R + (n + 1), m, g * 16 + (first_of(m) + 16 * ((n + 1) // R)))
                    eng.wait_ge(u_done, g * R + (n + 1))
                    eng.wait_ge(act_stored[n % 2], g * 32 + 16 * (n // 2))
                    nc.scalar.activation(act[:, n % 2], ps[n % 2][:, 0:T], ACT.Gelu_apprx_tanh).then_inc(gelued, 1)
                    if tokens4:
                        eng.wait_ge(hot_used, g * (2 * R) + 2 * (n + 1 - BEFORE))
                        nc.scalar.activation(gate_mat[:, :, bass.ds(g * (4 * R) + 4 * (n - BEFORE), 4)],
                                             ps[2 + n % 2][:, :].rearrange("p (t i) -> p i t", t=4), ACT.Copy)\
                            .then_inc(gate_copied, 1)

            with eng.Fori(1, SOFTMAX // R) as g:
                turn(g, False)
            for t in range(NT):
                rows = tokens(t)[1]
                eng.wait_ge(top_max, t + 1)
                nc.scalar.activation(tv[0:rows, t], tv[0:rows, t], ACT.Exp).then_inc(top_exp, 1)
            with eng.Fori(SOFTMAX // R, TURN // R) as g:
                turn(g, False)
            for n in range(3):
                eng.wait_ge(picks_turned, n + 1)
                nc.scalar.activation(parts[:, n], pa[n][:, 0:T], ACT.Copy).then_inc(picks_copied, 1)
            turn(TURN // R, False)
            eng.wait_ge(parts_ready, 5)
            with eng.Fori(BEFORE // R, (BEFORE + MIXED) // R) as g:
                turn(g, True)
            with eng.Fori((BEFORE + MIXED) // R, NSUB // R) as g:
                turn(g, False)
            def v_turn(g, first=False, last=False):
                for n in range(R):
                    eng.wait_ge(weighted, g * R + (n + 1))
                    if not first or n >= 2:
                        eng.wait_ge(o_done, g * R + (n - 1))
                    nc.scalar.activation(wr[:, n % 2, 0], act_b[:, n], ACT.Copy).then_inc(w_hi, 1)
                    m = (n + 1) % R
                    if not (last and n == R - 1):
                        cut_high(g * R + (NSUB + n + 1), m, g * 16 + (first_of(m) + 16 * (NSUB // R + (n + 1) // R)))

            eng.wait_ge(u_done, NSUB)
            v_turn(0, first=True)
            with eng.Fori(1, NSUB // R - 1) as g:
                v_turn(g)
            v_turn(NSUB // R - 1, last=True)

        @block.vector
        def _(dve):
            V = nc.vector
            steps = [0]

            def step(ins):
                steps[0] += 1
                ins.then_inc(dve_step, 1)

            def settle(back=0):
                dve.wait_ge(dve_step, steps[0] - back)

            def root(n):
                dve.wait_ge(stat_r, n)
                step(V.reciprocal(rstd, rstd))
                settle()

            def over_chunks(v):
                return v.unsqueeze(1).to_broadcast([P, KC, T])

            def wide(v):
                return v.unsqueeze(2).to_broadcast([P, NSEQ, TD])

            def modulate(src, dst, which, ready):
                for k in range(KC):
                    step(V.tensor_tensor(xn[:, k], src[:, k], rstd, ALU.mult))
                    smp = seq(dst[:, k, TP:T])
                    settle()
                    V.tensor_tensor(smp, seq(xn[:, k, TP:T]), wide(scl[:, which, k, 1:NG]), ALU.mult)\
                        .then_inc(ready, 1)
                    V.tensor_scalar(dst[:, k, 0:TP], xn[:, k, 0:TP], scl[:, which, k, 0:1],
                                    mod[:, 3 * which, k, 0:1], ALU.mult, ALU.add).then_inc(ready, 1)
                    dve.wait_ge(ready, 3 * k + 1)
                    V.tensor_tensor(smp, smp, wide(mod[:, 3 * which, k, 1:NG]), ALU.add).then_inc(ready, 1)

            dve.wait_ge(c_sig, 1)
            V.tensor_tensor(cs, cs, cT, ALU.mult).then_inc(c_silu, 1)
            root(1)
            dve.wait_ge(consts, 64)
            step(V.tensor_copy(iota[:, :], iota_f))
            dve.wait_ge(mod_turned, 1)

            def modulation(turned_rows, lo, hi, w):
                n = (hi - lo) * KC
                step(V.tensor_tensor(mod[:, lo:hi].rearrange("p a k g -> p (a k) g"),
                                     turned_rows[:, 0:n * NG].rearrange("p (a g) -> p a g", g=NG),
                                     badaT[:, lo * KC:hi * KC].unsqueeze(2).to_broadcast([P, n, NG]), ALU.add))
                settle()
                step(V.tensor_scalar(scl[:, w], mod[:, 3 * w + 1], 1.0, None, ALU.add))
                settle()
                step(V.tensor_tensor(scl[:, w], scl[:, w], gnorm[:, w].unsqueeze(2).to_broadcast([P, KC, NG]),
                                     ALU.mult))
                settle()

            modulation(pa[0], 0, 2, 0)
            modulate(x, hT, 0, h_ready)

            dve.wait_ge(conv_in, 64)
            dve.wait_ge(zeroed, 3)
            for pair in range(KC // 2):
                for k in (2 * pair, 2 * pair + 1):
                    dve.wait_ge(tile_done, TILE["conv_a", k] + 1)
                    dve.wait_ge(sig_ready, k + 1)
                    V.tensor_tensor(zp[:, k, LEFT:], pa[k % 4][:, 0:TP], sig[:, k, 0:TP], ALU.mult)\
                        .then_inc(z_ready, 1)
                    V.tensor_tensor(zs[:, k, :, LEFT:], seq(pa[k % 4][:, TP:T]), seq(sig[:, k, TP:T]), ALU.mult)\
                        .then_inc(z_ready, 1)
                dve.wait_ge(z_ready, 4 * pair + 4)
                for j in range(CW):
                    for k in (2 * pair, 2 * pair + 1):
                        yp, w = y[:, k, 0:TP], wdw[:, k, j:j + 1]
                        if j == 0:
                            ins = V.tensor_scalar(yp, zp[:, k, 0:TP], w, cvec[:, 0, k:k + 1], ALU.mult, ALU.add)
                        else:
                            settle(1 if j < CW - 1 or k % 2 == 0 else 0)
                            ins = V.scalar_tensor_tensor(yp, zp[:, k, j:j + TP], w, yp, ALU.mult, ALU.add)
                        if j < CW - 1:
                            step(ins)
                        else:
                            ins.then_inc(y_prompt, 1)
            for n, (kind, m) in enumerate(QK):
                dve.wait_ge(qk_root, n + 1)
                step(V.reciprocal(sq_qk[n], sq_qk[n]))
                settle()
                v, gain = (kT[:, m], qkg[:, 1:2]) if kind == "k" else (q[:, m], qkg[:, 0:1])
                V.scalar_tensor_tensor(v, v, gain, sq_qk[n], ALU.mult, ALU.mult).then_inc(qk_ready, 1)
            dve.wait_ge(y_prompt, KC)
            dve.wait_ge(y_sample, KC // 2)
            dve.wait_ge(conv_stored, 32)
            wi = vtok[0:TS, NQ, KV * P:VW].rearrange("p (pair par) -> p par pair", par=2)
            for par in range(2):
                V.tensor_tensor(wi_diag[0:TS, par * 4:par * 4 + 4], wi[:, par].unsqueeze(2).to_broadcast([TS, 4, TS]),
                                ident[0:TS, 0:TS].unsqueeze(1).to_broadcast([TS, 4, TS]), ALU.mult).then_inc(s_wi, 1)
            dve.wait_ge(stats, 2)
            step(V.tensor_scalar(rstd, stb[:, 0:T], 1.0 / D, None, ALU.mult))
            settle()
            V.tensor_tensor(y[:, :, :], y[:, :, :], over_chunks(rstd), ALU.subtract).then_inc(y_centred, 1)

            dve.wait_ge(mask_in, 32)
            for n in range(NQ * IH):
                t, h = divmod(n, IH)
                keys = P * (t + 1)
                dve.wait_ge(idx_relu, n + 1)
                w = vtok[:, t, KV * P + h:KV * P + h + 1]
                acc = isc[:, t, 0:keys]
                if h == 0:
                    ins = V.tensor_scalar(acc, relu[:, n % 2, 0:keys], w, None, ALU.mult)
                else:
                    dve.wait_ge(idx_used, n)
                    ins = V.scalar_tensor_tensor(acc, relu[:, n % 2, 0:keys], w, acc, ALU.mult, ALU.add)
                ins.then_inc(idx_used, 1)
            dve.wait_ge(idx_used, NQ * IH)
            for t in range(NQ):
                keys = P * (t + 1)
                step(V.scalar_tensor_tensor(isc[:, t, 0:keys], isc[:, t, 0:keys], HEAD_SCALE, causal[t],
                                            ALU.mult, ALU.add))

            dve.wait_ge(attn_in, 48)
            dve.wait_ge(s_wi_prod, 1)
            step(V.tensor_copy(wi_all, pa[2][:, 0:IH * TS].rearrange("p (a b) -> p a b", b=TS)))
            settle()
            dve.wait_ge(s_relued, 4)
            wi_flat = wi_all.rearrange("p a b -> p (a b)")
            for m in range(NPAGES):
                step(V.tensor_tensor(s_relu[:, m], s_relu[:, m], wi_flat, ALU.mult))
            step(V.tensor_tensor(n_relu[0:TS], n_relu[0:TS], wi_flat[0:TS], ALU.mult))
            settle()
            V.tensor_reduce(s_iscT[:, 0:NPAGES], s_relu.rearrange("p m (a b) -> p m b a", b=TS), AX.X, ALU.add)\
                .then_inc(s_summed, 1)
            V.tensor_reduce(s_iscT[0:TS, NPAGES], n_relu[0:TS].rearrange("p (a b) -> p b a", b=TS), AX.X, ALU.add)\
                .then_inc(s_summed, 1)
            dve.wait_ge(y_centred, 1)
            root(2)
            step(V.tensor_tensor(y[:, :, :], y[:, :, :], over_chunks(rstd), ALU.mult))
            settle()
            for k in range(KC):
                V.tensor_scalar(y[:, k], y[:, k], cvec[:, 1, k:k + 1], cvec[:, 2, k:k + 1], ALU.mult, ALU.add)\
                    .then_inc(y_scaled, 1)
            dve.wait_ge(s_turned, 1)
            keys = PAST + TS
            step(V.scalar_tensor_tensor(s_isc[0:TS], pa[3][0:TS, 0:keys], HEAD_SCALE, own[0:TS], ALU.mult, ALU.add))
            lists = [(isc[:, t, 0:P * (t + 1)], max8[:, t]) for t in range(NQ)] + [(s_isc[0:TS], s_max8[0:TS])]
            for taken in range(0, SAMPLE_TOPK, 8):
                left = SAMPLE_TOPK - taken
                now = lists if taken < PROMPT_TOPK else lists[NQ:]
                for scores, best in now:
                    settle(len(now) - 1)
                    step(V.max(out=best, in_=scores))
                if left < 8:
                    settle()
                    step(V.memset(s_max8[0:TS, left:8], TAKEN))
                for scores, best in now:
                    settle(len(now) - 1)
                    step(V.match_replace(out=scores, in_to_replace=best, in_values=scores, imm_value=TAKEN))
                if taken == 8:
                    dve.wait_ge(y_sig, 1)
                    V.tensor_tensor(y[:, :, :], y[:, :, :], xn[:, :, :], ALU.mult).then_inc(conv_ready, 1)
            settle()
            for t in range(NQ):
                keys = P * (t + 1)
                step(V.tensor_scalar(selb[:, t, 0:keys], isc[:, t, 0:keys], TAKEN, NEG, ALU.not_equal, ALU.mult))
            step(V.tensor_scalar(s_sel[0:TS], s_isc[0:TS], TAKEN, NEG, ALU.not_equal, ALU.mult))
            settle()
            for t in range(NQ):
                keys = P * (t + 1)
                V.tensor_tensor(selb[:, t, 0:keys], selb[:, t, 0:keys], causal[t], ALU.add)\
                    .then_inc(sel_ready, 1)
            V.tensor_tensor(s_sel[0:TS], s_sel[0:TS], own[0:TS], ALU.add).then_inc(s_sel_ready, 1)
            dve.wait_ge(s_logits, 1)
            for m in range(NPAGES):
                step(V.scalar_tensor_tensor(s_lT[:, m], pa[0][:, m * 256:m * 256 + 256], QK_SCALE, alibi_past[:, m],
                                            ALU.mult, ALU.add))
            V.scalar_tensor_tensor(s_lT[0:TS, NPAGES], pa[1][0:TS, 0:256], QK_SCALE, alibi_new[0:TS],
                                   ALU.mult, ALU.add).then_inc(s_scaled, 1)

            for n in range(KC):
                key = ("conv_out", n)
                dve.wait_ge(tile_done, TILE[key] + 1)
                dve.wait_ge(act_evac, ACT_EVAC["gate_b", n])
                V.tensor_tensor(gb[:, n], lin[BANK[key]][:, 0:T], gb[:, n], ALU.mult).then_inc(gated, 1)

            for n in range(NQ * H + 1):
                if n < NQ * H:
                    t, h = divmod(n, H)
                    keys = P * (t + 1)
                    slope = 2.0 ** (-8.0 * (h + 1) / H)
                    if n == 0:
                        dve.wait_ge(sel_ready, NQ)
                    if n >= 2:
                        dve.wait_ge(turned, n - 1)
                    step(V.scalar_tensor_tensor(bias_h[:, n % 2, 0:keys], dist[t], -slope,
                                                selb[:, t, 0:keys], ALU.mult, ALU.add))
                    settle()
                    dve.wait_ge(logits, n + 1)
                    V.scalar_tensor_tensor(lg[:, n % 2, 0:keys], pa[n % 2][:, 0:keys], QK_SCALE,
                                           bias_h[:, n % 2, 0:keys], ALU.mult, ALU.add).then_inc(biased, 1)
                    dve.wait_ge(biased, n + 1)
                    V.tensor_reduce(stat[:, n, 0:1], lg[:, n % 2, 0:keys], AX.X, ALU.max, negate=True)\
                        .then_inc(row_max, 1)
                if n >= 1:
                    m = n - 1
                    keys = P * (m // H + 1)
                    dve.wait_ge(exped, m + 1)
                    step(V.reciprocal(stat[:, m, 2:3], stat[:, m, 1:2]))
                    settle()
                    V.tensor_scalar(lg[:, m % 2, 0:keys], lg[:, m % 2, 0:keys], stat[:, m, 2:3], None, ALU.mult)\
                        .then_inc(normed, 1)

            dve.wait_ge(s_selT_prod, 1)
            step(V.tensor_copy(s_selT[:, 0:NPAGES], pa[2][:, 0:NPAGES * TS].rearrange("p (m b) -> p m b", b=TS)))
            step(V.tensor_copy(s_selT[0:TS, NPAGES], pa[2][0:TS, NPAGES * TS:(NPAGES + 1) * TS]))
            settle()
            for m in range(NPAGES + 1):
                rows = P if m < NPAGES else TS
                v = s_lT[0:rows, m].rearrange("p (b h t) -> p b h t", h=H, t=TD)
                V.tensor_tensor(v, v, seq(s_selT[0:rows, m]).unsqueeze(2).to_broadcast([rows, NSEQ, H, TD]), ALU.add)\
                    .then_inc(s_biased, 1)
            for g in range(2):
                dve.wait_ge(s_rows, g + 1)
                step(V.tensor_copy(s_row[:, g], pa[2 + g][:, 0:PAST + TS]))
                settle()
                V.tensor_reduce(s_stat[:, g, 0:1], s_row[:, g], AX.X, ALU.max, negate=True).then_inc(s_rowmax, 1)
            for g in range(2):
                dve.wait_ge(s_exped, g + 1)
                step(V.reciprocal(s_stat[:, g, 2:3], s_stat[:, g, 1:2]))
                settle()
                V.tensor_scalar(s_row[:, g], s_row[:, g], s_stat[:, g, 2:3], None, ALU.mult).then_inc(s_normed, 1)
            dve.wait_ge(s_back, 1)
            V.tensor_copy(s_prT[:, 0:NPAGES], pa[0][:, :].rearrange("p (m r) -> p m r", m=NPAGES))\
                .then_inc(s_back_copied, 1)
            V.tensor_copy(s_prT[0:TS, NPAGES], pa[1][0:TS, 0:256]).then_inc(s_back_copied, 1)
            dve.wait_ge(s_mixed, 1)
            for g in range(2):
                V.tensor_copy(s_out[:, g], pa[2 + g][:, 0:KV * P]).then_inc(s_out_copied, 1)
            dve.wait_ge(s_out_turned, 1)
            for g in range(2):
                for kv in range(KV):
                    heads = slice(kv * HG, (kv + 1) * HG)
                    src = pa[0][:, (g * KV + kv) * P:(g * KV + kv + 1) * P].rearrange("p (b h t) -> p b h t", h=H, t=TD)
                    at = TP + g * TS // 2
                    V.tensor_copy(attn[:, heads, at:at + TS // 2].rearrange("p h (b t) -> p b h t", t=TD),
                                  src[:, :, heads]).then_inc(s_mixed_copied, 1)

            def low_rhs(src, stage):
                for k in range(KC):
                    part = slice(k * T, (k + 1) * T)
                    dve.wait_ge(rhs_hi, stage * KC + k + 1)
                    V.tensor_tensor(rhs_parts[:, 1, part], src[:, k], rhs_parts[:, 0, part].bitcast(f32), ALU.subtract)\
                        .then_inc(rhs_lo, 1)

            dve.wait_ge(s_mixed_copied, 4)
            low_rhs(attn, 2)
            for n in range(KC):
                key = ("attn_out", n)
                dve.wait_ge(tile_done, TILE[key] + 1)
                V.tensor_tensor(ga[:, n], lin[BANK[key]][:, 0:T], ga[:, n], ALU.mult).then_inc(gated, 1)
                dve.wait_ge(gated, KC + n + 1)
                V.tensor_tensor(ga[:, n], ga[:, n], gb[:, n], ALU.add).then_inc(merged, 1)
            low_rhs(ga, 3)

            dve.wait_ge(mod_turned, 1 + NGRP - NFIRST)
            modulation(stb, 2, 6, 1)

            def residual(k, src, which, xin, dst, tmp, done):
                V.scalar_tensor_tensor(dst[:, k, 0:TP], src[0], mod[:, which, k, 0:1], xin[:, k, 0:TP],
                                       ALU.mult, ALU.add).then_inc(done, 1)
                V.tensor_tensor(seq(tmp), seq(src[1]), mod[:, which, k, 1:NG].unsqueeze(2).to_broadcast([P, NSEQ, TD]),
                                ALU.mult).then_inc(done, 1)
                dve.wait_ge(done, 3 * k + 2)
                V.tensor_tensor(dst[:, k, TP:T], tmp, xin[:, k, TP:T], ALU.add).then_inc(done, 1)
                dve.wait_ge(done, 3 * k + 3)

            for n in range(KC):
                key = ("out", n)
                dve.wait_ge(tile_done, TILE[key] + 1)
                bank = lin[BANK[key]]
                residual(n, (bank[:, 0:TP], bank[:, TP:T]), 2, x, x, dtmp_early, x1_ready)
            root(3)
            modulate(x, h2, 1, h2_ready)
            low_rhs(h2, 4)

            for grp in range(4):
                dve.wait_ge(pscore_copied, (grp + 1) * NT)
                units = [(t, n) for t in range(NT) for n in range(4 * grp, 4 * grp + 4)]
                nu = len(units)

                def each(fn):
                    for t, n in units:
                        rows = tokens(t)[1]
                        settle(nu - 1)
                        step(fn(rows, t, n))

                each(lambda r, t, n: V.max(out=va[0:r, t, n, 0:8], in_=sc[0:r, t, n]))
                each(lambda r, t, n: V.max_index(out=ix[0:r, t, n, 0:8], in_max=va[0:r, t, n, 0:8],
                                                 in_values=sc[0:r, t, n]))
                each(lambda r, t, n: V.match_replace(out=scw[0:r, t, n], in_to_replace=va[0:r, t, n, 0:8],
                                                     in_values=sc[0:r, t, n], imm_value=TAKEN))
                each(lambda r, t, n: V.max(out=va[0:r, t, n, 8:16], in_=scw[0:r, t, n]))
                each(lambda r, t, n: V.max_index(out=ix[0:r, t, n, 8:16], in_max=va[0:r, t, n, 8:16],
                                                 in_values=scw[0:r, t, n]))
                settle()
                units = [(t, h) for t in range(NT) for h in (2 * grp, 2 * grp + 1)]
                nu = len(units)
                each(lambda r, t, h: V.tensor_tensor(
                    cand[0:r, t, h].rearrange("p (a b) -> p a b", b=PTOP),
                    va[0:r, t, 2 * h].unsqueeze(2).to_broadcast([r, PTOP, PTOP]),
                    va[0:r, t, 2 * h + 1].unsqueeze(1).to_broadcast([r, PTOP, PTOP]), ALU.add))
                each(lambda r, t, h: V.max(out=tv[0:r, t, h, 0:8], in_=cand[0:r, t, h]))
                each(lambda r, t, h: V.max_index(out=tj[0:r, t, h, 0:8], in_max=tv[0:r, t, h, 0:8],
                                                 in_values=cand[0:r, t, h]))
                each(lambda r, t, h: V.match_replace(out=cand[0:r, t, h], in_to_replace=tv[0:r, t, h, 0:8],
                                                     in_values=cand[0:r, t, h], imm_value=TAKEN))
                each(lambda r, t, h: V.max(out=tv[0:r, t, h, 8:16], in_=cand[0:r, t, h]))
                each(lambda r, t, h: V.max_index(out=tj[0:r, t, h, 8:16], in_max=tv[0:r, t, h, 8:16],
                                                 in_values=cand[0:r, t, h]))
                settle()
            for t in range(NT):
                r = tokens(t)[1]
                step(V.tensor_copy(gsum[0:r, t, :, 0], tv[0:r, t, :, 0]))
            settle()
            for t in range(NT):
                r = tokens(t)[1]
                V.tensor_tensor(tv[0:r, t], tv[0:r, t], gsum[0:r, t, :, 0].unsqueeze(2)
                                .to_broadcast([r, PH, PTOP]), ALU.subtract).then_inc(top_max, 1)
            for t in range(NT):
                r = tokens(t)[1]
                flat_j = tj[0:r, t].rearrange("p h k -> p (h k)")
                step(V.tensor_single_scalar(tab_u[0:r, 0, t], flat_j, 4, ALU.logical_shift_right))
                step(V.tensor_single_scalar(tab_u[0:r, 1, t], flat_j, PTOP - 1, ALU.bitwise_and))
                step(V.tensor_copy(ixf[0:r, t], ix[0:r, t]))
            settle()
            for t in range(NT):
                r = tokens(t)[1]
                for w in range(2):
                    step(V.tensor_copy(tab[0:r, w, t], tab_u[0:r, w, t]))
            settle()
            for t in range(NT):
                r = tokens(t)[1]
                for w in range(2):
                    step(V.tensor_tensor(eq[0:r], tab[0:r, w, t].unsqueeze(2).to_broadcast([r, PH * PTOP, PTOP]),
                                         iota[0:r, 0:PTOP].unsqueeze(1).to_broadcast([r, PH * PTOP, PTOP]),
                                         ALU.is_equal))
                    settle()
                    eq4 = eq[0:r].rearrange("p (h k) a -> p h k a", k=PTOP)
                    idx = ixf[0:r, t].rearrange("p (h w) a -> p w h a", w=2)[:, w]
                    step(V.tensor_tensor(eq4, eq4, idx.unsqueeze(2).to_broadcast([r, PH, PTOP, PTOP]), ALU.mult))
                    settle()
                    step(V.tensor_reduce(tsel[0:r, t, w], eq[0:r], AX.X, ALU.add))
                    settle()
            dve.wait_ge(top_exp, NT)
            for t in range(NT):
                r = tokens(t)[1]
                step(V.tensor_reduce(gsum[0:r, t, :, 1], tv[0:r, t], AX.X, ALU.add))
            settle()
            for t in range(NT):
                r = tokens(t)[1]
                step(V.reciprocal(gsum[0:r, t, :, 1], gsum[0:r, t, :, 1]))
            settle()
            for t in range(NT):
                r = tokens(t)[1]
                V.tensor_tensor(tsel[0:r, t, 2].rearrange("p (h k) -> p h k", k=PTOP), tv[0:r, t],
                                gsum[0:r, t, :, 1].unsqueeze(2).to_broadcast([r, PH, PTOP]), ALU.mult)\
                    .then_inc(picks, 1)

            dve.wait_ge(picks_copied, 3)
            for n in range(2):
                V.tensor_copy(picked[:, n], parts[:, n]).then_inc(parts_ready, 1)
            rest = parts[:, 2]
            for n in range(NPARTS):
                V.tensor_copy(picked[:, 2 + n], rest).then_inc(parts_ready, 1)
                if n < NPARTS - 1:
                    dve.wait_ge(parts_ready, 3 + n)
                    step(V.tensor_tensor(parts[:, 3 + n], rest, picked[:, 2 + n], ALU.subtract))
                    settle()
                    rest = parts[:, 3 + n]
            dve.wait_ge(parts_ready, 5)

            def one_hot(token, slot):
                col = bass.ds(token, 1)
                V.tensor_scalar(hot2[:, slot], iota[:, :], picked[:, 1, col], None, ALU.is_equal)
                for n in range(NPARTS):
                    last = V.tensor_scalar(hot1[:, slot, n], iota[:, :], picked[:, 0, col], picked[:, 2 + n, col],
                                           ALU.is_equal, ALU.mult)
                return last

            def token_pairs(g, first=False):
                for pair in range(2):
                    if not first:
                        dve.wait_ge(hot_used, g * 2 + (pair - 1))
                    for j in range(2):
                        last = one_hot(g * 4 + (2 * pair + j), 2 * pair + j)
                    last.then_inc(hot_ready, 1)

            token_pairs(0, True)
            with dve.Fori(1, MIXED) as g:
                token_pairs(g)

            dve.wait_ge(gate_copied, MIXED)

            def weights(g, behind):
                for n in range(R):
                    dve.wait_ge(act_loaded[n], g * 16 + 16)
                    V.tensor_tensor(act_b[:, n], act_b[:, n],
                                    gate_mat[:, bass.ds(g * R + n, 1)].rearrange("p o t -> p (o t)"), ALU.mult)\
                        .then_inc(weighted, 1)
                    if n or behind:
                        low(g * R + (n - 1), (n - 1) % R)

            def low(c, n):
                dve.wait_ge(w_hi, c + 1)
                V.tensor_tensor(wr[:, n % 2, 1], act_b[:, n], wr[:, n % 2, 0].bitcast(f32), ALU.subtract)\
                    .then_inc(w_lo, 1)

            weights(0, False)
            with dve.Fori(1, NSUB // R) as g:
                weights(g, True)
            low(NSUB - 1, R - 1)
            dve.wait_ge(x_loaded, 16)
            for k in range(KC):
                dve.wait_ge(bank_done, k + 1)
                residual(k, (ps[k][:, 0:TP], ps[k][:, TP:T]), 5, xe, ye, dtmp, y_out)

        @block.tensor
        def _(pe):
            MM = nc.tensor.matmul

            def sums(src, out, n):
                for k in range(n):
                    last = MM(out[:, 0:T], ones[:, :], src[:, k], start=(k == 0), stop=(k == n - 1))
                return last

            def linear(key, rhs, chunk_ready=None):
                if key[0] == "conv_a":
                    bank = pa[key[1] % 4]
                    if key[1] >= 4:
                        pe.wait_ge(z_ready, 2 * (key[1] - 4) + 2)
                else:
                    bank = lin[BANK[key]]
                    free(BANKED.index(key))
                pe.wait_ge(tile_loaded[TILE[key] % R], 16 * (TILE[key] // R + 1))
                w = ring[:, TILE[key] % R, :].rearrange("p (k m) -> p k m", m=P)
                for k in range(KC):
                    if chunk_ready is not None:
                        pe.wait_ge(chunk_ready, 3 * k + 3)
                    last = MM(bank[:, 0:T], w[:, k], rhs[:, k], start=(k == 0), stop=(k == KC - 1))
                last.then_inc(tile_done, 1)

            def free(n):
                if n < NBANK:
                    return
                kind, m = key = BANKED[n - NBANK]
                if kind == "conv_g":
                    pe.wait_ge(sig_ready, m + 1)
                elif kind in ("conv_out", "attn_out"):
                    pe.wait_ge(gated, m + 1 + (KC if kind == "attn_out" else 0))
                elif kind == "out":
                    pe.wait_ge(x1_ready, 3 * m + 2)
                else:
                    pe.wait_ge(act_evac, ACT_EVAC[key])

            h_hi, h_lo = (rhs_parts[:, part].rearrange("p (k t) -> p k t", t=T) for part in range(2))

            def linear_cut(key):
                n = CUT.index(key)
                stage, = (i for i, kinds in enumerate(STAGES) if key[0] in kinds)
                first = n == 0 or CUT[n - 1][0] not in STAGES[stage]
                free(BANKED.index(key))
                out = lin[BANK[key]][:, 0:T]
                hi, lo = (split[:, n % 2, part].rearrange("p (k m) -> p k m", m=P) for part in range(2))
                pe.wait_ge(lin_hi, n + 1)
                for k in range(KC):
                    if first:
                        pe.wait_ge(rhs_hi, stage * KC + k + 1)
                    MM(out, hi[:, k], h_hi[:, k], start=(k == 0), stop=False)
                for k in range(KC):
                    if first:
                        pe.wait_ge(rhs_lo, stage * KC + k + 1)
                    last = MM(out, hi[:, k], h_lo[:, k], start=False, stop=False)
                last.then_inc(lin_hi_used, 1)
                pe.wait_ge(lin_lo, n + 1)
                for k in range(KC):
                    last = MM(out, lo[:, k], h_hi[:, k], start=False, stop=(k == KC - 1))
                last.then_inc(tile_done, 1)

            pe.wait_ge(zeroed, 3)
            pe.wait_ge(squares, 1)
            sums(xn, stb, KC).then_inc(stats, 1)
            pe.wait_ge(c_silu, 1)

            def ada_columns(g):
                for b in range(2):
                    for s in range(R):
                        pe.wait_ge(tile_loaded[s], g * 32 + 16 * (b + 1))
                        w = ring[:, s, :].rearrange("p (k m) -> p k m", m=ADA_COLS)
                        for j in range(2):
                            k = 2 * s + j
                            last = MM(lin[b][0:NG, :], cs[:, k], w[:, j], start=(k == 0), stop=(k == KC - 1))
                        last.then_inc(tile_done, 1)

            ada_columns(0)
            with pe.Fori(1, NFIRST // 2) as g:
                pe.wait_ge(ada_copied, g * 2)
                ada_columns(g)
            pe.wait_ge(ada_copied, NFIRST)
            pe.wait_ge(consts, 64)
            for n in range(2 * KC):
                last = nc.tensor.transpose(pa[0][:, n * NG:(n + 1) * NG], m_row[:, n * P:(n + 1) * P],
                                           ident[0:NG, 0:NG])
            last.then_inc(mod_turned, 1)

            pe.wait_ge(vw_in, 16)

            def qk_sum(n):
                pe.wait_ge(act_evac, ACT_EVAC[QK[n]])
                if n:
                    pe.wait_ge(qk_root, n)
                MM(stb[:, 0:T], ones[:, :], sq_qk[n], start=True, stop=True).then_inc(qk_sums, 1)

            for key in LINEAR[:LINEAR.index(("gate_a", 0))]:
                if key == ("k", 0):
                    for t in range(NT):
                        n = BANKED.index(("v", t))
                        free(n)
                        cols, rows = tokens(t)
                        for k in range(KC):
                            last = MM(lin[n % NBANK][0:rows, 0:VW], hT[:, k, cols], v_w[:, k], start=(k == 0),
                                      stop=(k == KC - 1))
                        last.then_inc(v_done, 1)
                linear(key, hT, h_ready if key == ("conv_a", 0) else None)
                if key in QK[1:]:
                    qk_sum(QK.index(key) - 1)
            pe.wait_ge(z_ready, 2 * KC)
            for n in range(NQ * IH):
                if n % 2 == 0:
                    linear_cut(("gate_a", n // 2))
                if n == 0:
                    qk_sum(len(QK) - 1)
                if n == 2:
                    pe.wait_ge(y_prompt, KC)
                    pe.wait_ge(y_sample, KC // 2)
                    pe.wait_ge(qk_root, len(QK))
                    sums(y, stb, KC).then_inc(stats, 1)
                if n == 10:
                    pe.wait_ge(squares, 2)
                    sums(xn, stb, KC).then_inc(stats, 1)
                t, h = divmod(n, IH)
                half = slice(ID * (h % 2), ID * (h % 2) + ID)
                if n >= 2:
                    pe.wait_ge(idx_relu, n - 1)
                MM(pa[n % 2][:, 0:P * (t + 1)], qi[half, h // 2, tokens(t)[0]], ki[half, 0:P * (t + 1)],
                   start=True, stop=True).then_inc(idx_prod, 1)
            pe.wait_ge(idx_relu, NQ * IH)
            pe.wait_ge(cache_in, 16 * 4 * NSEQ * NPAGES)
            for m in range(NPAGES):
                for par in range(2):
                    half = slice(ID * par, ID * par + ID)
                    for b in range(NSEQ):
                        out = pa[par][:, m * 128:m * 128 + 128]\
                            .rearrange("p (pair s) -> p pair s", s=TS)[:, :, b * TD:b * TD + TD]
                        MM(out, cache_i[half, b * NPAGES + m], qi[half, :, TP + b * TD:TP + b * TD + TD],
                           start=True, stop=True)
            for par in range(2):
                half = slice(ID * par, ID * par + ID)
                last = MM(pa[par][0:TS, 256:384].rearrange("p (a b) -> p a b", b=TS),
                          ki[half, TP:T], qi[half, :, TP:T], start=True, stop=True)
            last.then_inc(s_idx_prod, 1)
            pe.wait_ge(s_wi, 2)
            MM(pa[2][:, 0:IH * TS], ones[0:TS, :], wi_diag[0:TS].rearrange("p a b -> p (a b)"), start=True, stop=True)\
                .then_inc(s_wi_prod, 1)
            for n in range(KC):
                linear_cut(("gate_b", n))
                if n == 1:
                    pe.wait_ge(s_summed, 2)
                    for m in range(NPAGES):
                        nc.tensor.transpose(pa[3][0:TS, m * P:(m + 1) * P], s_iscT[:, m], ident[:, :])
                    nc.tensor.transpose(pa[3][0:TS, PAST:PAST + TS], s_iscT[0:TS, NPAGES], ident[0:TS, 0:TS])\
                        .then_inc(s_turned, 1)
            pe.wait_ge(qk_ready, len(QK))
            pe.wait_ge(s_relued, 4)
            for m in range(NPAGES):
                for b in range(NSEQ):
                    for kv in range(KV):
                        at = m * 256 + b * H * TD + kv * HG * TD
                        MM(pa[0][:, at:at + HG * TD].rearrange("p (h t) -> p h t", t=TD),
                           cache_k[:, b * NPAGES + m, kv],
                           q[:, kv * HG:(kv + 1) * HG, TP + b * TD:TP + b * TD + TD], start=True, stop=True)
            for kv in range(KV):
                out = pa[1][0:TS, 0:256].rearrange("p (b h t) -> p h b t", h=H, t=TD)[:, kv * HG:(kv + 1) * HG]
                last = MM(out, kT[:, kv, TP:T],
                          q[:, kv * HG:(kv + 1) * HG, TP:T].rearrange("p h (b t) -> p h b t", t=TD),
                          start=True, stop=True)
            last.then_inc(s_logits, 1)
            pe.wait_ge(conv_ready, 1)
            for n in range(KC):
                linear_cut(("conv_out", n))
            def ada_half(g, part):
                key = ("ada", NFIRST + g)
                if part == 0:
                    free(BANKED.index(key))
                for s in (2 * part, 2 * part + 1):
                    n = TILE[key] + s
                    pe.wait_ge(tile_loaded[n % R], 16 * (n // R + 1))
                    w = ring[:, n % R, :].rearrange("p (k m) -> p k m", m=ADA_COLS)
                    for j in range(2):
                        k = 2 * s + j
                        last = MM(lin[BANK[key]][0:NG, :], cs[:, k], w[:, j], start=(k == 0), stop=(k == KC - 1))
                    last.then_inc(tile_done, 1)

            def ada_turn(g):
                pe.wait_ge(act_evac, ACT_EVAC["ada", NFIRST + g])
                for j in range(CG):
                    at = (g * CG + j) * NG
                    last = nc.tensor.transpose(stb[:, at:at + NG], m_row2[:, g % 2, j * P:(j + 1) * P],
                                               ident[0:NG, 0:NG])
                last.then_inc(mod_turned, 1)

            pe.wait_ge(s_scaled, 1)
            for n in range(NQ * H + 2):
                if n < NQ * H:
                    t, h = divmod(n, H)
                    if n >= 2:
                        pe.wait_ge(biased, n - 1)
                    MM(pa[n % 2][:, 0:P * (t + 1)], q[:, h, tokens(t)[0]], kT[:, h // HG, 0:P * (t + 1)],
                       start=True, stop=True).then_inc(logits, 1)
                    ada_half(n // 2, n % 2)
                if 1 <= n <= NQ * H:
                    m = n - 1
                    pe.wait_ge(normed, m + 1)
                    if m >= 1:
                        pe.wait_ge(turned_copied, m)
                    for blk in range(m // H + 1):
                        last = nc.tensor.transpose(pa[2][:, blk * P:(blk + 1) * P],
                                                   lg[:, m % 2, blk * P:(blk + 1) * P], ident[:, :])
                    last.then_inc(turned, 1)
                if n >= 2:
                    m = n - 2
                    t, h = divmod(m, H)
                    pe.wait_ge(turned_copied, m + 1)
                    if m >= 1:
                        pe.wait_ge(mixed_copied, m)
                    kv = h // HG
                    for blk in range(t + 1):
                        last = MM(pa[3][:, 0:P], vtok[:, blk, kv * P:(kv + 1) * P], prT[:, m % 2, blk * P:(blk + 1) * P],
                                  start=(blk == 0), stop=(blk == t))
                    last.then_inc(mixed, 1)
                    if n % 2 == 0:
                        ada_turn(n // 2 - 1)
            pe.wait_ge(turned_copied, NQ * H)
            for m in range(NPAGES):
                nc.tensor.transpose(pa[2][:, m * TS:(m + 1) * TS], s_sel[0:TS, m * P:(m + 1) * P], ident[0:TS, 0:TS])
            nc.tensor.transpose(pa[2][0:TS, NPAGES * TS:(NPAGES + 1) * TS], s_sel[0:TS, PAST:PAST + TS],
                                ident[0:TS, 0:TS]).then_inc(s_selT_prod, 1)
            pe.wait_ge(s_biased, NPAGES + 1)
            pe.wait_ge(mixed_copied, NQ * H)
            for g in range(2):
                for m in range(NPAGES):
                    nc.tensor.transpose(pa[2 + g][:, m * P:(m + 1) * P], s_lT[:, m, g * P:(g + 1) * P], ident[:, :])
                nc.tensor.transpose(pa[2 + g][:, PAST:PAST + TS], s_lT[0:TS, NPAGES, g * P:(g + 1) * P],
                                    ident[0:TS, 0:TS]).then_inc(s_rows, 1)
            pe.wait_ge(s_normed, 2)
            for g in range(2):
                for m in range(NPAGES):
                    nc.tensor.transpose(pa[0][:, m * 256 + g * P:m * 256 + (g + 1) * P],
                                        s_row[:, g, m * P:(m + 1) * P], ident[:, :])
                last = nc.tensor.transpose(pa[1][0:TS, g * P:(g + 1) * P], s_row[:, g, PAST:PAST + TS], ident[:, :])
            last.then_inc(s_back, 1)
            pe.wait_ge(s_back_copied, 2)
            for b in range(NSEQ):
                g, at = b // 4, b % 4 * TS
                out = pa[2 + g][at:at + TS, 0:KV * P]
                for m in range(NPAGES):
                    MM(out, s_prT[:, m, b * TS:(b + 1) * TS], cache_v[:, b * NPAGES + m, :], start=(m == 0), stop=False)
                last = MM(out, s_prT[0:TS, NPAGES, b * TS:(b + 1) * TS], vtok[0:TS, NQ, 0:KV * P], start=False,
                          stop=True)
            last.then_inc(s_mixed, 1)
            pe.wait_ge(s_out_copied, 2)
            for g in range(2):
                for kv in range(KV):
                    last = nc.tensor.transpose(pa[0][:, (g * KV + kv) * P:(g * KV + kv + 1) * P],
                                               s_out[:, g, kv * P:(kv + 1) * P], ident[:, :])
            last.then_inc(s_out_turned, 1)
            pe.wait_ge(s_mixed_copied, 4)
            for n in range(KC):
                linear_cut(("attn_out", n))
            for n in range(KC + 1):
                if n < KC:
                    linear_cut(("out", n))
                if n:
                    pe.wait_ge(squares2, n)
                    last = MM(stb[:, 0:T], ones[:, :], xn[:, n - 1], start=(n == 1), stop=(n == KC))
            last.then_inc(stats, 1)
            pe.wait_ge(peer_in, 32)
            for n in range(2 * PH):
                linear_cut(("peer_q", n))
                if n % 4 == 3:
                    pe.wait_ge(act_evac, ACT_EVAC["peer_q", n])
                    for t in range(NT):
                        m = n // 4 * NT + t
                        cols, rows = tokens(t)
                        if m >= 4:
                            pe.wait_ge(pscore_copied, m - 3)
                        for j in range(4):
                            last = MM(pa[m % 4][0:rows, j * P:(j + 1) * P], qh[:, n - 3 + j, cols], sk[:, j % 2],
                                      start=True, stop=True)
                        last.then_inc(pscore, 1)
            pe.wait_ge(pscore_copied, 4 * NT)

            def scores(c, n, first=False, gates=None):
                pe.wait_ge(hi_ready, c + 1)
                if not first:
                    pe.wait_ge(gelued, c - 1)
                u_hi, u_lo = (split[:, n % 2, part].rearrange("p (k m) -> p k m", m=P) for part in range(2))
                out = ps[n % 2][:, 0:T]
                for k in range(KC):
                    MM(out, u_hi[:, k], h_hi[:, k], start=(k == 0), stop=False)
                    last = MM(out, u_hi[:, k], h_lo[:, k], start=False, stop=False)
                last.then_inc(hi_used, 1)
                if gates:
                    gates(0)
                pe.wait_ge(lo_ready, c + 1)
                for k in range(KC):
                    last = MM(out, u_lo[:, k], h_hi[:, k], start=False, stop=(k == KC - 1))
                last.then_inc(u_done, 1)
                if gates:
                    gates(1)

            for c in range(R):
                scores(c, c, c < 2)
            with pe.Fori(1, TURN // R) as g:
                for n in range(R):
                    scores(g * R + n, n)
            pe.wait_ge(picks, NT)
            for n in range(3):
                for t in range(NT):
                    cols, rows = tokens(t)
                    last = nc.tensor.transpose(pa[n][:, cols], tsel[0:rows, t, n], ident[0:rows, 0:rows])
                last.then_inc(picks_turned, 1)
            for n in range(R):
                scores(TURN + n, n)

            def gate_tokens(q, n, pair, first=False):
                if pair == 0 and not first:
                    pe.wait_ge(gate_copied, q - 1)
                pe.wait_ge(hot_ready, q * 2 + (pair + 1))
                for s in (2 * pair, 2 * pair + 1):
                    for part in range(NPARTS):
                        last = MM(ps[2 + n % 2][:, s * P:(s + 1) * P], hot2[:, s], hot1[:, s, part],
                                  start=(part == 0), stop=(part == NPARTS - 1))
                last.then_inc(hot_used, 1)

            for n in range(R):
                scores(BEFORE + n, n, gates=lambda pair: gate_tokens(n, n, pair, n < 2))
            with pe.Fori(1, MIXED // R) as g:
                for n in range(R):
                    scores(g * R + (BEFORE + n), n, gates=lambda pair: gate_tokens(g * R + n, n, pair))
            with pe.Fori((BEFORE + MIXED) // R, NSUB // R) as g:
                for n in range(R):
                    scores(g * R + n, n)

            def outputs(c, n, first=False, last=False):
                v = [split[:, n % 2, part].rearrange("p (k m) -> p k m", m=P) for part in range(2)]

                def product(v_part, w_part, start=False, stop=False):
                    for k in range(KC):
                        ins = MM(ps[k][:, 0:T], v[v_part][:, k], wr[:, n % 2, w_part], start=start, stop=stop)
                        if stop:
                            ins.then_inc(bank_done, 1)
                    return ins

                pe.wait_ge(hi_ready, c + (NSUB + 1))
                pe.wait_ge(w_hi, c + 1)
                product(0, 0, start=first)
                pe.wait_ge(w_lo, c + 1)
                product(0, 1).then_inc(hi_used, 1)
                pe.wait_ge(lo_ready, c + (NSUB + 1))
                if last:
                    product(1, 0, stop=True)
                else:
                    product(1, 0).then_inc(o_done, 1)

            pe.wait_ge(gelued, NSUB)
            pe.wait_ge(gate_copied, MIXED)
            for n in range(R):
                outputs(n, n, first=n == 0)
            with pe.Fori(1, NSUB // R - 1) as g:
                for n in range(R):
                    outputs(g * R + n, n)
            for n in range(R):
                outputs(NSUB - R + n, n, last=n == R - 1)


def constants():
    p, s = np.arange(P), np.arange(TP)
    pos = (np.arange(NQ)[None, :] * P + p[:, None])[:, :, None]
    dist = (pos - s).astype(np.float32)[:, NQ - 1]
    slope = 2.0 ** (-8.0 * np.arange(1, H + 1) / H)
    t4 = np.arange(TD)
    key = np.arange(NPAGES)[None, :] * P + p[:, None]
    past = -slope[:, None] * (PAST + t4 - key[:, :, None, None])
    past = np.broadcast_to(past[:, :, None], (P, NPAGES, NSEQ, H, TD))
    ts = np.arange(TS)
    new = -slope[:, None] * (t4 - (ts % TD)[:, None, None])
    new = np.broadcast_to(new[:, None], (TS, NSEQ, H, TD))
    own = np.zeros((TS, PAST + TS))
    same = (ts[:, None] // TD == ts // TD) & (ts <= ts[:, None])
    own[:, PAST:] = np.where(same, 0.0, NEG)
    made = {
        "ident": np.eye(P), "iota": np.broadcast_to(p, (P, P)), "dist": dist,
        "causal": np.where(dist >= 0, 0.0, NEG), "alibi_past": past.reshape(P, NPAGES, -1),
        "alibi_new": new.reshape(TS, -1), "own": own,
    }
    return {n: np.ascontiguousarray(v, dtype=np.float32) for n, v in made.items()}


def layouts(v):
    def chunks(m):
        return m.reshape(-1, m.shape[-1] // P, P).transpose(2, 1, 0)

    def cut(w):
        return w.reshape(KC, P, -1, P).transpose(2, 1, 0, 3).reshape(-1, P, D)

    w_in = v["w_in"]
    edges = np.cumsum([H * P, KV * P, KV * P, IH * ID, ID, IH, 2 * D, 2 * D])
    w_q, w_k, w_v, w_qi, w_ki, w_wi, w_conv, w_gate = (
        w_in[:, lo:hi] for lo, hi in zip([0, *edges[:-1]], edges))
    tiles = {"conv_a": cut(w_conv[:, :D]), "conv_g": cut(w_conv[:, D:]), "ki": cut(np.concatenate([w_ki, w_ki], 1)),
             "qi": cut(w_qi), "k": cut(w_k), "q": cut(w_q), "gate_a": cut(w_gate[:, :D]), "gate_b": cut(w_gate[:, D:]),
             "conv_out": cut(v["w_conv_out"]), "attn_out": cut(v["w_o_attn"]), "out": cut(v["w_out"]),
             "peer_q": cut(v["w_q_peer"])}
    stream = np.empty((NTILES, P, D), np.float32)
    ada = v["w_ada"].reshape(R, 2, P, NGRP, ADA_COLS).transpose(3, 0, 2, 1, 4).reshape(NGRP, R, P, D)
    stream[:NFIRST * R] = ada[:NFIRST].reshape(-1, P, D)
    for key, n in TILE.items():
        if key[0] == "ada":
            stream[n:n + R] = ada[key[1]]
        else:
            stream[n] = tiles[key[0]][key[1]]
    stream[NLIN:NLIN + NSUB] = v["u_emb"].reshape(NSUB, P, KC, P).transpose(0, 3, 2, 1).reshape(NSUB, P, D)
    stream[NLIN + NSUB:] = v["v_emb"].reshape(NSUB, P, D)
    xs = np.concatenate([v["x_prompt"].reshape(TP, D), v["x_sample"].reshape(TS, D)])
    cond = np.concatenate([v["c_prompt"], v["c_sample"]])
    vw = np.concatenate([w_v, w_wi], 1)
    pool = v["cache_k"].shape[0]
    made = {
        "stream": stream, "xT": chunks(xs), "cT": chunks(cond), "badaT": v["b_ada"].reshape(-1, P).T,
        "gnorm": chunks(np.stack([v["g_norm1"], v["g_norm2"]])).transpose(0, 2, 1),
        "v_w": vw.reshape(KC, P, VW).transpose(1, 0, 2),
        "stateT": v["state_conv"].reshape(NSEQ, LEFT, KC, P).transpose(3, 2, 0, 1),
        "wdw": v["w_dw"].reshape(CW, KC, P).transpose(2, 1, 0),
        "cvec": chunks(np.stack([v["b_dw"], v["ln_g"], v["ln_b"]])).transpose(0, 2, 1),
        "qkg": np.stack([v["g_q"], v["g_k"]], 1),
        "cache_k": v["cache_k"].transpose(0, 3, 2, 1).reshape(pool, P, KV * PAGE),
        "cache_v": v["cache_v"].reshape(pool, PAGE, KV * P),
        "cache_i": v["cache_idx_k"].transpose(0, 2, 1), "pages": v["page_table"].reshape(1, -1),
        "sub_keys": np.stack([v["sub_keys1"].T, v["sub_keys2"].T]),
    }
    return {n: np.ascontiguousarray(m) for n, m in made.items()} | constants()


OUTS = {"yT": (P, KC, T), "kT": (P, KV, T), "v_prompt": (P, NQ, KV * P), "v_sample": (TS, KV * P), "kiT": (ID, T),
        "convpT": (P, KC, LEFT), "convsT": (P, KC, NSEQ, LEFT)}


def kernel(**inputs):
    import concourse.bacc as bacc
    from concourse.bass_utils import run_bass_kernel_spmd

    arrays = layouts({n: np.asarray(v) for n, v in inputs.items()})
    nc = bacc.Bacc("TRN2", target_bir_lowering=False, num_devices=1)
    aps = {}
    for name, m in arrays.items():
        aps[name] = nc.dram_tensor(f"in_{name}", m.shape, mybir.dt.from_np(m.dtype), kind="ExternalInput").ap()
    for name, shape in OUTS.items():
        aps[name] = nc.dram_tensor(f"out_{name}", shape, mybir.dt.float32, kind="ExternalOutput").ap()
    build(nc, aps)
    got = run_bass_kernel_spmd(nc, [{f"in_{n}": m for n, m in arrays.items()}], core_ids=[0]).results[0]
    out = {n: got[f"out_{n}"] for n in OUTS}
    y = out["yT"].transpose(2, 1, 0).reshape(T, D)
    k = out["kT"].transpose(2, 1, 0)
    ki = out["kiT"].T
    return (y[:TP].reshape(1, TP, D), y[TP:].reshape(NSEQ, TD, D),
            k[:TP].reshape(1, TP, KV, P), out["v_prompt"].transpose(1, 0, 2).reshape(1, TP, KV, P),
            ki[:TP].reshape(1, TP, ID), out["convpT"].transpose(2, 1, 0).reshape(1, LEFT, D),
            k[TP:].reshape(NSEQ, TD, KV, P), out["v_sample"].reshape(NSEQ, TD, KV, P),
            ki[TP:].reshape(NSEQ, TD, ID), out["convsT"].transpose(2, 3, 1, 0).reshape(NSEQ, LEFT, D))
```
